# Optimizing a Trainium2 kernel written in Bass

```python
import jax, jax.numpy as jnp
from jax import lax
import numpy as np
import math

D_MODEL = 1024
BATCH = 1
SEQ = 256
DEPTH = 1

LRU_WIDTH = 512
LRU_BLOCKS = 8
LRU_BLOCK_DIM = LRU_WIDTH // LRU_BLOCKS
LRU_C = 8.0
CONV_WIDTH = 4
GDN_HEADS = 4
GDN_DK = 128
GDN_DV = 128
GDN_CHUNK = 64
SB_HEADS = 8
SB_DH = 64
SB_BLOCK = 128
GLA_HEADS = 4
GLA_DK = 128
GLA_DV = 128
GLA_GATE_RANK = 16
GLA_TAU = 16.0
GLA_CHUNK = 16
N_BRANCHES = 4
BRANCH_WIDTH = 512
N_EXPERTS = 16
N_GROUPS = 4
EXPERTS_PER_GROUP = N_EXPERTS // N_GROUPS
TOP_K = 2
D_EXPERT = 512
LN_EPS = 1e-5
NORM_EPS = 1e-6
DN_ALPHA = (2 * DEPTH) ** 0.25
DN_BETA = (8 * DEPTH) ** -0.25

IN_SPLITS = (
    LRU_WIDTH,
    3 * GDN_HEADS * GDN_DK,
    GDN_HEADS,
    GDN_HEADS,
    GDN_HEADS * GDN_DV,
    3 * SB_HEADS * SB_DH,
    GLA_HEADS * (2 * GLA_DK + GLA_DV),
    GLA_GATE_RANK,
    GLA_HEADS * GLA_DV,
    N_BRANCHES * D_MODEL,
)
D_IN = sum(IN_SPLITS)


def layer_norm(x, g, b):
    xf = x.astype(jnp.float32)
    mu = jnp.mean(xf, -1, keepdims=True)
    var = jnp.mean(jnp.square(xf - mu), -1, keepdims=True)
    y = (xf - mu) * lax.rsqrt(var + LN_EPS) * g.astype(jnp.float32) + b.astype(jnp.float32)
    return y.astype(x.dtype)

def rms_norm(x, g):
    xf = x.astype(jnp.float32)
    return xf * lax.rsqrt(jnp.mean(jnp.square(xf), -1, keepdims=True) + NORM_EPS) * g.astype(jnp.float32)

def l2_normalize(x):
    return x * lax.rsqrt(jnp.sum(jnp.square(x), -1, keepdims=True) + NORM_EPS)

def causal_depthwise_conv(x, w):
    return lax.conv_general_dilated(
        x, w[:, None, :].astype(x.dtype), window_strides=(1,),
        padding=((w.shape[0] - 1, 0),), dimension_numbers=("NWC", "WIO", "NWC"),
        feature_group_count=x.shape[-1])

def _to_chunks(t, c):
    b, s, h = t.shape[:3]
    return jnp.moveaxis(t.reshape((b, s // c, c, h) + t.shape[3:]), 3, 1)

def _from_chunks(t):
    b, h, n, c, d = t.shape
    return jnp.moveaxis(t, 1, 3).reshape(b, n * c, h, d)

def rg_lru(u, conv_w, conv_b, w_a, b_a, w_x, b_x, lam):
    b, s, _ = u.shape
    xc = (causal_depthwise_conv(u, conv_w) + conv_b).astype(jnp.float32)
    xblk = xc.reshape(b, s, LRU_BLOCKS, LRU_BLOCK_DIM)
    r = jax.nn.sigmoid(jnp.einsum("bsgi,gij->bsgj", xblk, w_a.astype(jnp.float32)).reshape(b, s, LRU_WIDTH) + b_a)
    i = jax.nn.sigmoid(jnp.einsum("bsgi,gij->bsgj", xblk, w_x.astype(jnp.float32)).reshape(b, s, LRU_WIDTH) + b_x)
    log_a = -LRU_C * r * jax.nn.softplus(-lam.astype(jnp.float32))
    a = jnp.exp(log_a)
    mult = jnp.sqrt(-jnp.expm1(2.0 * log_a))
    mult = jnp.where(jnp.arange(s)[None, :, None] == 0, 1.0, mult)
    inp = mult * i * xc

    def combine(lhs, rhs):
        return (lhs[0] * rhs[0], rhs[0] * lhs[1] + rhs[1])

    _, h = lax.associative_scan(combine, (a, inp), axis=1)
    return h

def gated_delta_rule_chunked(q, k, v, g, beta):
    b, s, h, dk = q.shape
    dv = v.shape[-1]
    c = GDN_CHUNK
    q, k, v = _to_chunks(q, c), _to_chunks(k, c), _to_chunks(v, c)
    g, beta = _to_chunks(g, c), _to_chunks(beta, c)
    gc = jnp.cumsum(g, axis=-1)
    causal = jnp.tril(jnp.ones((c, c), dtype=bool))
    strict = jnp.tril(jnp.ones((c, c), dtype=bool), k=-1)
    decay = jnp.exp(jnp.where(causal, gc[..., :, None] - gc[..., None, :], -jnp.inf))
    k_beta = k * beta[..., None]
    a_mat = jnp.where(strict, jnp.einsum("bhnik,bhnjk->bhnij", k_beta, k) * decay, 0.0)
    eye = jnp.broadcast_to(jnp.eye(c, dtype=a_mat.dtype), a_mat.shape)
    t_inv = lax.linalg.triangular_solve(a_mat, eye, left_side=True, lower=True, unit_diagonal=True)
    u = t_inv @ (v * beta[..., None])
    w = t_inv @ (k_beta * jnp.exp(gc)[..., None])
    q_dec = q * jnp.exp(gc)[..., None]
    attn = jnp.einsum("bhnik,bhnjk->bhnij", q, k) * decay
    k_dec = k * jnp.exp(gc[..., -1:] - gc)[..., None]
    g_last = jnp.exp(gc[..., -1])

    def step(state, xs):
        u_i, w_i, q_i, attn_i, kd_i, gl_i = xs
        v_new = u_i - w_i @ state
        o_i = q_i @ state + attn_i @ v_new
        state = state * gl_i[..., None, None] + jnp.swapaxes(kd_i, -1, -2) @ v_new
        return state, o_i

    xs = tuple(jnp.moveaxis(t, 2, 0) for t in (u, w, q_dec, attn, k_dec, g_last))
    state0 = jnp.zeros((b, h, dk, dv), q.dtype)
    _, o = lax.scan(step, state0, xs)
    return _from_chunks(jnp.moveaxis(o, 0, 2))

def gla_chunked(q, k, v, gk):
    b, s, h, dk = q.shape
    dv = v.shape[-1]
    c = GLA_CHUNK
    q, k, v, gk = (_to_chunks(t, c) for t in (q, k, v, gk))
    bcum = jnp.cumsum(gk, axis=-2)
    q_dec = q * jnp.exp(bcum)
    k_inv = k * jnp.exp(-bcum)
    causal = jnp.tril(jnp.ones((c, c), dtype=bool))
    attn = jnp.where(causal, jnp.einsum("bhnik,bhnjk->bhnij", q_dec, k_inv), 0.0)
    o_intra = attn @ v
    k_dec = k * jnp.exp(bcum[..., -1:, :] - bcum)
    g_last = jnp.exp(bcum[..., -1, :])

    def step(state, xs):
        q_i, kd_i, v_i, gl_i = xs
        o_i = q_i @ state
        state = state * gl_i[..., :, None] + jnp.swapaxes(kd_i, -1, -2) @ v_i
        return state, o_i

    xs = tuple(jnp.moveaxis(t, 2, 0) for t in (q_dec, k_dec, v, g_last))
    state0 = jnp.zeros((b, h, dk, dv), q.dtype)
    _, o_inter = lax.scan(step, state0, xs)
    return _from_chunks(o_intra + jnp.moveaxis(o_inter, 0, 2))

def stick_breaking_attention(q, k, v):
    b, s, h, dh = q.shape
    q = jnp.swapaxes(q, 1, 2) * dh ** -0.5
    k = jnp.swapaxes(k, 1, 2)
    v = jnp.swapaxes(v, 1, 2)
    outs = []
    for blk in range(s // SB_BLOCK):
        start = blk * SB_BLOCK
        end = start + SB_BLOCK
        z = jnp.einsum("bhqd,bhkd->bhqk", q[:, :, start:end], k[:, :, :end])
        strict = jnp.arange(end)[None, :] < (start + jnp.arange(SB_BLOCK))[:, None]
        log_keep = jnp.where(strict, jax.nn.log_sigmoid(-z), 0.0)
        between = lax.cumsum(log_keep, axis=3, reverse=True) - log_keep
        weights = jnp.where(strict, jnp.exp(jax.nn.log_sigmoid(z) + between), 0.0)
        outs.append(jnp.einsum("bhqk,bhkd->bhqd", weights, v[:, :, :end]))
    o = jnp.concatenate(outs, axis=2)
    return jnp.swapaxes(o, 1, 2).reshape(b, s, h * dh)

def mixer(x, w_in, conv_a_w, conv_a_b, rg_w_a, rg_b_a, rg_w_x, rg_b_x, rg_lambda,
          gdn_conv_w, gdn_a_log, gdn_dt_bias, gdn_norm_w,
          gla_w_gate_up, gla_b_gate, gla_norm_w, w_branch, w_out):
    b, s, _ = x.shape
    f32 = jnp.float32
    proj = jnp.einsum("bsd,de->bse", x, w_in)
    offsets = np.cumsum(IN_SPLITS)[:-1].tolist()
    (a_in, gdn_qkv, gdn_beta_in, gdn_decay_in, gdn_gate_in,
     sb_qkv, gla_qkv, gla_lr, gla_gate_in, merge_in) = jnp.split(proj, offsets, axis=-1)

    y_a = rg_lru(a_in, conv_a_w, conv_a_b, rg_w_a, rg_b_a, rg_w_x, rg_b_x, rg_lambda)

    qkv = jax.nn.silu(causal_depthwise_conv(gdn_qkv, gdn_conv_w)).astype(f32)
    q, k, v = jnp.split(qkv, [GDN_HEADS * GDN_DK, 2 * GDN_HEADS * GDN_DK], axis=-1)
    q = l2_normalize(q.reshape(b, s, GDN_HEADS, GDN_DK)) * GDN_DK ** -0.5
    k = l2_normalize(k.reshape(b, s, GDN_HEADS, GDN_DK))
    v = v.reshape(b, s, GDN_HEADS, GDN_DV)
    beta = jax.nn.sigmoid(gdn_beta_in.astype(f32))
    g = -jnp.exp(gdn_a_log.astype(f32)) * jax.nn.softplus(gdn_decay_in.astype(f32) + gdn_dt_bias)
    o_b = gated_delta_rule_chunked(q, k, v, g, beta)
    y_b = (rms_norm(o_b, gdn_norm_w) * jax.nn.silu(gdn_gate_in.reshape(b, s, GDN_HEADS, GDN_DV).astype(f32))).reshape(b, s, -1)

    q, k, v = jnp.split(sb_qkv.astype(f32), 3, axis=-1)
    y_c = stick_breaking_attention(q.reshape(b, s, SB_HEADS, SB_DH), k.reshape(b, s, SB_HEADS, SB_DH),
                                   v.reshape(b, s, SB_HEADS, SB_DH))

    q, k, v = jnp.split(gla_qkv.astype(f32), [GLA_HEADS * GLA_DK, 2 * GLA_HEADS * GLA_DK], axis=-1)
    gk = jax.nn.log_sigmoid(jnp.einsum("bsr,rc->bsc", gla_lr.astype(f32), gla_w_gate_up.astype(f32)) + gla_b_gate) / GLA_TAU
    o_d = gla_chunked(q.reshape(b, s, GLA_HEADS, GLA_DK) * GLA_DK ** -0.5, k.reshape(b, s, GLA_HEADS, GLA_DK),
                      v.reshape(b, s, GLA_HEADS, GLA_DV), gk.reshape(b, s, GLA_HEADS, GLA_DK))
    y_d = (rms_norm(o_d, gla_norm_w) * jax.nn.silu(gla_gate_in.reshape(b, s, GLA_HEADS, GLA_DV).astype(f32))).reshape(b, s, -1)

    gates = jax.nn.sigmoid(merge_in.reshape(b, s, N_BRANCHES, D_MODEL))
    merged = jnp.zeros_like(x)
    for n, y_n in enumerate((y_a, y_b, y_c, y_d)):
        merged = merged + gates[:, :, n] * jnp.einsum("bsc,cd->bsd", y_n.astype(x.dtype), w_branch[n])
    return jnp.einsum("bsd,de->bse", merged, w_out)

def moe(x, w_router, router_bias, w_gate, w_up, w_down):
    b, s, _ = x.shape
    scores = jax.nn.sigmoid(jnp.einsum("bsd,de->bse", x.astype(jnp.float32), w_router.astype(jnp.float32)))
    biased = scores + router_bias.astype(jnp.float32)
    grouped = biased.reshape(b, s, N_GROUPS, EXPERTS_PER_GROUP)
    group_score = jnp.sum(lax.top_k(grouped, TOP_K)[0], axis=-1)
    group_mask = jnp.argmax(group_score, axis=-1)[..., None] == jnp.arange(N_GROUPS)
    masked = jnp.where(group_mask[..., None], grouped, -jnp.inf).reshape(b, s, N_EXPERTS)
    _, expert_idx = lax.top_k(masked, TOP_K)
    w = jnp.take_along_axis(scores, expert_idx, axis=-1)
    w = w / jnp.sum(w, axis=-1, keepdims=True)
    combine = jnp.sum(jax.nn.one_hot(expert_idx, N_EXPERTS, dtype=jnp.float32) * w[..., None], axis=-2)
    combine = combine.astype(x.dtype)
    y = jnp.zeros_like(x)
    for e in range(N_EXPERTS):
        h = jax.nn.silu(jnp.einsum("bsd,df->bsf", x, w_gate[e])) * jnp.einsum("bsd,df->bsf", x, w_up[e])
        y = y + combine[..., e:e + 1] * jnp.einsum("bsf,fd->bsd", h, w_down[e])
    return y

def first_inputs(seed: int = 0) -> dict:
    key = jax.random.key(seed)
    ks = jax.random.split(key, 32)
    f32 = jnp.float32
    L = DEPTH

    def nrm(i, shape, scale):
        return jax.random.normal(ks[i], shape, f32) * scale

    x = nrm(0, (BATCH, SEQ, D_MODEL), 1.0)
    w_in = nrm(1, (L, D_MODEL, D_IN), D_MODEL ** -0.5)
    conv_a_w = nrm(2, (L, CONV_WIDTH, LRU_WIDTH), CONV_WIDTH ** -0.5)
    conv_a_b = nrm(3, (L, LRU_WIDTH), 0.01)
    rg_w_a = nrm(4, (L, LRU_BLOCKS, LRU_BLOCK_DIM, LRU_BLOCK_DIM), LRU_BLOCK_DIM ** -0.5)
    rg_b_a = nrm(5, (L, LRU_WIDTH), 0.01)
    rg_w_x = nrm(6, (L, LRU_BLOCKS, LRU_BLOCK_DIM, LRU_BLOCK_DIM), LRU_BLOCK_DIM ** -0.5)
    rg_b_x = nrm(7, (L, LRU_WIDTH), 0.01)
    a_pow = jax.random.uniform(ks[8], (L, LRU_WIDTH), f32, 0.9, 0.999)
    a0 = a_pow ** (1.0 / LRU_C)
    rg_lambda = jnp.log(a0) - jnp.log1p(-a0)
    gdn_conv_w = nrm(9, (L, CONV_WIDTH, 3 * GDN_HEADS * GDN_DK), CONV_WIDTH ** -0.5)
    gdn_a_log = jnp.log(jax.random.uniform(ks[10], (L, GDN_HEADS), f32, 1.0, 16.0))
    dt = jnp.exp(jax.random.uniform(ks[11], (L, GDN_HEADS), f32, float(np.log(1e-3)), float(np.log(1e-1))))
    gdn_dt_bias = dt + jnp.log(-jnp.expm1(-dt))
    gdn_norm_w = 1.0 + nrm(12, (L, GDN_DV), 0.01)
    gla_w_gate_up = nrm(13, (L, GLA_GATE_RANK, GLA_HEADS * GLA_DK), GLA_GATE_RANK ** -0.5)
    gla_b_gate = nrm(14, (L, GLA_HEADS * GLA_DK), 0.01)
    gla_norm_w = 1.0 + nrm(15, (L, GLA_DV), 0.01)
    w_branch = nrm(16, (L, N_BRANCHES, BRANCH_WIDTH, D_MODEL), BRANCH_WIDTH ** -0.5)
    w_out = nrm(17, (L, D_MODEL, D_MODEL), D_MODEL ** -0.5 * DN_BETA)
    ln1_g = 1.0 + nrm(18, (L, D_MODEL), 0.01)
    ln1_b = nrm(19, (L, D_MODEL), 0.01)
    w_router = nrm(20, (D_MODEL, N_EXPERTS), D_MODEL ** -0.5)
    router_bias = nrm(21, (N_EXPERTS,), 0.01)
    w_gate = nrm(22, (L, N_EXPERTS, D_MODEL, D_EXPERT), D_MODEL ** -0.5)
    w_up = nrm(23, (L, N_EXPERTS, D_MODEL, D_EXPERT), D_MODEL ** -0.5)
    w_down = nrm(24, (L, N_EXPERTS, D_EXPERT, D_MODEL), D_EXPERT ** -0.5 * DN_BETA)
    ln2_g = 1.0 + nrm(25, (L, D_MODEL), 0.01)
    ln2_b = nrm(26, (L, D_MODEL), 0.01)
    return {"x": x, "w_in": w_in, "conv_a_w": conv_a_w, "conv_a_b": conv_a_b,
            "rg_w_a": rg_w_a, "rg_b_a": rg_b_a, "rg_w_x": rg_w_x, "rg_b_x": rg_b_x,
            "rg_lambda": rg_lambda, "gdn_conv_w": gdn_conv_w, "gdn_a_log": gdn_a_log,
            "gdn_dt_bias": gdn_dt_bias, "gdn_norm_w": gdn_norm_w, "gla_w_gate_up": gla_w_gate_up,
            "gla_b_gate": gla_b_gate, "gla_norm_w": gla_norm_w, "w_branch": w_branch,
            "w_out": w_out, "ln1_g": ln1_g, "ln1_b": ln1_b, "w_router": w_router,
            "router_bias": router_bias, "w_gate": w_gate, "w_up": w_up, "w_down": w_down,
            "ln2_g": ln2_g, "ln2_b": ln2_b}

def first_block(x, w_in, conv_a_w, conv_a_b, rg_w_a, rg_b_a, rg_w_x, rg_b_x, rg_lambda,
              gdn_conv_w, gdn_a_log, gdn_dt_bias, gdn_norm_w, gla_w_gate_up, gla_b_gate,
              gla_norm_w, w_branch, w_out, ln1_g, ln1_b, w_router, router_bias,
              w_gate, w_up, w_down, ln2_g, ln2_b):
    for l in range(DEPTH):
        h = mixer(x, w_in[l], conv_a_w[l], conv_a_b[l], rg_w_a[l], rg_b_a[l], rg_w_x[l], rg_b_x[l],
                  rg_lambda[l], gdn_conv_w[l], gdn_a_log[l], gdn_dt_bias[l], gdn_norm_w[l],
                  gla_w_gate_up[l], gla_b_gate[l], gla_norm_w[l], w_branch[l], w_out[l])
        x = layer_norm(DN_ALPHA * x + h, ln1_g[l], ln1_b[l])
        h = moe(x, w_router, router_bias, w_gate[l], w_up[l], w_down[l])
        x = layer_norm(DN_ALPHA * x + h, ln2_g[l], ln2_b[l])
    return x


_first_inputs = first_inputs


def first_inputs(seed=0):
    import zlib

    import numpy as np

    out = dict(_first_inputs(seed))
    spreads = {}
    factors = {'conv_a_b': 5.658,
     'rg_b_a': 8.0,
     'rg_b_x': 8.0,
     'gdn_norm_w': 8.0,
     'gla_b_gate': 8.0,
     'gla_norm_w': 8.0,
     'ln1_b': 3.457,
     'ln2_g': 5.612,
     'ln2_b': 5.603}
    for name, (base, spread) in spreads.items():
        noise = np.random.default_rng([zlib.crc32(name.encode()), seed]).standard_normal(out[name].shape)
        drawn = base * np.exp(spread * noise) if base else spread * noise
        out[name] = __import__('jax').numpy.asarray(drawn.astype(out[name].dtype))
    for name, factor in factors.items():
        out[name] = (out[name] * factor).astype(out[name].dtype)
    return out


_narrow_inputs = first_inputs


def first_inputs(seed=0):
    out = dict(_narrow_inputs(seed))
    wider = {'rg_b_a': 12.0, 'rg_b_x': 12.0, 'gla_norm_w': 5.25, 'ln2_g': 6.32, 'ln2_b': 6.31}
    for name, times in wider.items():
        mean = out[name].mean()
        out[name] = (mean + times * (out[name] - mean)).astype(out[name].dtype)
    return out


DEPTH_2 = 2

N_MIXERS = 2
N_LAYERS_A = (DEPTH_2 + 1) // 2
N_LAYERS_B = DEPTH_2 // 2
D_FF = 2752
FFN_HALF = 0.5
ROPE_THETA = 500000.0
ROT_FRAC = 4
Q_BLOCK = 128
EPS = 1e-6
N_MOD = 9

A_HEADS = 16
A_HEAD_DIM = 64
A_KV_DIM = 64
IDX_HEADS = 8
IDX_DIM = 64
TOPK_MAX = 256
A_Q = A_HEADS * A_HEAD_DIM
A_IN = A_Q + 2 * A_KV_DIM + IDX_HEADS * IDX_DIM + IDX_DIM + IDX_HEADS

B_HEADS = 8
B_HEAD_DIM = 64
B_V_DIM = 2 * B_HEAD_DIM
B_QK = 2 * B_HEADS * B_HEAD_DIM
B_IN = 2 * B_QK + B_HEADS * B_V_DIM


def rmsnorm(x, g):
    xf = x.astype(jnp.float32)
    y = xf * lax.rsqrt(jnp.mean(xf * xf, axis=-1, keepdims=True) + EPS)
    return (y * g.astype(jnp.float32)).astype(x.dtype)

def modulate(h, shift, scale):
    return h * (1.0 + scale[:, None, :]) + shift[:, None, :]

def swiglu(h, w_gate, w_up, w_down):
    return (jax.nn.silu(h @ w_gate) * (h @ w_up)) @ w_down

def rope_tables(positions, head_dim):
    rot = head_dim // ROT_FRAC
    inv = ROPE_THETA ** (-jnp.arange(0, rot, 2, dtype=jnp.float32) / rot)
    ang = positions.astype(jnp.float32)[..., None] * inv
    return jnp.cos(ang), jnp.sin(ang)

def apply_rope(x, cos, sin):
    half = cos.shape[-1]
    rot = 2 * half
    shp = cos.shape[:2] + (1,) * (x.ndim - 3) + (half,)
    cos = cos.reshape(shp)
    sin = sin.reshape(shp)
    x1 = x[..., :half].astype(jnp.float32)
    x2 = x[..., half:rot].astype(jnp.float32)
    xr = jnp.concatenate([x1 * cos - x2 * sin, x2 * cos + x1 * sin], axis=-1)
    return jnp.concatenate([xr.astype(x.dtype), x[..., rot:]], axis=-1)

def dsa_mixer(h, w_in, w_out, cos, sin):
    B, S, _ = h.shape
    top_k = min(TOPK_MAX, S // 4)
    proj = h @ w_in
    o1 = A_Q
    o2 = o1 + A_KV_DIM
    o3 = o2 + A_KV_DIM
    o4 = o3 + IDX_HEADS * IDX_DIM
    o5 = o4 + IDX_DIM
    q = apply_rope(proj[..., :o1].reshape(B, S, A_HEADS, A_HEAD_DIM), cos, sin)
    k = apply_rope(proj[..., o1:o2], cos, sin)
    v = proj[..., o2:o3]
    qi = apply_rope(proj[..., o3:o4].reshape(B, S, IDX_HEADS, IDX_DIM), cos, sin)
    ki = apply_rope(proj[..., o4:o5], cos, sin)
    wi = proj[..., o5:].astype(jnp.float32) * (IDX_HEADS ** -0.5 * IDX_DIM ** -0.5)
    ki32 = ki.astype(jnp.float32)
    key_pos = jnp.arange(S)
    scale = A_HEAD_DIM ** -0.5
    gather = jax.vmap(lambda arr, ids: arr[ids])

    def block(i):
        start = i * Q_BLOCK
        t = start + jnp.arange(Q_BLOCK)
        q_b = lax.dynamic_slice_in_dim(q, start, Q_BLOCK, axis=1)
        qi_b = lax.dynamic_slice_in_dim(qi, start, Q_BLOCK, axis=1)
        wi_b = lax.dynamic_slice_in_dim(wi, start, Q_BLOCK, axis=1)
        logits = jnp.einsum('bthd,bsd->bths', qi_b.astype(jnp.float32), ki32)
        score = jnp.einsum('bth,bths->bts', wi_b, jax.nn.relu(logits))
        causal = key_pos[None, :] <= t[:, None]
        score = jnp.where(causal[None], score, -jnp.inf)
        _, idx = lax.top_k(score, top_k)
        k_sel = gather(k, idx).astype(jnp.float32)
        v_sel = gather(v, idx).astype(jnp.float32)
        s = jnp.einsum('bthd,btkd->bhtk', q_b.astype(jnp.float32), k_sel) * scale
        valid = idx <= t[None, :, None]
        s = jnp.where(valid[:, None], s, -jnp.inf)
        p = jax.nn.softmax(s, axis=-1)
        o = jnp.einsum('bhtk,btkd->bthd', p, v_sel)
        return o.reshape(B, Q_BLOCK, A_HEADS * A_KV_DIM).astype(h.dtype)

    out = lax.map(block, jnp.arange(S // Q_BLOCK))
    out = jnp.transpose(out, (1, 0, 2, 3)).reshape(B, S, A_HEADS * A_KV_DIM)
    return out @ w_out

def diff_mixer(h, w_in, w_out, lam, subln_g, cos, sin, layer_idx):
    B, S, _ = h.shape
    lam_init = 0.8 - 0.6 * math.exp(-0.3 * layer_idx)
    proj = h @ w_in
    q = apply_rope(proj[..., :B_QK].reshape(B, S, 2, B_HEADS, B_HEAD_DIM), cos, sin)
    k = apply_rope(proj[..., B_QK:2 * B_QK].reshape(B, S, 2, B_HEADS, B_HEAD_DIM), cos, sin)
    v = proj[..., 2 * B_QK:].reshape(B, S, B_HEADS, B_V_DIM)
    lam32 = lam.astype(jnp.float32)
    lam_val = (jnp.exp(jnp.sum(lam32[0] * lam32[1])) - jnp.exp(jnp.sum(lam32[2] * lam32[3]))
               + lam_init)
    k32 = k.astype(jnp.float32)
    v32 = v.astype(jnp.float32)
    key_pos = jnp.arange(S)
    scale = B_HEAD_DIM ** -0.5

    def block(i):
        start = i * Q_BLOCK
        t = start + jnp.arange(Q_BLOCK)
        q_b = lax.dynamic_slice_in_dim(q, start, Q_BLOCK, axis=1).astype(jnp.float32)
        s = jnp.einsum('btchd,bschd->bchts', q_b, k32) * scale
        causal = key_pos[None, :] <= t[:, None]
        s = jnp.where(causal, s, -jnp.inf)
        p = jax.nn.softmax(s, axis=-1)
        a = p[:, 0] - lam_val * p[:, 1]
        o = jnp.einsum('bhts,bshe->bthe', a, v32)
        o = rmsnorm(o, subln_g) * (1.0 - lam_init)
        return o.reshape(B, Q_BLOCK, B_HEADS * B_V_DIM).astype(h.dtype)

    out = lax.map(block, jnp.arange(S // Q_BLOCK))
    out = jnp.transpose(out, (1, 0, 2, 3)).reshape(B, S, B_HEADS * B_V_DIM)
    return out @ w_out

def second_inputs(seed: int = 0) -> dict:
    key = jax.random.key(seed)
    ks = jax.random.split(key, 18)
    f32 = jnp.float32

    def nrm(k, shape, fan_in, scale=1.0):
        return jax.random.normal(k, shape, f32) * (scale * fan_in ** -0.5)

    x = jax.random.normal(ks[0], (BATCH, SEQ, D_MODEL), f32)
    c = jax.random.normal(ks[1], (BATCH, D_MODEL), f32)
    offsets = jax.random.randint(ks[2], (BATCH, 1), 0, 1024, dtype=jnp.int32)
    positions = offsets + jnp.arange(SEQ, dtype=jnp.int32)[None, :]
    return {
        "x": x,
        "c": c,
        "positions": positions,
        "ada_w": nrm(ks[3], (DEPTH_2, D_MODEL, N_MOD * D_MODEL), D_MODEL, 0.5),
        "ada_b": 0.02 * jax.random.normal(ks[4], (DEPTH_2, N_MOD * D_MODEL), f32),
        "pre_norm": 1.0 + 0.05 * jax.random.normal(ks[5], (DEPTH_2, 3, D_MODEL), f32),
        "post_norm": 1.0 + 0.05 * jax.random.normal(ks[6], (DEPTH_2, 3, D_MODEL), f32),
        "ffn_w_gate": nrm(ks[7], (DEPTH_2, 2, D_MODEL, D_FF), D_MODEL),
        "ffn_w_up": nrm(ks[8], (DEPTH_2, 2, D_MODEL, D_FF), D_MODEL),
        "ffn_w_down": nrm(ks[9], (DEPTH_2, 2, D_FF, D_MODEL), D_FF),
        "dsa_w_in": nrm(ks[10], (N_LAYERS_A, D_MODEL, A_IN), D_MODEL),
        "dsa_w_out": nrm(ks[11], (N_LAYERS_A, A_HEADS * A_KV_DIM, D_MODEL), A_HEADS * A_KV_DIM),
        "diff_w_in": nrm(ks[12], (N_LAYERS_B, D_MODEL, B_IN), D_MODEL),
        "diff_w_out": nrm(ks[13], (N_LAYERS_B, B_HEADS * B_V_DIM, D_MODEL), B_HEADS * B_V_DIM),
        "diff_lambda": 0.1 * jax.random.normal(ks[14], (N_LAYERS_B, 4, B_HEAD_DIM), f32),
        "diff_subln": 1.0 + 0.05 * jax.random.normal(ks[15], (N_LAYERS_B, B_V_DIM), f32),
    }

def second_block(x, c, positions, ada_w, ada_b, pre_norm, post_norm, ffn_w_gate, ffn_w_up,
              ffn_w_down, dsa_w_in, dsa_w_out, diff_w_in, diff_w_out, diff_lambda, diff_subln):
    cos, sin = rope_tables(positions, A_HEAD_DIM)
    cond = jax.nn.silu(c)
    for i in range(DEPTH_2):
        mod = cond @ ada_w[i] + ada_b[i]
        sh0, sc0, g0, sh1, sc1, g1, sh2, sc2, g2 = jnp.split(mod, N_MOD, axis=-1)
        h = modulate(rmsnorm(x, pre_norm[i, 0]), sh0, sc0)
        y = swiglu(h, ffn_w_gate[i, 0], ffn_w_up[i, 0], ffn_w_down[i, 0])
        x = x + FFN_HALF * g0[:, None, :] * rmsnorm(y, post_norm[i, 0])
        h = modulate(rmsnorm(x, pre_norm[i, 1]), sh1, sc1)
        j = i // N_MIXERS
        if i % N_MIXERS == 0:
            y = dsa_mixer(h, dsa_w_in[j], dsa_w_out[j], cos, sin)
        else:
            y = diff_mixer(h, diff_w_in[j], diff_w_out[j], diff_lambda[j], diff_subln[j],
                           cos, sin, i)
        x = x + g1[:, None, :] * rmsnorm(y, post_norm[i, 1])
        h = modulate(rmsnorm(x, pre_norm[i, 2]), sh2, sc2)
        y = swiglu(h, ffn_w_gate[i, 1], ffn_w_up[i, 1], ffn_w_down[i, 1])
        x = x + FFN_HALF * g2[:, None, :] * rmsnorm(y, post_norm[i, 2])
    return x


def setup_inputs(seed=0):
    out = dict(first_inputs(seed))
    for name, value in second_inputs(seed + 1).items():
        if name != "x":
            out[name + "_2"] = value
    return out


def reference(
    x, w_in, conv_a_w, conv_a_b, rg_w_a, rg_b_a, rg_w_x, rg_b_x, rg_lambda, gdn_conv_w,
    gdn_a_log, gdn_dt_bias, gdn_norm_w, gla_w_gate_up, gla_b_gate, gla_norm_w, w_branch, w_out,
    ln1_g, ln1_b, w_router, router_bias, w_gate, w_up, w_down, ln2_g, ln2_b, c_2, positions_2,
    ada_w_2, ada_b_2, pre_norm_2, post_norm_2, ffn_w_gate_2, ffn_w_up_2, ffn_w_down_2,
    dsa_w_in_2, dsa_w_out_2, diff_w_in_2, diff_w_out_2, diff_lambda_2, diff_subln_2,
):
    x = first_block(
        x, w_in, conv_a_w, conv_a_b, rg_w_a, rg_b_a, rg_w_x, rg_b_x, rg_lambda, gdn_conv_w,
        gdn_a_log, gdn_dt_bias, gdn_norm_w, gla_w_gate_up, gla_b_gate, gla_norm_w, w_branch,
        w_out, ln1_g, ln1_b, w_router, router_bias, w_gate, w_up, w_down, ln2_g, ln2_b,
    )
    return second_block(
        x, c_2, positions_2, ada_w_2, ada_b_2, pre_norm_2, post_norm_2, ffn_w_gate_2,
        ffn_w_up_2, ffn_w_down_2, dsa_w_in_2, dsa_w_out_2, diff_w_in_2, diff_w_out_2,
        diff_lambda_2, diff_subln_2,
    )


_drawn_inputs = setup_inputs


def setup_inputs(seed=0):
    import zlib

    import numpy as np

    out = dict(_drawn_inputs(seed))
    spreads = {}
    factors = {'ada_b_2': 6.74,
     'pre_norm_2': 7.525,
     'post_norm_2': 8.0,
     'diff_lambda_2': 8.0,
     'diff_subln_2': 8.0}
    for name, (base, spread) in spreads.items():
        noise = np.random.default_rng([zlib.crc32(name.encode()), seed]).standard_normal(out[name].shape)
        drawn = base * np.exp(spread * noise) if base else spread * noise
        out[name] = __import__('jax').numpy.asarray(drawn.astype(out[name].dtype))
    for name, factor in factors.items():
        out[name] = (out[name] * factor).astype(out[name].dtype)
    return out
```

```python
import math
from collections import Counter
from contextlib import ExitStack

import numpy as np

import concourse.bass as bass
from concourse import mybir

F32 = mybir.dt.float32
I32 = mybir.dt.int32
ALU = mybir.AluOpType
ACT = mybir.ActivationFunctionType
AX = mybir.AxisListType

S = 256
D = 1024
DT = D // 128
LRU, BRANCH, HEADS = 512, 512, 4
EXPERTS, D_EXPERT = 16, 512
D_FF = 2752
A_IN, DIFF_IN = 1736, 3072
TOPK = 64
DN_ALPHA = 2 ** 0.25
LN_EPS, EPS = 1e-5, 1e-6
BIG = 1e30
LAM_INIT = 0.8 - 0.6 * math.exp(-0.3 * 1)

R = 6
UNIT = 2048
CH = 288
N_MOD = 9 * D

C_A, C_GDN, C_BETA, C_GATE_B, C_SB, C_GLA, C_LR, C_GATE_D, C_MERGE = (
    0, 512, 2048, 2056, 2568, 4104, 5640, 5656, 6168)
V_CONV_A, V_CONV_AB, V_BA, V_BX, V_LAM, V_BGLA, V_NB, V_ND, V_SUB, V_CONV_B, V_C = (
    0, 16, 20, 24, 28, 32, 36, 37, 38, 40, 88)

BRANCH_ORDER = [0, 2, 3, 1]

STEPS = [("small",), ("proj", "a"), ("a_conv",), ("proj", "b"), ("a_gates",), ("proj", "c"), ("b_conv",),
         ("proj", "d"), ("b_norm",)]


def _weave(steps, tiles):
    out, put = [], 0
    for n, s in enumerate(steps):
        out.append(s)
        while put < len(tiles) and put * len(steps) < (n + 1) * len(tiles):
            out.append(tiles[put])
            put += 1
    return out + tiles[put:]


_MERGE = [("merge", k) for k in range(4 * DT)]
STEPS += _weave([(s, hp) for hp in range(4) for s in ("c_z", "c_cum", "c_out")], _MERGE[0:8])
STEPS += _weave([("d_gate",), ("d_attn",), ("d_intra",)] + [("d_chunk", c) for c in range(16)] + [("d_end",)],
                _MERGE[8:16])
STEPS += _weave([("b_rows",), ("b_decay",), ("b_kk",), ("b_nat",)]
                + [(s, lv) for lv in range(1, 6) for s in ("b_y", "b_xy")]
                + [("b_uw",)] + [(s, c) for c in range(4) for s in ("b_w", "b_o")] + [("b_end",)],
                _MERGE[16:24])
STEPS += _MERGE[24:32]


def weight_loads(A):
    out = []

    def cols(w, c0, n):
        for c in range(c0, c0 + n, 256):
            m = min(256, c0 + n - c)
            out.append((w[:, c:c + m].rearrange("(t p) n -> p t n", p=128), w.shape[0] // 128, m, 128))

    def rows(w, r0, n):
        m = max(n // 128, 1)
        p = min(n, 128)
        out.append((w[r0:r0 + n, :].rearrange("(t p) n -> p t n", p=p), m, w.shape[1], p))

    def square(w):
        for r in range(0, D, 256):
            rows(w, r, 256)

    w_in, w_branch = A["w_in"][0], A["w_branch"][0]
    for c, n in ((C_A, 512), (C_GDN, 1536), (C_GATE_B, 512), (C_SB, 1536), (C_GLA, 1536), (C_GATE_D, 512)):
        cols(w_in, c, n)
    for b in BRANCH_ORDER:
        for half in range(2):
            out.append((w_branch[b][:, half * 512:half * 512 + 512].rearrange("(t p) n -> p t n", p=128),
                        4, 512, 128))
            cols(w_in, C_MERGE + b * D + half * 512, 512)
    square(A["w_out"][0])
    marks = {"moe": len(out)}
    for e in range(EXPERTS):
        for c in range(0, D_EXPERT, 256):
            cols(A["w_gate"][0][e], c, 256)
            cols(A["w_up"][0][e], c, 256)
            rows(A["w_down"][0][e], c, 256)
    for layer in range(2):
        for half in range(2):
            if half:
                mix = "dsa" if layer == 0 else "diff"
                cols(A[mix + "_w_in_2"][0], 0, A_IN if layer == 0 else DIFF_IN)
                square(A[mix + "_w_out_2"][0])
            marks[layer, half] = len(out)
            g, u, d = (A["ffn_w_%s_2" % k][layer][half] for k in ("gate", "up", "down"))
            for c in range(0, D_FF, 256):
                m = min(256, D_FF - c)
                cols(g, c, m)
                cols(u, c, m)
                if m == 256:
                    rows(d, c, 256)
                else:
                    rows(d, c, 128)
                    rows(d, c + 128, m - 128)
    return out, marks


class Line:

    def __init__(self, eng, sem, own):
        self.eng, self.sem, self.own = eng, sem, own
        self.sent, self.seen = Counter(), Counter()

    def done(self, ins, name=None):
        name = name or self.own
        self.sent[name] += 1
        ins.then_inc(self.sem(name), 1)
        self.eng.wait_ge(self.sem(name), self.sent[name])

    def tell(self, ins, name, n=1):
        self.sent[name] += n
        ins.then_inc(self.sem(name), n)

    def see(self, name, k=1):
        self.seen[name] += k
        self.eng.wait_ge(self.sem(name), self.seen[name])

    def mark(self, name, n=1):
        self.sent[name] += n
        self.eng.sem_inc(self.sem(name), n)


def build(nc, A, out, first=0, last=7, mod_in=None):
    ctx = ExitStack()
    sems = {}

    def sem(name):
        if name not in sems:
            sems[name] = ctx.enter_context(nc.semaphore("s_" + name))
        return sems[name]

    def buf(name, *shape, dt=F32, ctx=ctx):
        return ctx.enter_context(nc.sbuf_tensor(name, list(shape), dt))

    loads, marks = weight_loads(A)
    starts = {0: 0, 1: marks["moe"], 2: marks[0, 0], 3: marks[0, 0] + 34, 4: marks[0, 1],
              5: marks[1, 0], 6: marks[1, 0] + 34, 7: marks[1, 1], 8: len(loads)}
    first_unit, end_unit = starts[first], starts[last + 1]
    mod = nc.dram_tensor("modulation", (2, N_MOD), F32, kind="Internal").ap() if mod_in is None else mod_in

    with ctx:
        ring = buf("ring", 128, R, UNIT)
        xs = buf("xs", 128, 2, D)
        xT = buf("xT", 128, DT, S)
        rowbc = buf("rowbc", 128, 5, D)
        ident = buf("ident", 128, 128)
        ones256 = buf("ones256", 128, S)
        ones = ones256[:, 0:128]
        lamb = buf("lamb", 128, S)
        cols = buf("cols", 128, 128)
        causal_neg = buf("causal_neg", 128, 128)
        causal_01 = buf("causal_01", 128, 128)
        rope = buf("rope", 128, 2, 2, 8)
        eps_ln = buf("eps_ln", 128, 2)
        st = buf("st", 128, 64)
        P = ctx.enter_context(nc.psum_tensor("P", [128, 8, 512], F32))

        m0 = ExitStack()
        masks = buf("masks", 128, 6, 128, ctx=m0)
        tri64 = buf("tri64", 128, 128, ctx=m0)
        blk64 = buf("blk64", 128, 128, ctx=m0)
        tri16 = buf("tri16", 128, 128, ctx=m0)
        suffix = buf("suffix", 128, 128, ctx=m0)
        mask3 = buf("mask3", 128, 384, ctx=m0)
        neg3 = buf("neg3", 128, 384, ctx=m0)
        parity = buf("parity", 128, 2, ctx=m0)
        small = buf("small", 128, 128, ctx=m0)
        wsm = buf("wsm", 128, DT, 24, ctx=m0)
        lrT = buf("lrT", 16, S, ctx=m0)
        wup = buf("wup", 16, 512, ctx=m0)
        yT = [buf(f"yT{b}", 128, 4, S, ctx=m0) for b in range(4)]
        merged = buf("merged", 128, DT, S, ctx=m0)
        sg = buf("sg", 128, 2, S, ctx=m0)
        tmpm = buf("tmpm", 128, S, ctx=m0)
        qkv = buf("qkv", 128, 12, S, ctx=m0)
        gate_b = buf("gate_b", 128, 4, S, ctx=m0)
        gate_d = buf("gate_d", 128, 4, S, ctx=m0)
        m1 = ExitStack()
        sb_q = buf("sb_q", 128, 4, S, ctx=m1)
        sb_k = buf("sb_k", 128, 4, S, ctx=m1)
        sb_v = buf("sb_v", 128, 2, 512, ctx=m1)
        gl_q = buf("gl_q", 128, 4, S, ctx=m1)
        gl_k = buf("gl_k", 128, 4, S, ctx=m1)
        gl_v = buf("gl_v", 128, 2, 512, ctx=m1)
        m2 = ExitStack()
        rowst = buf("rowst", 128, 128, ctx=m2)
        a_pad = buf("a_pad", 128, 4, S + 3, ctx=m2)
        qkv_pad = buf("qkv_pad", 128, 12, S + 3, ctx=m2)
        wbd = buf("wbd", 128, 2, 4, 128, ctx=m2)
        a_x = buf("a_x", 128, 4, S, ctx=m2)
        a_r = buf("a_r", 128, 4, S, ctx=m2)
        a_i, a_t, nsq = yT[1], yT[3], merged
        m2.close()
        m2 = ExitStack()
        c_zs = buf("c_zs", 128, 2, 384, ctx=m2)
        c_e = buf("c_e", 128, 2, 384, ctx=m2)
        c_sp = buf("c_sp", 128, 2, 384, ctx=m2)
        c_w = buf("c_w", 128, 2, 384, ctx=m2)
        m2.close()
        m2 = ExitStack()
        d_B = buf("d_B", 128, 4 * S, ctx=m2)
        d_y = buf("d_y", 128, 4 * S, ctx=m2)
        d_e = buf("d_e", 128, 4 * S, ctx=m2)
        d_reset = buf("d_reset", 128, 4 * S, ctx=m2)
        d_gl = buf("d_gl", 128, 4, 16, ctx=m2)
        d_kd = buf("d_kd", 128, 4, S, ctx=m2)
        d_at = buf("d_at", 128, 8, 128, ctx=m2)
        d_kn = buf("d_kn", 128, 2, 8, 128, ctx=m2)
        d_S = d_B[:, :].rearrange("p (a b) -> p a b", b=512)
        m2.close()
        m1.close()
        m1 = ExitStack()
        b_r1 = buf("b_r1", 128, 8, 128, ctx=m1)
        b_r2 = buf("b_r2", 128, 8, 128, ctx=m1)
        b_dm = buf("b_dm", 128, 8, 128, ctx=m1)
        b_eg = buf("b_eg", 128, 8, 128, ctx=m1)
        b_N = buf("b_N", 128, 8, 128, ctx=m1)
        b_at = buf("b_at", 128, 8, 128, ctx=m1)
        b_X = buf("b_X", 128, 8, 128, ctx=m1)
        b_XT = buf("b_XT", 128, 8, 128, ctx=m1)
        b_kbg = buf("b_kbg", 128, 8, 128, ctx=m1)
        b_kd = buf("b_kd", 128, 8, 128, ctx=m1)
        b_vb = buf("b_vb", 128, 8, 128, ctx=m1)
        b_vn = buf("b_vn", 128, 4, 128, ctx=m1)
        b_S = buf("b_S", 128, 4, 128, ctx=m1)
        b_Nl, b_Y, b_u, b_wT, b_qd, b_sq = b_r1, b_r2, b_r1, b_dm, b_eg, b_X
        m1.close()
        m0.close()

        m0 = ExitStack()
        hid = buf("hid", 128, 4, S, ctx=m0)
        silu = buf("silu", 128, 2, S, ctx=m0)
        adac = buf("adac", 96, 192, ctx=m0)
        adab = buf("adab", 96, 2, 96, ctx=m0)
        modr = buf("modr", 96, 2, 96, ctx=m0)
        m1 = ExitStack()
        ada = buf("ada", 128, 4, DT, CH, ctx=m1)
        acc = buf("acc", 128, 4, CH, ctx=m1)
        wr = buf("wr", 128, DT, 16, ctx=m1)
        rt = buf("rt", 128, 16, 32, ctx=m1)
        sc = buf("sc", 128, 32, ctx=m1)
        comb = buf("comb", 128, 32, ctx=m1)
        m1.close()
        m1 = ExitStack()
        h = buf("h", 128, 2, D, ctx=m1)
        proj = buf("proj", 128, 2, DIFF_IN, ctx=m1)
        qT = buf("qT", 128, 8, S, ctx=m1)
        kT = buf("kT", 128, 8, S, ctx=m1)
        oT = buf("oT", 128, 8, S, ctx=m1)
        dup = buf("dup", 128, 2, 128, ctx=m1)
        keep = buf("keep", 128, 2, S, ctx=m1)
        big = buf("big", 128, 4, S, ctx=m1)
        pr = buf("pr", 128, 4, S, ctx=m1)
        pT = buf("pT", 128, 2, 4, 128, ctx=m1)
        m1.close()
        m0.close()
        qiT = proj[:, 0, 2048:3072].rearrange("p (a b) -> p a b", b=S)
        score = h[:, 0, 0:256]
        rl = h[:, 0, 256:512]
        wk = h[:, 0, 512:1024].rearrange("p (a b) -> p a b", b=S)
        sq_o = h[:, :, :].rearrange("p a b -> p (a b)")

        block = ctx.enter_context(nc.Block())

        def halves(bank0):
            return P[:, bank0:bank0 + 2, :].rearrange("p b (h s) -> p (b h) s", s=S)

        @block.sync
        def _(sp):
            sp.dma_start(xs[:, :, :], A["x"][0].rearrange("(i p) d -> p i d", p=128)).then_inc(sem("x_here"), 16)
            for n, (src, m, k, p) in enumerate(loads[first_unit:end_unit]):
                if n >= R:
                    sp.wait_ge(sem("unit_used"), n - R + 1)
                sp.dma_start(ring[0:p, n % R, 0:m * k].rearrange("p (m k) -> p m k", k=k), src)\
                  .then_inc(sem("unit%d" % (n % R)), 16)
            sp.wait_ge(sem("x_final"), 1)
            sp.dma_start(out[0].rearrange("(i p) d -> p i d", p=128), xs[:, :, :]).then_inc(sem("stored"), 16)
            sp.wait_ge(sem("stored"), 16)

        @block.gpsimd
        def _(pool):
            g = Line(pool, sem, "pool")

            def select(ap, pattern, base, mult, op=ALU.is_ge, fill=0.0):
                g.done(pool.affine_select(out=ap, in_=ap, compare_op=op, fill=fill, base=base, pattern=pattern,
                                          channel_multiplier=mult))

            def load(dst, src, name, **kw):
                pool.dma_start(dst, src, **kw).then_inc(sem(name), 16)

            g.done(pool.memset(ident[:, :], 0.0))
            g.done(pool.memset(ones256[:, :], 1.0))
            select(ident[:, :], [[-1, 128]], 0, 1, ALU.not_equal, 1.0)
            g.done(pool.memset(eps_ln[:, 0:1], LN_EPS))
            g.done(pool.memset(eps_ln[:, 1:2], EPS))
            g.done(pool.memset(causal_01[:, :], 1.0))
            select(causal_01[:, :], [[-1, 128]], 0, 1)
            g.done(pool.tensor_scalar(causal_neg[:, :], causal_01[:, :], -1.0, BIG, ALU.add, ALU.mult))
            g.mark("consts")
            load(lamb[:, :], A["diff_lambda_2"][0].rearrange("a b -> (a b)").partition_broadcast(128), "lam_here")
            load(st[:, 60:62].bitcast(I32), A["positions_2"][0].rearrange("(i p) -> p i", p=128), "pos_here",
                 allow_slow_non_contiguous=True)
            v = A["conv_a_w"][0], A["gdn_conv_w"][0]
            g.done(pool.memset(rowst[:, :], 0.0))
            tiles = [(V_CONV_A, v[0].rearrange("w (t p) -> w t p", p=128).rearrange("w t p -> (w t) p"), 16),
                     (V_CONV_B, v[1].rearrange("w (t p) -> w t p", p=128).rearrange("w t p -> (w t) p"), 48)]
            for c, name, n in ((V_CONV_AB, "conv_a_b", 4), (V_BA, "rg_b_a", 4), (V_BX, "rg_b_x", 4),
                               (V_LAM, "rg_lambda", 4), (V_BGLA, "gla_b_gate", 4), (V_NB, "gdn_norm_w", 1),
                               (V_ND, "gla_norm_w", 1), (V_SUB, "diff_subln_2", 1), (V_C, "c_2", 8)):
                tiles.append((c, A[name][0].rearrange("(t p) -> t p", p=128), n))
            for c, src, n in tiles:
                load(rowst[c:c + n, :], src, "rows_here")
            if first == 0:
                load(wsm[:, :, 0:8], A["w_in"][0][:, C_BETA:C_BETA + 8].rearrange("(t p) n -> p t n", p=128), "small_here")
                load(wsm[:, :, 8:24], A["w_in"][0][:, C_LR:C_LR + 16].rearrange("(t p) n -> p t n", p=128), "small_here")
                load(small[:, 0:4], A["gdn_dt_bias"][0].partition_broadcast(128), "small_here")
                load(small[:, 4:8], A["gdn_a_log"][0].partition_broadcast(128), "small_here")
                load(wup[:, :], A["gla_w_gate_up"][0], "wup_here")
                g.tell(pool.memset(a_pad[:, :, 0:3], 0.0), "pads")
                g.tell(pool.memset(qkv_pad[:, :, 0:3], 0.0), "pads")
                g.done(pool.memset(wbd[:, :, :, :], 0.0))
                for k, name in enumerate(("rg_w_a", "rg_w_x")):
                    w = A[name][0].rearrange("(t e) i j -> e i t j", e=2)
                    for e in range(2):
                        load(wbd[64 * e:64 * e + 64, k, :, 64 * e:64 * e + 64], w[e], "wbd_here")
                for k, name in enumerate(("ln1_g", "ln1_b", "ln2_g", "ln2_b")):
                    load(rowbc[:, k, :], A[name][0].partition_broadcast(128), "ln_here")
                for m, w in ((blk64, 64), (tri64, 64), (tri16, 16)):
                    g.done(pool.memset(m[:, :], 1.0))
                    v = m[:, :].rearrange("p (a b) -> p a b", b=w)
                    select(v, [[-w, 128 // w], [0, w]], 0, 1)
                    select(v, [[w, 128 // w], [0, w]], w - 1, -1)
                for m in (tri64, tri16):
                    select(m[:, :], [[1, 128]], 0, -1)
                g.done(pool.memset(suffix[:, :], 1.0))
                select(suffix[:, :], [[-1, 128]], 0, 1)
                g.done(pool.memset(mask3[:, :], 1.0))
                for b in (0, 2):
                    select(mask3[:, 128 * b:128 * b + 128], [[1, 128]], 0, -1, ALU.is_gt)
                g.done(pool.tensor_scalar(neg3[:, :], mask3[:, :], -1.0, BIG, ALU.add, ALU.mult))
                g.done(pool.memset(masks[:, :, :], 0.0))
                for lv in range(6):
                    b = 1 << lv
                    v = masks[:, lv, :].rearrange("p (n two b) -> p n two b", two=2, b=b)[:, :, 1, :]
                    g.done(pool.memset(v, 1.0))
                    select(v, [[-2 * b, 64 // b], [0, b]], 0, 1)
                    select(v, [[2 * b, 64 // b], [0, b]], b - 1, -1)
                g.done(pool.memset(small[:, 64:72], 1.0))
                for b in range(4):
                    select(small[:, 64 + b:65 + b], [[0, 1]], -32 * b, 1)
                    select(small[:, 64 + b:65 + b], [[0, 1]], 32 * b + 15, -1)
                g.done(pool.tensor_tensor(small[:, 64:66], small[:, 64:66], small[:, 66:68], ALU.add))
                g.done(pool.tensor_tensor(parity[:, 0:1], small[:, 64:65], small[:, 65:66], ALU.add))
                g.done(pool.tensor_scalar(parity[:, 1:2], parity[:, 0:1], -1.0, -1.0, ALU.add, ALU.mult))
                g.mark("masks")

            if first <= 1 <= last:
                if first == 1:
                    for k, name in ((2, "ln2_g"), (3, "ln2_b")):
                        load(rowbc[:, k, :], A[name][0].partition_broadcast(128), "ln_here")
                    for k in range(2):
                        load(rowbc[:, k, :], A["ln1_g"][0].partition_broadcast(128), "ln_here")
                else:
                    pool.wait_ge(sem("mixed"), 1)
                load(wr[:, :, :], A["w_router"].rearrange("(t p) n -> p t n", p=128), "wr_here")
                load(rt[:, 15, 0:16], A["router_bias"].partition_broadcast(128), "wr_here")
                load(adab[:, :, :], A["ada_b_2"].rearrange("l (p q) -> p l q", q=96), "wr_here")

                def chunk(layer, r, j, used):
                    if used is not None:
                        pool.wait_ge(sem("ada_used"), used)
                    src = A["ada_w_2"][layer].rearrange("(t p) n -> p t n", p=128)
                    pool.dma_start(ada[:, j, :, :], src[:, :, bass.ds(r * (4 * CH) + j * CH, CH)])\
                        .then_inc(sem("ada%d" % j), 16)

                for j in range(4):
                    chunk(0, 0, j, None)
                with pool.Fori(1, 8) as r:
                    for j in range(4):
                        chunk(0, r, j, r * 4 + (j - 3))
                with pool.Fori(0, 8) as r:
                    for j in range(4):
                        chunk(1, r, j, r * 4 + (32 + j - 3))
                g.see("modr")
                pool.dma_start(mod.rearrange("l (p q) -> p l q", q=96), modr[:, :, :]).then_inc(sem("mod_stored"), 16)
                pool.wait_ge(sem("mod_stored"), 16)

            def mod_row(layer, k):
                return mod[layer][k * D:k * D + D]

            for n in range(max(first - 2, 0), max(last - 1, 0)):
                layer, sub = n // 3, n % 3
                if first <= 1 or n > first - 2:
                    g.see("pre_free")
                load(rowbc[:, 0, :], A["pre_norm_2"][layer][sub].partition_broadcast(128), "pre_here")
                load(rowbc[:, 1, :], mod_row(layer, 3 * sub + 1).partition_broadcast(128), "pre_here")
                load(rowbc[:, 2, :], mod_row(layer, 3 * sub).partition_broadcast(128), "pre_here")
                if n > max(first - 2, 0):
                    g.see("post_free")
                load(rowbc[:, 3, :], A["post_norm_2"][layer][sub].partition_broadcast(128), "post_here")
                load(rowbc[:, 4, :], mod_row(layer, 3 * sub + 2).partition_broadcast(128), "post_here")

        @block.tensor
        def _(pe):
            t = Line(pe, sem, "pe")
            unit = [0]

            def take(ahead=0):
                n = unit[0]
                unit[0] += 1
                pe.wait_ge(sem("unit%d" % (n % R)), 16 * (n // R + 1))
                return ring[:, n % R, :]

            def mm(o, l, r, start=True, stop=True, **kw):
                return pe.matmul(o, l, r, start=start, stop=stop, **kw)

            def turn_x(src):
                for i in range(2):
                    for b in range(2):
                        for k in range(4):
                            c = 4 * b + k
                            last_t = pe.transpose(P[:, 4 + 2 * i + b, k * 128:k * 128 + 128],
                                                  src[:, i, c * 128:c * 128 + 128], ident[:, :])
                        t.tell(last_t, "xt_psum%d" % b)
                t.see("xt_dve", 2)
                t.see("xt_act", 2)

            def square_out(lhs, tiles=8):
                for u in range(4):
                    w = take().rearrange("p (m n) -> p m n", n=D)
                    for k in range(2):
                        for i in range(2):
                            for c in range(2):
                                x = mm(P[:, 4 + 2 * i + c, :], lhs(2 * u + k, i), w[:, k, c * 512:c * 512 + 512],
                                       start=(u + k == 0), stop=(2 * u + k == 7))
                    if u < 3:
                        t.tell(x, "unit_used")
                return x

            def tile_cm(w, c, n=128):
                k = t.sent["proj"]
                if k >= 2:
                    pe.wait_ge(sem("proj_out"), k - 1)
                for d in range(DT):
                    x = mm(P[:, k % 2, 0:S], w[:, d, c:c + 128], xT[:, d, :], start=d == 0, stop=d == DT - 1)
                t.tell(x, "proj")
                return x

            def tiles_tm(w, n=256):
                for i in range(2):
                    k = t.sent["proj"]
                    if k >= 2:
                        pe.wait_ge(sem("proj_out"), k - 1)
                    for d in range(DT):
                        x = mm(P[:, k % 2, 0:n], xT[:, d, i * 128:i * 128 + 128], w[:, d, :],
                               start=d == 0, stop=d == DT - 1)
                    t.tell(x, "proj")
                return x

            def cm_units(n):
                for _ in range(n):
                    w = take().rearrange("p (m n) -> p m n", n=256)
                    for c in range(2):
                        tile_cm(w, c * 128)

            def tm_units(n, width=256):
                for _ in range(n):
                    w = take()[:, 0:DT * width].rearrange("p (m n) -> p m n", n=width)
                    tiles_tm(w, width)

            def p_small():
                pe.wait_ge(sem("small_here"), 64)
                for i in range(2):
                    for d in range(DT):
                        mm(P[:, 2, 8 * i:8 * i + 8], xT[:, d, i * 128:i * 128 + 128], wsm[:, d, 0:8],
                           start=d == 0, stop=d == DT - 1)
                for d in range(DT):
                    x = mm(P[0:16, 3, 0:S], wsm[:, d, 8:24], xT[:, d, :], start=d == 0, stop=d == DT - 1)
                t.tell(x, "small_psum")

            def p_proj(which):
                if which == "a":
                    cm_units(2)
                elif which == "b":
                    cm_units(8)
                else:
                    cm_units(4)
                    tm_units(2)
                    if which == "d":
                        cm_units(2)

            def p_a_gates():
                pe.wait_ge(sem("wbd_here"), 64)
                t.see("masks")
                t.see("a_x")
                t.see("small_free")
                for g in range(2):
                    for c in range(4):
                        x = mm(P[:, 2 + 2 * g + c // 2, (c % 2) * S:(c % 2) * S + S], wbd[:, g, c, :], a_x[:, c, :])
                    t.tell(x, "a_ri")

            def p_b_norm():
                t.see("b_sq")
                for c in range(4):
                    x = mm(P[:, 4 + c, :], ones, nsq[:, 2 * c:2 * c + 2, :].rearrange("p a b -> p (a b)"))
                t.tell(x, "b_ss")

            def p_c_z(hp):
                if hp == 0:
                    t.see("a_done")
                    t.see("b_rs")
                    pe.wait_ge(sem("proj_out"), t.sent["proj"])
                for s in range(2):
                    r = slice(64 * s, 64 * s + 64)
                    mm(P[:, 2 + s, 0:S], sb_k[r, hp, 0:128], sb_q[r, hp, :])
                    x = mm(P[:, 2 + s, S:384], sb_k[r, hp, 128:S], sb_q[r, hp, 128:S])
                t.tell(x, "c_z")

            def p_c_cum(hp):
                t.see("c_sp")
                for s in range(2):
                    mm(P[:, 4 + s, 0:384], suffix[:, :], c_sp[:, s, :])
                    x = mm(P[:, 4 + s, 128:S], ones[:, :], c_sp[:, s, S:384], start=False, skip_group_check=True)
                t.tell(x, "c_cum")

            def p_c_out(hp):
                t.see("c_w")
                if hp >= 2:
                    pe.wait_ge(sem("y2"), hp - 1)
                for s in range(2):
                    r = slice(64 * s, 64 * s + 64)
                    c = (2 * hp + s) * 64
                    mm(P[r, 6 + hp % 2, 0:S], sb_v[:, 0, c:c + 64], c_w[:, s, 0:S])
                    x = mm(P[r, 6 + hp % 2, 128:S], sb_v[:, 1, c:c + 64], c_w[:, s, S:384], start=False,
                           skip_group_check=True)
                t.tell(x, "c_o")

            def p_d_gate():
                pe.wait_ge(sem("wup_here"), 16)
                for c in range(4):
                    x = mm(P[:, 2 + c // 2, (c % 2) * S:(c % 2) * S + S], wup[:, c * 128:c * 128 + 128], lrT[:, :])
                t.tell(x, "d_psum")

            def p_d_attn():
                t.see("d_q")
                pe.wait_ge(sem("y2"), 4)
                for i in range(2):
                    for hh in range(4):
                        r = slice(i * 128, i * 128 + 128)
                        x = mm(P[:, 4 + i, hh * 128:hh * 128 + 128], gl_k[:, hh, r], gl_q[:, hh, r])
                t.tell(x, "d_psum")
                for i in range(2):
                    for hh in range(4):
                        x = pe.transpose(P[:, 6 + i, hh * 128:hh * 128 + 128], d_kd[:, hh, i * 128:i * 128 + 128], ident[:, :])
                t.tell(x, "d_psum")

            def p_d_intra():
                t.see("d_am")
                for hh in range(4):
                    for i in range(2):
                        o = (hh % 2) * S + i * 128
                        mm(P[:, 4 + hh // 2, o:o + 128], gl_v[:, i, hh * 128:hh * 128 + 128], d_at[:, 4 * i + hh, :],
                           start=(hh % 2 == 0 and i == 0), skip_group_check=True)

            def p_d_chunk(c):
                if c < 15:
                    if c >= 2:
                        pe.wait_ge(sem("d_S"), c - 1)
                    i, b = c // 8, (c % 8) // 2
                    r = slice(32 * b, 32 * b + 32)
                    for hh in range(4):
                        x = mm(P[:, 2 + c % 2, hh * 128:hh * 128 + 128], d_kn[r, c % 2, 4 * i + hh, :],
                               gl_v[r, i, hh * 128:hh * 128 + 128])
                    t.tell(x, "d_psum")
                if c >= 1:
                    pe.wait_ge(sem("d_S"), c)
                    for hh in range(4):
                        o = (hh % 2) * S + c * 16
                        x = mm(P[:, 4 + hh // 2, o:o + 16], d_S[:, (c - 1) % 2, hh * 128:hh * 128 + 128],
                               gl_q[:, hh, c * 16:c * 16 + 16], start=False, skip_group_check=True)
                    t.tell(x, "d_I")

            def norm_sum(bank, name_in, name_out, sq):
                t.see(name_in)
                for b in range(2):
                    x = mm(P[:, bank + b, :], ones[:, :], sq[:, b * 512:b * 512 + 512])
                t.tell(x, name_out)

            def p_d_end():
                norm_sum(6, "d_sq", "d_ss", d_e)

            def p_b_rows():
                t.see("b_R")
                pe.wait_ge(sem("y3"), 1)
                for i in range(2):
                    mm(P[:, 2 + i, :], ones[:, :], b_r1[:, 4 * i:4 * i + 4, :].rearrange("p a b -> p (a b)"))
                    mm(P[:, 4 + i, :], ones[:, :], b_r2[:, 4 * i:4 * i + 4, :].rearrange("p a b -> p (a b)"))
                for i in range(2):
                    gi = small[:, 24 + 4 * i:28 + 4 * i]
                    mm(P[:, 6, 4 * i:4 * i + 4], tri64[:, :], gi)
                    mm(P[:, 6, 8 + 4 * i:12 + 4 * i], blk64[:, :], gi)
                    for s in range(2):
                        r = slice(64 * s, 64 * s + 64)
                        x = mm(P[:, 6 + s, 16 + 4 * i:20 + 4 * i], ones[r, :], small[r, 24 + 4 * i:28 + 4 * i])
                t.tell(x, "b_rows")

            def p_b_decay():
                pass

            def p_b_kk():
                t.see("b_dm")
                for i in range(2):
                    r = slice(i * 128, i * 128 + 128)
                    for hh in range(4):
                        mm(P[:, 2 + i, hh * 128:hh * 128 + 128], qkv[:, 4 + hh, r], qkv[:, 4 + hh, r])
                        x = mm(P[:, 6 + i, hh * 128:hh * 128 + 128], qkv[:, 4 + hh, r], qkv[:, hh, r])
                t.tell(x, "b_kk")

            def p_b_nat():
                t.see("b_X0")
                for i in range(2):
                    r = slice(i * 128, i * 128 + 128)
                    for hh in range(4):
                        o = slice(hh * 128, hh * 128 + 128)
                        pe.transpose(P[:, 2 + i, o], qkv[:, 4 + hh, r], ident[:, :])
                        pe.transpose(P[:, 4 + i, o], qkv[:, 8 + hh, r], ident[:, :])
                        x = pe.transpose(P[:, 6 + i, o], b_XT[:, 4 * i + hh, :], ident[:, :])
                t.tell(x, "b_nat")

            def p_b_y(lv):
                t.see("b_Nl")
                for u in range(8):
                    x = mm(P[:, 2 + u // 4, (u % 4) * 128:(u % 4) * 128 + 128], b_Nl[:, u, :], b_X[:, u, :])
                t.tell(x, "b_Yp")

            def p_b_xy(lv):
                t.see("b_Y")
                for u in range(8):
                    o = slice((u % 4) * 128, (u % 4) * 128 + 128)
                    mm(P[:, 4 + u // 4, o], b_XT[:, u, :], b_Y[:, u, :])
                    x = mm(P[:, 6 + u // 4, o], b_Y[:, u, :], b_XT[:, u, :])
                t.tell(x, "b_XY")

            def p_b_uw():
                t.see("b_inv")
                for u in range(8):
                    o = slice((u % 4) * 128, (u % 4) * 128 + 128)
                    mm(P[:, 2 + u // 4, o], b_XT[:, u, :], b_vb[:, u, :])
                    x = mm(P[:, 4 + u // 4, o], b_kbg[:, u, :], b_XT[:, u, :])
                t.tell(x, "b_uw")

            def p_b_w(c):
                if c == 0:
                    t.see("b_uws")
                    return
                i, b = c // 2, 64 * (c % 2)
                t.see("b_St")
                for hh in range(4):
                    x = mm(P[b:b + 64, 2, hh * 128:hh * 128 + 128], b_wT[:, 4 * i + hh, b:b + 64], b_S[:, hh, :])
                t.tell(x, "b_wS")

            def p_b_o(c):
                i, b = c // 2, 64 * (c % 2)
                r = slice(b, b + 64)
                t.see("b_vn")
                for hh in range(4):
                    u = 4 * i + hh
                    o = P[:, 6 + hh // 2, (hh % 2) * S + c * 64:(hh % 2) * S + c * 64 + 64]
                    if c:
                        mm(o, b_S[:, hh, :], b_qd[:, u, r], stop=False)
                    x = mm(o, b_vn[r, hh, :], b_at[r, u, r], start=not c)
                if c < 3:
                    for hh in range(4):
                        x = mm(P[:, 3, hh * 128:hh * 128 + 128], b_kd[r, 4 * i + hh, :], b_vn[r, hh, :])
                t.tell(x, "b_o")

            def p_b_end():
                norm_sum(2, "b_sq2", "b_ss2", b_sq[:, :, :].rearrange("p a b -> p (a b)"))

            held = {}

            def p_merge(k):
                n, d = BRANCH_ORDER[k // DT], k % DT
                if d == 0:
                    pe.wait_ge(sem("y%d" % n), 4 if n == 2 else 1)
                if k == 0:
                    pe.wait_ge(sem("proj_out"), t.sent["proj"])
                if d % 4 == 0:
                    held["w"] = take().rearrange("p (m n) -> p m n", n=512)
                if d % 2 == 0:
                    held["g"] = take().rearrange("p (m n) -> p m n", n=256)
                if k >= 2:
                    pe.wait_ge(sem("merged"), k - 1)
                for c in range(DT):
                    mm(P[:, k % 2, 0:S], held["g"][:, c, (d % 2) * 128:(d % 2) * 128 + 128], xT[:, c, :],
                           start=c == 0, stop=c == DT - 1)
                for c in range(4):
                    x = mm(P[:, k % 2, S:2 * S], held["w"][:, c, (d % 4) * 128:(d % 4) * 128 + 128], yT[n][:, c, :],
                           start=c == 0, stop=c == 3)
                t.tell(x, "branch_psum")

            pe_steps = {"small": p_small, "proj": p_proj, "a_conv": lambda: None, "a_gates": p_a_gates,
                        "b_conv": lambda: None, "b_norm": p_b_norm, "c_z": p_c_z, "c_cum": p_c_cum, "c_out": p_c_out,
                        "d_gate": p_d_gate, "d_attn": p_d_attn, "d_intra": p_d_intra, "d_chunk": p_d_chunk,
                        "d_end": p_d_end, "b_rows": p_b_rows, "b_decay": p_b_decay, "b_kk": p_b_kk, "b_nat": p_b_nat,
                        "b_y": p_b_y, "b_xy": p_b_xy, "b_uw": p_b_uw, "b_w": p_b_w, "b_o": p_b_o, "b_end": p_b_end,
                        "merge": p_merge}

            def first_mixer():
                turn_x(xs)
                for step in STEPS:
                    pe_steps[step[0]](*step[1:])
                pe.wait_ge(sem("merged"), 4 * DT)
                t.see("b_read")
                t.tell(square_out(lambda k, i: merged[:, k, i * 128:i * 128 + 128]), "mixer_out")

            def gate_up(f, w, gate, up, col, read):
                if read is not None:
                    pe.wait_ge(sem("hid"), read)
                for k, src in enumerate((gate, up)):
                    for d in range(DT):
                        x = mm(P[0:w, f % 2, k * S:k * S + S], src[:, d, col:col + w], xT[:, d, :],
                               start=d == 0, stop=d == DT - 1)
                return x

            def down(f, w, wd, row, ready, start, stop):
                pe.wait_ge(sem("hid"), ready)
                for i in range(2):
                    for c in range(2):
                        x = mm(P[:, 4 + 2 * i + c, :], hid[0:w, f, i * 128:i * 128 + 128],
                               wd[0:w, row, c * 512:c * 512 + 512], start=start, stop=stop)
                return x

            def unit_at(n0, j, r, wide=256):
                pe.wait_ge(sem("unit%d" % ((n0 + j) % R)), r * 16 + 16 * ((n0 + j) // R + 1))
                return ring[:, (n0 + j) % R, 0:(DT * wide if wide != D else UNIT)].rearrange("p (m n) -> p m n", n=wide)

            def four_tiles(n0, r, h0, first_tile, fresh, before_first_down=None, between=None, waits=False):
                wide = [None, None]
                for f in range(4):
                    c = f // 2
                    if f % 2 == 0:
                        wide = unit_at(n0, 3 * c, r), unit_at(n0, 3 * c + 1, r)
                    x = gate_up(f, 128, wide[0], wide[1], (f % 2) * 128,
                                None if first_tile and f < 2 and not waits else r * 4 + (h0 + f - 1))
                    x.then_inc(sem("gu"), 1)
                    if f == 0:
                        if not first_tile:
                            last_down(n0 - R, r, h0 - 4, fresh)
                        if between is not None:
                            between()
                        continue
                    g = f - 1
                    if g == 0 and before_first_down is not None:
                        before_first_down()
                    wd = unit_at(n0, 3 * (g // 2) + 2, r, D)
                    x = down(g, 128, wd, g % 2, r * 4 + (h0 + g + 1), start=(g == 0 and (fresh or first_tile)), stop=False)
                    if f == 1:
                        x.then_inc(sem("unit_used"), 2)
                    if f == 2:
                        x.then_inc(sem("unit_used"), 1)
                    if f == 3:
                        x.then_inc(sem("unit_used"), 2)

            def last_down(n0, r, h0, stop):
                wd = unit_at(n0, 5, r, D)
                x = down(3, 128, wd, 1, r * 4 + (h0 + 4), start=False, stop=stop)
                x.then_inc(sem("expert_out" if stop else "unit_used"), 1)

            def ada_sums(r):
                pe.wait_ge(sem("ada_used"), r * 4 + 4)
                for j in range(4):
                    for q in range(3):
                        x = mm(P[0:96, 2, bass.ds(r * 12 + (3 * j + q), 1)], acc[:, j, q * 96:q * 96 + 96], ones[:, 0:1])
                x.then_inc(sem("ada_read"), 1)

            def experts():
                turn_x(xs)
                pe.wait_ge(sem("wr_here"), 48)
                for i in range(2):
                    for d in range(DT):
                        x = mm(P[:, 3, 16 * i:16 * i + 16], xT[:, d, i * 128:i * 128 + 128], wr[:, d, :],
                               start=d == 0, stop=d == DT - 1)
                t.tell(x, "route_psum")
                n0 = unit[0]
                four_tiles(n0, 0, 0, True, True)
                with pe.Fori(0, EXPERTS - 1) as r:
                    def y_read():
                        pe.wait_ge(sem("y_added"), r + 1)
                    four_tiles(n0 + 6, r, 4, False, True, y_read, lambda: ada_sums(r))
                last_down(n0 + 6 * 15, 0, 4 * 15, True)
                ada_sums(EXPERTS - 1)
                unit[0] += 6 * EXPERTS
                t.see("adac")
                for l in range(2):
                    x = pe.transpose(P[0:96, 3, l * 128:l * 128 + 96], adac[:, l * 96:l * 96 + 96], ident[0:96, 0:96])
                t.tell(x, "modt")

            tiles_before = [4 * EXPERTS if first <= 1 else 0]

            def ffn():
                n0, h0 = unit[0], tiles_before[0]
                four_tiles(n0, 0, h0, True, False, waits=h0 > 0)
                with pe.Fori(0, 4) as r:
                    four_tiles(n0 + 6, r, h0 + 4, False, False)
                m, k0 = n0 + 30, h0 + 20
                wide = unit_at(m, 0, 0, 192), unit_at(m, 1, 0, 192)
                gate_up(0, 128, wide[0], wide[1], 0, k0 - 1).then_inc(sem("gu"), 1)
                last_down(m - R, 0, k0 - 4, False)
                x = gate_up(1, 64, wide[0], wide[1], 128, k0)
                x.then_inc(sem("gu"), 1)
                down(0, 128, unit_at(m, 2, 0, D), 0, k0 + 1, False, False).then_inc(sem("unit_used"), 3)
                t.tell(down(1, 64, unit_at(m, 3, 0, D), 0, k0 + 2, False, True), "out")
                unit[0] += 34
                tiles_before[0] += 22

            def turns(pieces):
                for k in range(0, len(pieces), 4):
                    q = t.sent["turn"]
                    if q >= 2:
                        pe.wait_ge(sem("turned"), q - 1)
                    part = pieces[k:k + 4]
                    for m, src in enumerate(part):
                        x = pe.transpose(P[:, 2 + q % 2, m * 128:m * 128 + 128], src, ident[:, :])
                    t.tell(x, "turn")

            def sparse():
                turn_x(h)
                for u in range(7):
                    tm_units(1, 256 if u < 6 else 200)
                t.see("roped")
                for i in range(2):
                    turns([proj[:, i, 128 * k:128 * k + 128] for k in range(8)])
                    turns([proj[:, i, 1152 + 128 * k:1280 + 128 * k] for k in range(4)])
                t.see("dup")
                for i in range(2):
                    turns([dup[:, i, :], dup2[:, i, :]])
                pe.wait_ge(sem("turned"), t.sent["turn"])
                n = 0
                for i in range(2):
                    kw = 128 * (i + 1)
                    for hh in range(8):
                        r = slice(64 * (hh % 2), 64 * (hh % 2) + 64)
                        if n >= 2:
                            pe.wait_ge(sem("idx_relu"), n - 1)
                        x = mm(P[:, n % 2, 0:kw], qiT[r, hh // 2, i * 128:i * 128 + 128], kT[r, 1, 0:kw])
                        t.tell(x, "idx")
                        n += 1
                units = [(i, hg) for i in range(2) for hg in range(4)]

                def scores(n):
                    i, hg = units[n]
                    kw = 128 * (i + 1)
                    if n >= 1:
                        pe.wait_ge(sem("s_read"), n)
                    else:
                        pe.wait_ge(sem("idx_relu"), 16)
                    for k in range(4):
                        hh = 4 * hg + k
                        r = slice(64 * (hh % 2), 64 * (hh % 2) + 64)
                        x = mm(P[:, k % 2, (k // 2) * S:(k // 2) * S + kw], qT[r, hh // 2, i * 128:i * 128 + 128],
                               kT[r, 0, 0:kw])
                    t.tell(x, "s_psum")
                scores(0)
                for n, (i, hg) in enumerate(units):
                    if n + 1 < len(units):
                        scores(n + 1)
                    t.see("p_ready")
                    for j in range(i + 1):
                        q = t.sent["pt"]
                        if q >= 2:
                            pe.wait_ge(sem("pt_out"), q - 1)
                        for k in range(4):
                            x = pe.transpose(P[:, 2 + q % 2, k * 128:k * 128 + 128], pr[:, k, j * 128:j * 128 + 128], ident[:, :])
                        t.tell(x, "pt")
                    pe.wait_ge(sem("pt_out"), t.sent["pt"])
                    if n >= 2:
                        pe.wait_ge(sem("o_out"), n - 1)
                    for s in range(2):
                        for j in range(i + 1):
                            x = mm(P[64 * s:64 * s + 64, 4 + n % 2, 0:S], proj[:, j, 1088:1152], pT[:, j, 2 * s:2 * s + 2, :],
                                   start=j == 0, stop=j == i)
                    t.tell(x, "o_psum")
                pe.wait_ge(sem("o_out"), len(units))
                t.tell(square_out(lambda k, i: oT[:, k, i * 128:i * 128 + 128]), "out")

            dup2 = big[:, 0, :].rearrange("p (a b) -> p a b", b=128)

            def differential():
                turn_x(h)
                tm_units(12)
                t.see("roped")
                for i in range(2):
                    turns([proj[:, i, 128 * k:128 * k + 128] for k in range(16)])
                pe.wait_ge(sem("turned"), t.sent["turn"])
                units = [(i, hg) for i in range(2) for hg in range(4)]
                base_s = t.sent["s_psum"]

                def scores(n):
                    i, hg = units[n]
                    kw = 128 * (i + 1)
                    if n >= 1:
                        pe.wait_ge(sem("s_read"), base_s + n)
                    else:
                        pe.wait_ge(sem("proj_out"), t.sent["proj"])
                    for k in range(4):
                        hh, c = 2 * hg + k // 2, k % 2
                        r = slice(64 * (hh % 2), 64 * (hh % 2) + 64)
                        tile = (8 * c + hh) // 2
                        x = mm(P[:, k // 2, (k % 2) * S:(k % 2) * S + kw], qT[r, tile, i * 128:i * 128 + 128],
                               kT[r, tile, 0:kw])
                    t.tell(x, "s_psum")
                scores(0)
                for n, (i, hg) in enumerate(units):
                    if n + 1 < len(units):
                        scores(n + 1)
                    t.see("p_ready")
                    q = t.sent["pt"]
                    if q >= 2:
                        pe.wait_ge(sem("pt_out"), q - 1)
                    for k in range(2):
                        for j in range(i + 1):
                            x = pe.transpose(P[:, 2 + q % 2, (2 * k + j) * 128:(2 * k + j) * 128 + 128],
                                             pr[:, k, j * 128:j * 128 + 128], ident[:, :])
                    t.tell(x, "pt")
                    pe.wait_ge(sem("pt_out"), t.sent["pt"])
                    for k in range(2):
                        hh = 2 * hg + k
                        for j in range(i + 1):
                            x = mm(P[:, 4 + hh // 2, (hh % 2) * S + i * 128:(hh % 2) * S + i * 128 + 128],
                                   proj[:, j, 2048 + hh * 128:2048 + hh * 128 + 128], pT[:, k // 2, 2 * (k % 2) + j, :],
                                   start=j == 0, stop=j == i)
                    t.tell(x, "o_psum")
                t.see("o_sq")
                for b in range(4):
                    x = mm(P[:, b, :], ones[:, :], sq_o[:, b * 512:b * 512 + 512])
                t.tell(x, "o_ss")
                t.see("o_normed")
                t.tell(square_out(lambda k, i: oT[:, k, i * 128:i * 128 + 128]), "out")

            t.see("consts")
            pe.wait_ge(sem("rows_here"), 16 * 11)
            t.tell(pe.transpose(P[:, 7, 0:128], rowst[:, :], ident[:, :]), "cols_psum")
            pe.wait_ge(sem("x_here"), 16)
            t.see("cols_ready")
            if first == 0:
                first_mixer()
            if first <= 1 <= last:
                if first == 0:
                    t.see("x_ready")
                experts()
                t.see("modr_read")
            for n in range(max(first, 2), last + 1):
                t.see("h_ready")
                sub = (n - 2) % 3
                if sub != 1:
                    turn_x(h)
                    ffn()
                elif n == 3:
                    sparse()
                else:
                    differential()

        @block.scalar
        def _(act):
            a = Line(act, sem, "act")

            def f(o, i, fn, name=None, **kw):
                a.done(act.activation(o, i, fn, **kw), name)

            def rsqrt(o, i, scale, eps, name=None):
                f(o, i, ACT.Ln, scale=scale, bias=eps)
                f(o, o, ACT.Exp, name, scale=-0.5)

            def take_xT():
                for i in range(2):
                    a.see("xt_psum1")
                    f(xT[:, 4:8, i * 128:i * 128 + 128], P[:, 5 + 2 * i, :].rearrange("p (a b) -> p a b", b=128), ACT.Copy, "xt_act")

            def out_tile(dst, fn=ACT.Copy, scale=1.0, width=S):
                a.see("proj")
                k = a.sent["proj_out"]
                f(dst, P[:, k % 2, 0:width], fn, "proj_out", scale=scale)
                if k % 2:
                    a.mark("unit_used")

            def a_small():
                a.see("small_psum")
                f(small[:, 16:24].rearrange("p (i k) -> p i k", k=4), P[:, 2, 0:16].rearrange("p (i k) -> p i k", k=8)[:, :, 0:4],
                  ACT.Sigmoid, "beta")
                f(lrT[:, :], P[0:16, 3, 0:S], ACT.Copy, "lrT")
                a.see("sp_in")
                f(small[:, 44:56], small[:, 44:56], ACT.Exp)
                f(small[:, 8:12], small[:, 4:8], ACT.Exp, "sp_e")

            def a_proj(which):
                if which == "a":
                    a.see("pads", 2)
                    for c in range(4):
                        out_tile(a_pad[:, c, 3:S + 3])
                elif which == "b":
                    for c in range(12):
                        out_tile(qkv_pad[:, c, 3:S + 3])
                    for c in range(4):
                        out_tile(gate_b[:, c, :], ACT.Silu)
                else:
                    q, k, v = (sb_q, sb_k, sb_v) if which == "c" else (gl_q, gl_k, gl_v)
                    scale = 64 ** -0.5 if which == "c" else 128 ** -0.5
                    for c in range(4):
                        out_tile(q[:, c, :], scale=scale)
                    for c in range(4):
                        out_tile(k[:, c, :])
                    for c in range(2):
                        for i in range(2):
                            out_tile(v[:, i, c * S:c * S + S])
                    if which == "d":
                        for c in range(4):
                            out_tile(gate_d[:, c, :], ACT.Silu)

            def a_a_gates():
                for g, (dst, bias) in enumerate(((a_r, V_BA), (a_i, V_BX))):
                    a.see("a_ri")
                    for c in range(4):
                        f(dst[:, c, :], P[:, 2 + 2 * g + c // 2, (c % 2) * S:(c % 2) * S + S], ACT.Sigmoid,
                          "a_act" if c == 3 else None, bias=cols[:, bias + c:bias + c + 1])
                a.see("a_dve")
                f(a_t[:, :, :], a_r[:, :, :], ACT.Tanh)
                f(a_r[:, :, :], a_r[:, :, :], ACT.Exp, "a_act")
                a.see("a_dve")
                f(a_t[:, :, :], a_t[:, :, :], ACT.Sqrt, "a_act")

            def a_b_conv():
                a.see("b_conv")
                f(qkv[:, :, :], qkv[:, :, :], ACT.Silu)
                f(nsq[:, :, :], qkv[:, 0:8, :], ACT.Square, "b_sq")

            def a_b_norm():
                a.see("b_ss")
                rsqrt(nsq[:, :, :], P[:, 4:8, :], 1.0, eps_ln[:, 1:2], "b_rs")

            def a_c_z(hp):
                a.see("c_z")
                if hp == 0:
                    a.see("a_done")
                    a.see("b_normed")
                f(c_zs[:, :, :], P[:, 2:4, 0:384], ACT.Copy, "c_act")
                a.see("c_dve")
                f(c_e[:, :, :], c_e[:, :, :], ACT.Exp)
                f(c_e[:, :, :], c_e[:, :, :], ACT.Ln, "c_act", bias=1.0)

            def a_c_cum(hp):
                a.see("c_dve")
                f(c_w[:, :, :], c_w[:, :, :], ACT.Exp, "c_w")

            def a_c_out(hp):
                a.see("c_o")
                f(yT[2][:, hp, :], P[:, 6 + hp % 2, 0:S], ACT.Copy, "y2")

            def a_d_gate():
                a.see("d_dve")
                f(d_e[:, :], d_e[:, :], ACT.Exp)
                f(d_e[:, :], d_e[:, :], ACT.Ln, "d_act", bias=1.0)
                a.see("d_dve")
                f(d_y[:, :], d_B[:, :], ACT.Exp, scale=-1 / 16)
                f(d_gl[:, :, :], d_B[:, :].rearrange("p (h c k) -> p h c k", h=4, k=16)[:, :, :, 15], ACT.Exp, scale=-1 / 16)
                f(d_e[:, :], d_B[:, :], ACT.Exp, "d_act", scale=1 / 16)
                a.see("d_dve")
                f(d_kd[:, :, :].rearrange("p a b -> p (a b)"), d_kd[:, :, :].rearrange("p a b -> p (a b)"), ACT.Exp,
                  "d_act", scale=-1 / 16)

            def a_d_end():
                a.see("d_I", 15)
                f(d_e[:, :], P[:, 4:6, :].rearrange("p a b -> p (a b)"), ACT.Square, "d_sq")
                a.see("d_ss")
                rsqrt(d_e[:, :], P[:, 6:8, :].rearrange("p a b -> p (a b)"), 1 / 128, eps_ln[:, 1:2], "d_act")

            def a_b_decay():
                a.see("b_st")
                f(small[:, 72:104], small[:, 72:104], ACT.Exp, "b_act")
                f(b_eg[:, :, :], P[:, 2:4, :], ACT.Exp)
                a.see("b_dif")
                f(b_dm[:, :, :], b_dm[:, :, :], ACT.Exp, "b_act")

            def a_b_nat():
                a.see("b_nat")
                f(b_X[:, :, :], P[:, 6:8, :], ACT.Copy, "b_act")

            def a_b_y(lv):
                a.see("b_Yp")
                f(b_Y[:, :, :], P[:, 2:4, :], ACT.Copy, "b_Y")

            def a_b_uw():
                a.see("b_uw")
                f(b_u[:, :, :], P[:, 2:4, :], ACT.Copy)
                f(b_wT[:, :, :], P[:, 4:6, :], ACT.Copy, "b_act")

            def a_b_end():
                a.see("b_o", 4)
                f(b_sq[:, :, :], P[:, 6:8, :], ACT.Square, "b_sq2")
                a.see("b_ss2")
                rsqrt(b_sq[:, :, :], P[:, 2:4, :], 1 / 128, eps_ln[:, 1:2], "b_act")

            def a_merge(k):
                if k >= 2:
                    act.wait_ge(sem("merged"), k - 1)
                a.see("branch_psum")
                f(sg[:, k % 2, :], P[:, k % 2, 0:S], ACT.Sigmoid, "sg")

            nothing = lambda *x: None
            act_steps = {"small": a_small, "proj": a_proj, "a_conv": nothing, "a_gates": a_a_gates, "b_conv": a_b_conv,
                         "b_norm": a_b_norm, "c_z": a_c_z, "c_cum": a_c_cum, "c_out": a_c_out, "d_gate": a_d_gate,
                         "d_attn": nothing, "d_intra": nothing, "d_chunk": nothing, "d_end": a_d_end, "b_rows": nothing,
                         "b_decay": a_b_decay, "b_kk": nothing, "b_nat": a_b_nat, "b_y": a_b_y, "b_xy": nothing,
                         "b_uw": a_b_uw, "b_w": nothing, "b_o": nothing, "b_end": a_b_end, "merge": a_merge}

            def layer_norm_rs():
                a.see("var")
                rsqrt(st[:, 4:6], st[:, 4:6], 1.0, eps_ln[:, 0:1], "rs")

            def silus(widths, r=0, h0=0, free=True):
                for k, p in enumerate(widths):
                    if free or k >= 2:
                        act.wait_ge(sem("hid"), r * 4 + (h0 + k - 1))
                    act.wait_ge(sem("gu"), r * 4 + (h0 + k + 1))
                    act.activation(silu[0:p, k % 2, :], P[0:p, k % 2, 0:S], ACT.Silu).then_inc(sem("silu"), 1)

            tiles = [0]

            def a_experts():
                take_xT()
                a.see("route_psum")
                f(sc[:, :], P[:, 3, 0:32], ACT.Sigmoid, "sc")
                f(cols[:, V_C:V_C + 8], cols[:, V_C:V_C + 8], ACT.Silu, "cond")
                silus([128] * 4, free=False)
                with act.Fori(0, EXPERTS - 1) as r:
                    silus([128] * 4, r=r, h0=4)
                tiles[0] += 4 * EXPERTS
                layer_norm_rs()

            def before(n):
                for i in range(2):
                    f(h[:, 0, :], xs[:, i, :], ACT.Square, accum_out=st[:, 8 + i:9 + i])
                rsqrt(st[:, 8:10], st[:, 8:10], 1 / D, eps_ln[:, 1:2], "rs_in")

            def after(n):
                a.see("out")
                a.mark("unit_used")
                for b in range(4):
                    f(h[:, 0, 0:512], P[:, 4 + b, :], ACT.Square, "y_ss" if b == 3 else None, accum_out=st[:, 12 + b:13 + b])
                a.see("y_sum")
                rsqrt(st[:, 16:18], st[:, 16:18], 1 / D, eps_ln[:, 1:2], "y_rs")

            def a_ffn():
                h0 = tiles[0]
                silus([128] * 4, h0=h0, free=h0 > 0)
                with act.Fori(0, 4) as r:
                    silus([128] * 4, r=r, h0=h0 + 4)
                silus([128, 64], h0=h0 + 20)
                tiles[0] += 22

            def turned(dsts):
                for dst in dsts:
                    a.see("turn")
                    k = a.sent["turned"]
                    n = dst.shape[1]
                    f(dst, P[:, 2 + k % 2, 0:n * 128].rearrange("p (a b) -> p a b", b=128), ACT.Copy, "turned")

            def softmax_exps(n, i):
                kw = 128 * (i + 1)
                a.see("nmax")
                for k in range(4):
                    f(big[:, k, 0:kw], big[:, k, 0:kw], ACT.Exp, "exps" if k == 3 else None,
                      bias=st[:, 24 + k:25 + k], accum_out=st[:, 28 + k:29 + k])

            def a_sparse():
                for u in range(7):
                    w = 256 if u < 6 else 200
                    for i in range(2):
                        out_tile(proj[:, i, u * 256:u * 256 + w], width=w)
                for i in range(2):
                    r = slice(i * 128, i * 128 + 128)
                    turned([qT[:, 0:4, r], qT[:, 4:8, r], qiT[:, 0:4, r]])
                for i in range(2):
                    turned([kT[:, 0:2, i * 128:i * 128 + 128]])
                n = 0
                for i in range(2):
                    kw = 128 * (i + 1)
                    for hh in range(8):
                        a.see("idx")
                        if n >= 2:
                            act.wait_ge(sem("idx_add"), n - 1)
                        f(wk[:, n % 2, 0:kw], P[:, n % 2, 0:kw], ACT.Relu, "idx_relu")
                        n += 1
                for n in range(8):
                    i, hg = n // 4, n % 4
                    softmax_exps(n, i)
                    for j in range(i + 1):
                        a.see("pt")
                        f(pT[:, j, :, :], P[:, 2 + a.sent["pt_out"] % 2, :].rearrange("p (a b) -> p a b", b=128), ACT.Copy, "pt_out")
                    a.see("o_psum")
                    f(oT[:, 2 * hg:2 * hg + 2, i * 128:i * 128 + 128],
                      P[:, 4 + n % 2, 0:S].rearrange("p (a b) -> p a b", b=128), ACT.Copy, "o_out")

            def a_differential():
                for u in range(12):
                    for i in range(2):
                        out_tile(proj[:, i, u * 256:u * 256 + 256])
                for i in range(2):
                    r = slice(i * 128, i * 128 + 128)
                    turned([qT[:, 0:4, r], qT[:, 4:8, r], kT[:, 0:4, r], kT[:, 4:8, r]])
                for n in range(8):
                    i, hg = n // 4, n % 4
                    softmax_exps(n, i)
                    a.see("pt")
                    src = P[:, 2 + a.sent["pt_out"] % 2, :].rearrange("p (k j b) -> p k j b", k=2, j=2)
                    f(pT[:, 0, :, :].rearrange("p (k j) b -> p k j b", j=2)[:, :, 0:i + 1, :], src[:, :, 0:i + 1, :], ACT.Copy, "pt_out")
                a.see("o_psum", 8)
                f(sq_o[:, :], P[:, 4:8, :].rearrange("p a b -> p (a b)"), ACT.Square, "o_sq")
                a.see("o_ss")
                rsqrt(sq_o[:, :], P[:, 0:4, :].rearrange("p a b -> p (a b)"), 1 / 128, eps_ln[:, 1:2], "o_rs")

            a.see("consts")
            a.see("angles")
            f(rope[:, :, :, :], rope[:, :, :, :], ACT.Sin)
            a.see("cols_ready")
            if first == 0:
                take_xT()
                for step in STEPS:
                    act_steps[step[0]](*step[1:])
                layer_norm_rs()
            if first > 0:
                act.wait_ge(sem("x_here"), 16)
            if first <= 1 <= last:
                a_experts()
            for n in range(max(first, 2), last + 1):
                if n > first:
                    a.see("x_ready2")
                before(n)
                take_xT()
                sub = (n - 2) % 3
                if sub != 1:
                    a_ffn()
                elif n == 3:
                    a_sparse()
                else:
                    a.see("lam_in")
                    f(st[:, 56:58], st[:, 56:58], ACT.Exp, "lam_exp")
                    a_differential()
                after(n)

        @block.vector
        def _(dve):
            v = Line(dve, sem, "dve")

            def tt(o, x, y, op, name=None):
                v.done(dve.tensor_tensor(o, x, y, op), name)

            def ts(o, x, s1, s2=None, op0=ALU.mult, op1=None, name=None):
                v.done(dve.tensor_scalar(o, x, s1, s2, op0, op1) if s2 is not None else
                       dve.tensor_scalar(o, x, s1, None, op0), name)

            def stt(o, x, s, y, op0, op1, name=None):
                v.done(dve.scalar_tensor_tensor(out=o, in0=x, scalar=s, in1=y, op0=op0, op1=op1), name)

            def copy(o, x, name=None):
                v.done(dve.tensor_copy(o, x), name)

            def recip(o, x, name=None):
                v.done(dve.reciprocal(o, x), name)

            def over(ap, n):
                return ap.unsqueeze(1).to_broadcast([128, n, ap.shape[1]])

            def along(ap, n):
                return ap.unsqueeze(2).to_broadcast([128, ap.shape[1], n])

            def take_xT():
                for i in range(2):
                    v.see("xt_psum0")
                    copy(xT[:, 0:4, i * 128:i * 128 + 128], P[:, 4 + 2 * i, :].rearrange("p (a b) -> p a b", b=128), "xt_dve")

            def rope_angles():
                dve.wait_ge(sem("pos_here"), 16)
                copy(st[:, 58:60], st[:, 60:62].bitcast(I32))
                for k in range(8):
                    v.done(dve.memset(st[:, 32 + k:33 + k], float(np.float32(500000.0 ** (-k / 8)))))
                for i in range(2):
                    for c in range(2):
                        ts(rope[:, i, c, :], st[:, 32:40], st[:, 58 + i:59 + i])
                rv = rope[:, :, :, :].rearrange("p i c k -> p c i k")
                turn = 2 * math.pi
                magic = 1.5 * 2.0 ** 23
                c1 = float(np.float32(6.28125))
                c2 = float(np.float32(int((turn - c1) * 2 ** 21) / 2 ** 21))
                c3 = float(np.float32(turn - c1 - c2))
                for c in range(2):
                    k = big_k[:, c, :].rearrange("p (i k) -> p i k", k=8)
                    ts(k, rv[:, c], 1 / turn, 0.25 * c, ALU.mult, ALU.add)
                    ts(k, k, magic, None, ALU.add)
                    ts(k, k, magic, None, ALU.subtract)
                    for cc in (c1, c2, c3):
                        stt(rv[:, c], k, -cc, rv[:, c], ALU.mult, ALU.add)
                    if c:
                        ts(rv[:, c], rv[:, c], math.pi / 2, None, ALU.add)
                    ts(rv[:, c], rv[:, c], 3.1415925, -3.1415925, ALU.min, ALU.max, "angles" if c else None)

            big_k = st[:, 0:32].rearrange("p (c k) -> p c k", k=16)

            def v_small():
                dve.wait_ge(sem("small_here"), 64)
                z, e, s, s2, q = (small[:, k:k + 12] for k in (32, 44, 72, 84, 96))
                ts(z[:, 0:4], cols[:, V_LAM:V_LAM + 4], -1.0)
                v.see("beta")
                tt(z[:, 4:12].rearrange("p (i k) -> p i k", k=4), P[:, 2, 0:16].rearrange("p (i k) -> p i k", k=8)[:, :, 4:8],
                   over(small[:, 0:4], 2), ALU.add)
                stt(e, z, -1.0, z, ALU.mult, ALU.min, "sp_in")
                v.see("sp_e")
                ts(s, e, 2.0, None, ALU.add)
                recip(s, s)
                tt(s, s, e, ALU.mult)
                tt(s2, s, s, ALU.mult)
                ts(q, s2, 1 / 17)
                for k in (15, 13, 11, 9, 7, 5, 3):
                    stt(q, q, 1 / k, s2, ALU.add, ALU.mult)
                ts(q, q, 1.0, 2.0, ALU.add, ALU.mult)
                tt(q, q, s, ALU.mult)
                stt(q, z, 0.0, q, ALU.max, ALU.add)
                ts(small[:, 12:16], q[:, 0:4], -8.0)
                stt(small[:, 24:32].rearrange("p (i k) -> p i k", k=4), q[:, 4:12].rearrange("p (i k) -> p i k", k=4), -1.0,
                    over(small[:, 8:12], 2), ALU.mult, ALU.mult, "small_free")

            def conv(dst, src, w0, stride, c, bias=None):
                tap = lambda w: cols[:, w0 + w * stride + c:w0 + w * stride + c + 1]
                if bias is None:
                    ts(dst, src[:, c, 0:S], tap(0))
                else:
                    ts(dst, src[:, c, 0:S], tap(0), bias, ALU.mult, ALU.add)
                for w in range(1, 4):
                    stt(dst, src[:, c, w:w + S], tap(w), dst, ALU.mult, ALU.add)

            def v_a_conv():
                dve.wait_ge(sem("proj_out"), 4)
                for c in range(4):
                    conv(a_x[:, c, :], a_pad, V_CONV_A, 4, c, cols[:, V_CONV_AB + c:V_CONV_AB + c + 1])
                v.mark("a_x")

            def v_a_gates():
                v.see("masks")
                v.see("a_act", 2)
                for c in range(4):
                    ts(a_r[:, c, :], a_r[:, c, :], small[:, 12 + c:13 + c], name="a_dve" if c == 3 else None)
                v.see("a_act")
                ts(nsq[:, 0:4, :], a_t[:, :, :], -1.0, 1.0, ALU.mult, ALU.add)
                recip(nsq[:, 0:4, :], nsq[:, 0:4, :])
                stt(a_t[:, :, :], a_t[:, :, :], -2.0, nsq[:, 0:4, :], ALU.mult, ALU.mult, "a_dve")
                v.see("a_act")
                v.done(dve.memset(a_t[:, :, 0:1], 1.0))
                tt(a_t[:, :, :], a_t[:, :, :], a_i[:, :, :], ALU.mult)
                tt(a_t[:, :, :], a_t[:, :, :], a_x[:, :, :], ALU.mult)
                for c in range(4):
                    v.done(dve.tensor_tensor_scan(yT[0][:, c, :], a_r[:, c, :], a_t[:, c, :], 0.0, ALU.mult, ALU.add),
                           "y0" if c == 3 else None)
                v.mark("a_done")

            def v_b_conv():
                dve.wait_ge(sem("proj_out"), 16)
                for c in range(12):
                    conv(qkv[:, c, :], qkv_pad, V_CONV_B, 12, c)
                v.mark("b_conv")

            def v_b_norm():
                v.see("b_rs")
                stt(qkv[:, 0:4, :], qkv[:, 0:4, :], 128 ** -0.5, nsq[:, 0:4, :], ALU.mult, ALU.mult)
                tt(qkv[:, 4:8, :], qkv[:, 4:8, :], nsq[:, 4:8, :], ALU.mult, "b_normed")

            def v_c_z(hp):
                v.see("c_act")
                stt(c_e[:, :, :], c_zs[:, :, :], -1.0, c_zs[:, :, :], ALU.mult, ALU.min, "c_dve")
                v.see("c_act")
                stt(c_sp[:, :, :], c_zs[:, :, :], 0.0, c_e[:, :, :], ALU.max, ALU.add)
                tt(c_sp[:, :, :], c_sp[:, :, :], over(mask3[:, :], 2), ALU.mult, "c_sp")

            def v_c_cum(hp):
                v.see("c_cum")
                if hp:
                    dve.wait_ge(sem("c_o"), hp)
                stt(c_w[:, :, :], P[:, 4:6, 0:384], -1.0, c_zs[:, :, :], ALU.mult, ALU.add)
                stt(c_w[:, :, :], c_w[:, :, :], 0.0, over(neg3[:, :], 2), ALU.min, ALU.add, "c_dve")

            def v_d_gate():
                dve.wait_ge(sem("c_o"), 4)
                v.done(dve.memset(d_reset[:, :], 1.0))
                v.done(dve.memset(d_reset[:, 0::16], 0.0))
                v.see("d_psum")
                for c in range(4):
                    ts(d_y[:, c * S:c * S + S], P[:, 2 + c // 2, (c % 2) * S:(c % 2) * S + S],
                       cols[:, V_BGLA + c:V_BGLA + c + 1], -1.0, ALU.add, ALU.mult)
                stt(d_e[:, :], d_y[:, :], -1.0, d_y[:, :], ALU.mult, ALU.min, "d_dve")
                v.see("d_act")
                stt(d_e[:, :], d_y[:, :], 0.0, d_e[:, :], ALU.max, ALU.add)
                v.done(dve.tensor_tensor_scan(d_B[:, :], d_reset[:, :], d_e[:, :], 0.0, ALU.mult, ALU.add), "d_dve")
                B4 = d_B[:, :].rearrange("p (c k) -> p c k", k=16)
                tt(d_kd[:, :, :].rearrange("p h (c k) -> p (h c) k", k=16), B4[:, :, 15:16].to_broadcast([128, 64, 16]), B4, ALU.subtract, "d_dve")
                v.see("d_act")
                q4, k4 = (x[:, :, :].rearrange("p a b -> p (a b)") for x in (gl_q, gl_k))
                v.see("d_act")
                tt(d_kd[:, :, :].rearrange("p a b -> p (a b)"), d_kd[:, :, :].rearrange("p a b -> p (a b)"), k4, ALU.mult)
                tt(q4, q4, d_y[:, :], ALU.mult)
                tt(k4, k4, d_e[:, :], ALU.mult, "d_q")

            def v_d_attn():
                v.see("d_psum")
                tt(d_at[:, :, :], P[:, 4:6, :].rearrange("p i (h s) -> p (i h) s", s=128), over(tri16[:, :], 8), ALU.mult)
                v.see("d_psum")
                for e in range(2):
                    ts(d_kn[:, e, :, :], P[:, 6:8, :].rearrange("p i (h s) -> p (i h) s", s=128), parity[:, e:e + 1],
                       name="d_am" if e else None)

            def v_d_chunk(c):
                if c == 15:
                    return
                v.see("d_psum")
                if c >= 2:
                    dve.wait_ge(sem("d_I"), c - 1)
                if c == 0:
                    copy(d_S[:, 0, :], P[:, 2, :], "d_S")
                    return
                for hh in range(4):
                    r = slice(hh * 128, hh * 128 + 128)
                    stt(d_S[:, c % 2, r], d_S[:, (c - 1) % 2, r], d_gl[:, hh, c:c + 1], P[:, 2 + c % 2, r],
                        ALU.mult, ALU.add, "d_S" if hh == 3 else None)

            def branch_end(rs, bank, scale_col, gate, y, name):
                tt(rs, rs, P[:, bank:bank + 2, :].rearrange("p a b -> p (a b)"), ALU.mult)
                stt(y[:, :, :].rearrange("p a b -> p (a b)"), rs, cols[:, scale_col:scale_col + 1],
                    gate[:, :, :].rearrange("p a b -> p (a b)"), ALU.mult, ALU.mult, name)

            def v_d_end():
                v.see("d_act")
                branch_end(d_e[:, :], 4, V_ND, gate_d, yT[3], "y3")

            def v_b_rows():
                for i in range(2):
                    for hh in range(4):
                        c = 4 * i + hh
                        ts(b_r1[:, c, :], tri64[:, :], small[:, 24 + c:25 + c])
                        ts(b_r2[:, c, :], ident[:, :], small[:, 16 + c:17 + c], name="b_R" if c == 7 else None)

            def v_b_decay():
                v.see("b_rows")
                copy(small[:, 72:88], P[:, 6, 0:16])
                for s in range(2):
                    copy(small[:, 88:104].rearrange("p (i s k) -> p i s k", s=2, k=4)[:, :, s, :],
                         P[:, 6 + s, 16:24].rearrange("p (i k) -> p i k", k=4))
                for u in range(8):
                    ts(b_dm[:, u, :], P[:, 2 + u // 4, (u % 4) * 128:(u % 4) * 128 + 128], small[:, 72 + u:73 + u], 0.0,
                       ALU.subtract, ALU.min, name="b_dif" if u == 7 else None)
                tt(small[:, 80:88], small[:, 80:88], small[:, 72:80], ALU.subtract, "b_st")
                v.see("b_act")
                tt(small[:, 104:112], small[:, 72:80], small[:, 16:24], ALU.mult)
                v.see("b_act")
                tt(b_dm[:, :, :], b_dm[:, :, :], over(tri64[:, :], 8), ALU.mult)
                tt(b_r1[:, :, :], b_dm[:, :, :], P[:, 4:6, :].rearrange("p i (h s) -> p (i h) s", s=128), ALU.mult, "b_dm")

            def v_b_kk():
                v.see("b_kk")
                tt(b_N[:, :, :], b_r1[:, :, :], P[:, 2:4, :].rearrange("p i (h s) -> p (i h) s", s=128), ALU.mult)
                tt(b_at[:, :, :], b_dm[:, :, :], P[:, 6:8, :].rearrange("p i (h s) -> p (i h) s", s=128), ALU.mult)
                tt(b_XT[:, :, :], b_N[:, :, :], over(masks[:, 0, :], 8), ALU.mult)
                tt(b_XT[:, :, :], over(ident[:, :], 8), b_XT[:, :, :], ALU.subtract, "b_X0")

            def v_b_nat():
                v.see("b_nat")
                kp = P[:, 2:4, :].rearrange("p i (h s) -> p (i h) s", s=128)
                vp = P[:, 4:6, :].rearrange("p i (h s) -> p (i h) s", s=128)
                tt(b_kbg[:, :, :], kp, along(small[:, 104:112], 128), ALU.mult)
                tt(b_kd[:, :, :], kp, along(small[:, 80:88], 128), ALU.mult)
                tt(b_vb[:, :, :], vp, along(small[:, 16:24], 128), ALU.mult)
                v.see("b_act")

            def v_b_y(lv):
                tt(b_Nl[:, :, :], b_N[:, :, :], over(masks[:, lv, :], 8), ALU.mult, "b_Nl")

            def v_b_xy(lv):
                v.see("b_XY")
                if lv < 5:
                    tt(b_X[:, :, :], b_X[:, :, :], P[:, 4:6, :].rearrange("p i (h s) -> p (i h) s", s=128), ALU.subtract)
                tt(b_XT[:, :, :], b_XT[:, :, :], P[:, 6:8, :].rearrange("p i (h s) -> p (i h) s", s=128), ALU.subtract,
                   "b_inv" if lv == 5 else None)

            def v_b_uw():
                for i in range(2):
                    tt(b_qd[:, 4 * i:4 * i + 4, :], qkv[:, 0:4, i * 128:i * 128 + 128], b_eg[:, 4 * i:4 * i + 4, :], ALU.mult)
                v.see("b_act")
                v.mark("b_uws")

            def v_b_w(c):
                i, b = c // 2, 64 * (c % 2)
                r = slice(b, b + 64)
                if c == 0:
                    copy(b_vn[r, :, :], b_u[r, 0:4, :], "b_vn")
                    return
                v.see("b_wS")
                tt(b_vn[r, :, :], b_u[r, 4 * i:4 * i + 4, :], P[r, 2, :].rearrange("p (h s) -> p h s", s=128), ALU.subtract, "b_vn")

            def v_b_o(c):
                v.see("b_o")
                if c == 3:
                    return
                if c == 0:
                    copy(b_S[:, :, :], P[:, 3, :].rearrange("p (h s) -> p h s", s=128), "b_St")
                    return
                tt(b_S[:, :, :], b_S[:, :, :], along(small[:, 88 + 4 * c:92 + 4 * c], 128), ALU.mult)
                tt(b_S[:, :, :], b_S[:, :, :], P[:, 3, :].rearrange("p (h s) -> p h s", s=128), ALU.add, "b_St")

            def v_b_end():
                v.see("b_act")
                branch_end(b_sq[:, :, :].rearrange("p a b -> p (a b)"), 6, V_NB, gate_b, yT[1], "y1")
                v.mark("b_read")

            def v_merge(k):
                d = k % DT
                v.see("sg")
                if d % 4 == 3:
                    v.mark("unit_used", 3)
                p = P[:, k % 2, S:2 * S]
                if k < DT:
                    tt(merged[:, d, :], sg[:, k % 2, :], p, ALU.mult, "merged")
                else:
                    tt(tmpm[:, :], sg[:, k % 2, :], p, ALU.mult)
                    tt(merged[:, d, :], merged[:, d, :], tmpm[:, :], ALU.add, "merged")

            nothing = lambda *x: None
            dve_steps = {"small": v_small, "proj": nothing, "a_conv": v_a_conv, "a_gates": v_a_gates, "b_conv": v_b_conv,
                         "b_norm": v_b_norm, "c_z": v_c_z, "c_cum": v_c_cum, "c_out": nothing, "d_gate": v_d_gate,
                         "d_attn": v_d_attn, "d_intra": nothing, "d_chunk": v_d_chunk, "d_end": v_d_end,
                         "b_rows": v_b_rows, "b_decay": v_b_decay, "b_kk": v_b_kk, "b_nat": v_b_nat, "b_y": v_b_y,
                         "b_xy": v_b_xy, "b_uw": v_b_uw, "b_w": v_b_w, "b_o": v_b_o, "b_end": v_b_end, "merge": v_merge}

            def layer_norm(g, b, name):
                for i in range(2):
                    for c in range(2):
                        v.done(dve.bn_stats(st[:, 20 + 6 * c:26 + 6 * c], xs[:, i, c * 512:c * 512 + 512]))
                    v.done(dve.bn_aggr(st[:, 2 * i:2 * i + 2], st[:, 20:32].rearrange("p (c k) -> p c k", k=6)))
                for i in range(2):
                    copy(st[:, 4 + i:5 + i], st[:, 2 * i + 1:2 * i + 2], "var" if i else None)
                v.see("rs")
                for i in range(2):
                    ts(xs[:, i, :], xs[:, i, :], st[:, 2 * i:2 * i + 1], st[:, 4 + i:5 + i], ALU.subtract, ALU.mult)
                tt(xs[:, :, :], xs[:, :, :], over(rowbc[:, g, :], 2), ALU.mult)
                tt(xs[:, :, :], xs[:, :, :], over(rowbc[:, b, :], 2), ALU.add, name)

            def route():
                s = lambda k: rt[:, k, :]
                g4 = lambda ap: ap.rearrange("p (i g e) -> p i g e", i=2, e=4)
                v.see("sc")
                tt(s(0).rearrange("p (i e) -> p i e", i=2), sc[:, :].rearrange("p (i e) -> p i e", i=2), over(rt[:, 15, 0:16], 2), ALU.add)
                b4 = g4(s(0)).rearrange("p i g e -> p (i g) e")
                gs, pair = s(1)[:, 0:8], s(2)[:, 0:8]
                first_pair = True
                for x in range(4):
                    for y in range(x + 1, 4):
                        tt((gs if first_pair else pair).unsqueeze(2), b4[:, :, x:x + 1], b4[:, :, y:y + 1], ALU.add)
                        if not first_pair:
                            tt(gs, gs, pair, ALU.max)
                        first_pair = False

                def first_best(vals, n, dst, cum):
                    v3 = vals.rearrange("p (i n) -> p i n", i=2)
                    d3 = dst.rearrange("p (i n) -> p i n", i=2)
                    v.done(dve.tensor_reduce(s(3)[:, 0:2], v3, AX.X, ALU.max))
                    tt(d3, v3, along(s(3)[:, 0:2], n), ALU.is_equal)
                    for i in range(2):
                        v.done(dve.tensor_tensor_scan(cum[:, i * n:i * n + n], ones[:, 0:n], dst[:, i * n:i * n + n], 0.0,
                                                      ALU.mult, ALU.add))
                    stt(dst, cum, 1.0, dst, ALU.is_equal, ALU.mult)

                first_best(gs, 4, s(4)[:, 0:8], s(5)[:, 0:8])
                ts(s(6)[:, 0:8], s(4)[:, 0:8], -1.0, BIG, ALU.add, ALU.mult)
                tt(s(7).rearrange("p (g e) -> p g e", e=4), b4, along(s(6)[:, 0:8], 4), ALU.add)
                first_best(s(7), 16, s(8), s(9))
                stt(s(7), s(8), -BIG, s(7), ALU.mult, ALU.add)
                first_best(s(7), 16, s(10), s(9))
                tt(s(8), s(8), s(10), ALU.add)
                tt(s(8), s(8), sc[:, :], ALU.mult)
                v.done(dve.tensor_reduce(s(3)[:, 0:2], s(8).rearrange("p (i n) -> p i n", i=2), AX.X, ALU.add))
                recip(s(3)[:, 0:2], s(3)[:, 0:2])
                tt(comb[:, :].rearrange("p (i n) -> p i n", i=2), s(8).rearrange("p (i n) -> p i n", i=2), along(s(3)[:, 0:2], 16), ALU.mult)
                ts(xs[:, :, :], xs[:, :, :], DN_ALPHA)

            def hidden(k, p, r, h0):
                dve.wait_ge(sem("silu"), r * 4 + (h0 + k + 1))
                dve.tensor_tensor(hid[0:p, k, :], silu[0:p, k % 2, :], P[0:p, k % 2, S:2 * S], ALU.mult).then_inc(sem("hid"), 1)

            def ada_chunk(j, r, prior=True):
                dve.wait_ge(sem("ada%d" % j), r * 16 + 16)
                if j == 0 and prior:
                    dve.wait_ge(sem("ada_read"), r)
                dve.tensor_scalar(acc[:, j, :], ada[:, j, 0, :], cols[:, V_C:V_C + 1], None, ALU.mult).then_inc(sem("ada_step"), 1)
                for d in range(1, DT):
                    dve.wait_ge(sem("ada_step"), r * 28 + (7 * j + d))
                    x = dve.scalar_tensor_tensor(out=acc[:, j, :], in0=ada[:, j, d, :], scalar=cols[:, V_C + d:V_C + d + 1],
                                                 in1=acc[:, j, :], op0=ALU.mult, op1=ALU.add)
                    x.then_inc(sem("ada_step" if d < DT - 1 else "ada_used"), 1)

            def add_expert(e, r):
                dve.wait_ge(sem("expert_out"), r)
                dve.sem_inc(sem("unit_used"), 1)
                dve.wait_ge(sem("y_added"), r - 1)
                for b in range(4):
                    i, c = b // 2, b % 2
                    x = dve.scalar_tensor_tensor(out=xs[:, i, c * 512:c * 512 + 512], in0=P[:, 4 + b, :],
                                                 scalar=comb[:, bass.ds(e + 16 * i, 1)], in1=xs[:, i, c * 512:c * 512 + 512],
                                                 op0=ALU.mult, op1=ALU.add)
                x.then_inc(sem("y_added"), 1)

            tiles = [0]

            def v_experts():
                take_xT()
                route()
                v.see("cond")
                for k in range(4):
                    hidden(k, 128, 0, 0)
                    ada_chunk(k, 0, False)
                with dve.Fori(0, EXPERTS - 1) as r:
                    hidden(0, 128, r, 4)
                    add_expert(r, r + 1)
                    ada_chunk(0, r + 1)
                    for k in range(1, 4):
                        hidden(k, 128, r, 4)
                        ada_chunk(k, r + 1)
                add_expert(EXPERTS - 1, EXPERTS)
                dve.wait_ge(sem("y_added"), EXPERTS)
                tiles[0] += 4 * EXPERTS
                dve.wait_ge(sem("ada_read"), EXPERTS)
                copy(adac[:, :], P[0:96, 2, 0:192], "adac")
                v.see("modt")
                for l in range(2):
                    tt(modr[:, l, :], P[0:96, 3, l * 128:l * 128 + 96], adab[:, l, :], ALU.add, "modr" if l else None)
                v.mark("modr_read")
                layer_norm(2, 3, "x_final" if last == 1 else "x_ready2")
                v.mark("pre_free")

            def before(n):
                k = n - max(first, 2)
                dve.wait_ge(sem("pre_here"), 48 * (k + 1))
                stt(rowbc[:, 1, :], rowbc[:, 1, :], 1.0, rowbc[:, 0, :], ALU.add, ALU.mult)
                v.see("rs_in")
                for i in range(2):
                    stt(h[:, i, :], xs[:, i, :], st[:, 8 + i:9 + i], rowbc[:, 1, :], ALU.mult, ALU.mult)
                tt(h[:, :, :], h[:, :, :], over(rowbc[:, 2, :], 2), ALU.add, "h_ready")
                v.mark("pre_free")
                take_xT()
                dve.wait_ge(sem("post_here"), 32 * (k + 1))
                stt(rowbc[:, 4, :], rowbc[:, 4, :], 1.0 if (n - 2) % 3 == 1 else 0.5, rowbc[:, 3, :], ALU.mult, ALU.mult)

            def after(n):
                v.see("y_ss")
                v.done(dve.tensor_reduce(st[:, 16:18], st[:, 12:16].rearrange("p (i c) -> p i c", c=2), AX.X, ALU.add), "y_sum")
                v.see("y_rs")
                for b in range(4):
                    i, c = b // 2, slice((b % 2) * 512, (b % 2) * 512 + 512)
                    stt(h[:, i, c], P[:, 4 + b, :], st[:, 16 + i:17 + i], rowbc[:, 4, c], ALU.mult, ALU.mult)
                tt(xs[:, :, :], xs[:, :, :], h[:, :, :], ALU.add, "x_final" if n == last else "x_ready2")
                if n < last:
                    v.mark("post_free")

            def v_ffn():
                h0 = tiles[0]
                for k in range(4):
                    hidden(k, 128, 0, h0)
                with dve.Fori(0, 4) as r:
                    for k in range(4):
                        hidden(k, 128, r, h0 + 4)
                hidden(0, 128, 0, h0 + 20)
                hidden(1, 64, 0, h0 + 20)
                tiles[0] += 22

            def apply_rope(i, c0, heads):
                x = proj[:, i, c0:c0 + 64 * heads].rearrange("p (h d) -> p h d", d=64)
                x1, x2 = x[:, :, 0:8], x[:, :, 8:16]
                w = [big[:, k, 0:8 * heads].rearrange("p (h d) -> p h d", d=8) for k in range(4)]
                sin, cos = over(rope[:, i, 0, :], heads), over(rope[:, i, 1, :], heads)
                tt(w[0], x1, cos, ALU.mult)
                tt(w[1], x2, sin, ALU.mult)
                tt(w[2], x2, cos, ALU.mult)
                tt(w[3], x1, sin, ALU.mult)
                tt(x1, w[0], w[1], ALU.subtract)
                tt(x2, w[2], w[3], ALU.add)

            def probs_rows(i, mask):
                kw = 128 * (i + 1)
                v.see("s_psum")
                s4 = halves(0)[:, :, 0:kw]
                stt(big[:, :, 0:kw], s4, 64 ** -0.5, over(mask, 4), ALU.mult, ALU.add, "s_read")
                v.done(dve.tensor_reduce(st[:, 24:28], big[:, :, 0:kw], AX.X, ALU.max))
                ts(st[:, 24:28], st[:, 24:28], -1.0, name="nmax")
                v.see("exps")
                recip(st[:, 28:32], st[:, 28:32])

            def v_sparse():
                dve.wait_ge(sem("proj_out"), proj_before[0] + 14)
                proj_before[0] += 14
                for i in range(2):
                    apply_rope(i, 0, 17)
                    apply_rope(i, 1152, 9)
                v.mark("roped")
                for i in range(2):
                    for e in range(2):
                        copy(dup[:, i, 64 * e:64 * e + 64], proj[:, i, 1024:1088])
                        copy(big[:, 0, 128 * i + 64 * e:128 * i + 64 * e + 64], proj[:, i, 1664:1728],
                             "dup" if i + e == 2 else None)
                n = 0
                for i in range(2):
                    kw = 128 * (i + 1)
                    w8 = st[:, 40:48]
                    ts(w8, proj[:, i, 1728:1736], float(np.float32(8 ** -0.5 * 64 ** -0.5)))
                    for hh in range(8):
                        v.see("idx_relu")
                        if hh == 0:
                            ts(score[:, 0:kw], wk[:, n % 2, 0:kw], w8[:, 0:1], name="idx_add")
                        else:
                            stt(score[:, 0:kw], wk[:, n % 2, 0:kw], w8[:, hh:hh + 1], score[:, 0:kw], ALU.mult, ALU.add, "idx_add")
                        n += 1
                    d0 = 128 * i
                    tt(score[:, d0:d0 + 128], score[:, d0:d0 + 128], causal_neg[:, :], ALU.add)
                    best = st[:, 48:56]
                    src = score[:, 0:kw]
                    for k in range(TOPK // 8):
                        v.done(dve.max(best, src))
                        if k < TOPK // 8 - 1:
                            v.done(dve.match_replace(rl[:, 0:kw], best, src, -3e38))
                            src = rl[:, 0:kw]
                    thr = best[:, 7:8]
                    m = keep[:, i, 0:kw]
                    more, same, cum = big[:, 1, 0:kw], big[:, 2, 0:kw], big[:, 3, 0:kw]
                    ts(more, score[:, 0:kw], thr, None, ALU.is_gt)
                    ts(same, score[:, 0:kw], thr, None, ALU.is_equal)
                    v.done(dve.tensor_reduce(st[:, 32:33], more, AX.X, ALU.add))
                    ts(st[:, 32:33], st[:, 32:33], -1.0, float(TOPK), ALU.mult, ALU.add)
                    v.done(dve.tensor_tensor_scan(cum, ones256[:, 0:kw], same, 0.0, ALU.mult, ALU.add))
                    stt(m, cum, st[:, 32:33], same, ALU.is_le, ALU.mult)
                    tt(m, m, more, ALU.add)
                    ts(m, m, -1.0, BIG, ALU.add, ALU.mult)
                    tt(keep[:, i, d0:d0 + 128], keep[:, i, d0:d0 + 128], causal_neg[:, :], ALU.add)
                for n in range(8):
                    i, hg = n // 4, n % 4
                    kw = 128 * (i + 1)
                    probs_rows(i, keep[:, i, 0:kw])
                    if n >= 1:
                        dve.wait_ge(sem("pt"), pt_count(n))
                    tt(pr[:, :, 0:kw], big[:, :, 0:kw], along(st[:, 28:32], kw), ALU.mult, "p_ready")

            def pt_count(n):
                return n if n <= 4 else 4 + 2 * (n - 4)

            proj_before = [48 if first == 0 else 0]

            def v_differential():
                n_pt = 12 if first <= 3 else 0
                dve.wait_ge(sem("lam_here"), 16)
                lam = lamb[:, :].rearrange("p (a b c) -> p a b c", a=2, b=2)
                tt(oT[:, 1, 0:128].rearrange("p (a c) -> p a c", a=2), lam[:, :, 0, :], lam[:, :, 1, :], ALU.mult)
                v.done(dve.tensor_reduce(st[:, 56:58], oT[:, 1, 0:128].rearrange("p (a c) -> p a c", a=2), AX.X, ALU.add), "lam_in")
                v.see("lam_exp")
                tt(st[:, 58:59], st[:, 56:57], st[:, 57:58], ALU.subtract)
                ts(st[:, 58:59], st[:, 58:59], LAM_INIT, None, ALU.add)
                dve.wait_ge(sem("proj_out"), proj_before[0] + 24)
                for i in range(2):
                    apply_rope(i, 0, 32)
                v.mark("roped")
                v.done(dve.memset(keep[:, 1, 0:128], 0.0))
                copy(keep[:, 1, 128:256], causal_neg[:, :])
                for n in range(8):
                    i, hg = n // 4, n % 4
                    kw = 128 * (i + 1)
                    probs_rows(i, keep[:, 1, 128:256] if i == 0 else keep[:, 1, :])
                    ts(st[:, 29:32:2], st[:, 29:32:2], st[:, 58:59])
                    if n >= 1:
                        dve.wait_ge(sem("pt"), n_pt + n)
                    for k in range(2):
                        ts(big[:, 2 * k + 1, 0:kw], big[:, 2 * k + 1, 0:kw], st[:, 29 + 2 * k:30 + 2 * k])
                        stt(pr[:, k, 0:kw], big[:, 2 * k, 0:kw], st[:, 28 + 2 * k:29 + 2 * k], big[:, 2 * k + 1, 0:kw],
                            ALU.mult, ALU.subtract, "p_ready" if k else None)
                ts(st[:, 59:60], cols[:, V_SUB:V_SUB + 1], 1.0 - LAM_INIT)
                v.see("o_rs")
                stt(oT[:, :, :].rearrange("p a b -> p (a b)"), sq_o[:, :], st[:, 59:60], P[:, 4:8, :].rearrange("p a b -> p (a b)"),
                    ALU.mult, ALU.mult, "o_normed")

            v.see("consts")
            rope_angles()
            v.see("cols_psum")
            copy(cols[:, :], P[:, 7, 0:128], "cols_ready")
            if first == 0:
                take_xT()
                for step in STEPS:
                    dve_steps[step[0]](*step[1:])
                v.see("mixer_out")
                v.mark("unit_used")
                for b in range(4):
                    i, c = b // 2, slice((b % 2) * 512, (b % 2) * 512 + 512)
                    stt(xs[:, i, c], xs[:, i, c], DN_ALPHA, P[:, 4 + b, :], ALU.mult, ALU.add)
                dve.wait_ge(sem("ln_here"), 64)
                layer_norm(0, 1, "x_final" if last == 0 else "x_ready")
                v.mark("mixed")
            if first > 0:
                dve.wait_ge(sem("x_here"), 16)
            if first <= 1 <= last:
                v_experts()
            for n in range(max(first, 2), last + 1):
                before(n)
                sub = (n - 2) % 3
                if sub != 1:
                    v_ffn()
                elif n == 3:
                    v_sparse()
                else:
                    v_differential()
                after(n)


def kernel(**inputs):
    import concourse.bacc as bacc
    from concourse.bass_utils import run_bass_kernel_spmd

    nc = bacc.Bacc("TRN2", target_bir_lowering=False, num_devices=1)
    arrays, aps = {}, {}
    for name, a in inputs.items():
        a = np.ascontiguousarray(a)
        arrays["in_" + name] = a
        aps[name] = nc.dram_tensor("in_" + name, a.shape, mybir.dt.from_np(a.dtype), kind="ExternalInput").ap()
    out = nc.dram_tensor("out", (1, S, D), F32, kind="ExternalOutput").ap()
    build(nc, aps, out)
    return run_bass_kernel_spmd(nc, [arrays], core_ids=[0]).results[0]["out"]
```

```python
import math
from collections import Counter
from contextlib import ExitStack

import numpy as np

import concourse.bass as bass
from concourse import mybir

F32 = mybir.dt.float32
I32 = mybir.dt.int32
F32R = mybir.dt.float32r
ALU = mybir.AluOpType
ACT = mybir.ActivationFunctionType
AX = mybir.AxisListType

S = 256
D = 1024
DT = D // 128
LRU, BRANCH, HEADS = 512, 512, 4
EXPERTS, D_EXPERT = 16, 512
D_FF = 2752
A_IN, DIFF_IN = 1736, 3072
TOPK = 64
DN_ALPHA = 2 ** 0.25
LN_EPS, EPS = 1e-5, 1e-6
BIG = 1e30
LAM_INIT = 0.8 - 0.6 * math.exp(-0.3 * 1)

R = 6
UNIT = 2048
N_MOD = 9 * D
CH = 2 * N_MOD // EXPERTS // 3
N_COLS = N_MOD // 128
FF_GROUPS = (D_FF + 255) // 256
FF_DONE = 256 * FF_GROUPS - D_FF

C_A, C_GDN, C_BETA, C_GATE_B, C_SB, C_GLA, C_LR, C_GATE_D, C_MERGE = (
    0, 512, 2048, 2056, 2568, 4104, 5640, 5656, 6168)
V_CONV_A, V_CONV_AB, V_BA, V_BX, V_LAM, V_BGLA, V_NB, V_ND, V_SUB, V_CONV_B, V_C = (
    0, 16, 20, 24, 28, 32, 36, 37, 38, 40, 88)

BRANCH_ORDER = [0, 2, 3, 1]

PROJ_UNITS = {"a": 2, "b": 8, "c": 6, "d": 8}
STEPS = [("proj", w, u) for w in "abcd" for u in range(PROJ_UNITS[w])]


def _put(after, steps):
    k = STEPS.index(after) + 1
    STEPS[k:k] = steps


_put(("proj", "a", 1), [("cols",), ("small",), ("a_conv",)])
_put(("proj", "b", 3), [("angles",)])
_put(("proj", "b", 7), [("a_gates",)])
_put(("proj", "c", 0), [("a_mult",)])
_put(("proj", "c", 1), [("a_scan",)])
_put(("proj", "c", 5), [("b_conv",)])
_put(("proj", "d", 3), [("b_norm",)])


def _weave(steps, tiles):
    out, put = [], 0
    for n, s in enumerate(steps):
        out.append(s)
        while put < len(tiles) and put * len(steps) < (n + 1) * len(tiles):
            out.append(tiles[put])
            put += 1
    return out + tiles[put:]


_MERGE = [("merge", k) for k in range(4 * DT)]
for hp in range(4):
    STEPS += [("c_z", hp), _MERGE[2 * hp], ("c_cum", hp), _MERGE[2 * hp + 1], ("c_out", hp)]
STEPS += [("d_gate",), _MERGE[8], _MERGE[9], ("d_attn",), _MERGE[10], ("d_intra",)]
STEPS += _weave([("d_chunk", c) for c in range(16)], _MERGE[11:14])
STEPS += [("d_end",), _MERGE[14], _MERGE[15], ("b_rows",), _MERGE[16], _MERGE[17], ("b_decay",), ("b_kk",), _MERGE[18],
          ("b_nat",), _MERGE[19]]
STEPS += _weave([(s, lv) for lv in range(1, 6) for s in ("b_y", "b_xy")]
                + [("b_uw",)] + [(s, c) for c in range(4) for s in ("b_w", "b_o")] + [("b_end",)],
                _MERGE[20:24])
STEPS += _MERGE[24:32]


def weight_loads(A):
    out = []

    def cols(w, c0, n):
        for c in range(c0, c0 + n, 256):
            m = min(256, c0 + n - c)
            out.append((w[:, c:c + m].rearrange("(t p) n -> p t n", p=128), w.shape[0] // 128, m, 128))

    def rows(w, r0, n):
        m = max(n // 128, 1)
        p = min(n, 128)
        out.append((w[r0:r0 + n, :].rearrange("(t p) n -> p t n", p=p), m, w.shape[1], p))

    def square(w):
        for r in range(0, D, 256):
            rows(w, r, 256)

    w_in, w_branch = A["w_in"][0], A["w_branch"][0]
    for c, n in ((C_A, 512), (C_GDN, 1536), (C_GATE_B, 512), (C_SB, 1536), (C_GLA, 1536), (C_GATE_D, 512)):
        cols(w_in, c, n)
    for b in BRANCH_ORDER:
        for half in range(2):
            out.append((w_branch[b][:, half * 512:half * 512 + 512].rearrange("(t p) n -> p t n", p=128),
                        4, 512, 128))
            cols(w_in, C_MERGE + b * D + half * 512, 512)
    square(A["w_out"][0])
    marks = {"moe": len(out)}
    for e in range(EXPERTS):
        for c in range(0, D_EXPERT, 256):
            cols(A["w_gate"][0][e], c, 256)
            cols(A["w_up"][0][e], c, 256)
            rows(A["w_down"][0][e], c, 256)
    for layer in range(2):
        for half in range(2):
            if half:
                mix = "dsa" if layer == 0 else "diff"
                cols(A[mix + "_w_in_2"][0], 0, A_IN if layer == 0 else DIFF_IN)
                square(A[mix + "_w_out_2"][0])
            marks[layer, half] = len(out)
            g, u, d = (A["ffn_w_%s_2" % k][layer][half] for k in ("gate", "up", "down"))
            for c in range(0, D_FF, 256):
                c = min(c, D_FF - 256)
                cols(g, c, 256)
                cols(u, c, 256)
                rows(d, c, 256)
    return out, marks


class Line:

    def __init__(self, eng, sem, own):
        self.eng, self.sem, self.own = eng, sem, own
        self.sent, self.seen = Counter(), Counter()

    def done(self, ins, name=None):
        name = name or self.own
        self.sent[name] += 1
        ins.then_inc(self.sem(name), 1)
        self.eng.wait_ge(self.sem(name), self.sent[name])

    def tell(self, ins, name, n=1):
        self.sent[name] += n
        ins.then_inc(self.sem(name), n)

    def see(self, name, k=1):
        self.seen[name] += k
        self.eng.wait_ge(self.sem(name), self.seen[name])

    def mark(self, name, n=1):
        self.sent[name] += n
        self.eng.sem_inc(self.sem(name), n)


def build(nc, A, out, first=0, last=7, mod_in=None):
    ctx = ExitStack()
    sems = {}

    def sem(name):
        if name not in sems:
            sems[name] = ctx.enter_context(nc.semaphore("s_" + name))
        return sems[name]

    def buf(name, *shape, dt=F32, ctx=ctx):
        return ctx.enter_context(nc.sbuf_tensor(name, list(shape), dt))

    loads, marks = weight_loads(A)
    starts = {0: 0, 1: marks["moe"], 2: marks[0, 0], 3: marks[0, 0] + 3 * FF_GROUPS, 4: marks[0, 1],
              5: marks[1, 0], 6: marks[1, 0] + 3 * FF_GROUPS, 7: marks[1, 1], 8: len(loads)}
    first_unit, end_unit = starts[first], starts[last + 1] + (3 if last == 1 else 0)
    split_no = {}
    split_runs = [(marks["moe"], 6 * EXPERTS)] + [(marks[l, h], 3 * FF_GROUPS) for l in range(2) for h in range(2)]
    for n in range(first_unit, end_unit):
        if any(a <= n < a + k for a, k in split_runs):
            split_no[n - first_unit] = len(split_no)

    lo_at, count = {}, Counter()
    for n in split_no:
        k = first_unit + n - marks["moe"]
        name = "w_lo_pool" if first <= 1 and k < 6 * EXPERTS + 3 and k % 3 == 2 else "w_lo"
        count[name] += 1 if name == "w_lo_pool" else 2
        lo_at[n] = name, count[name]

    def lo_wait(eng, n, r=0, back=0):
        name, c = lo_at[n]
        experts = first <= 1 and first_unit + n < marks["moe"] + 6 * EXPERTS
        eng.wait_ge(sem(name), r * (2 if name == "w_lo_pool" else 8 if experts else 12) + (c - (back if name == "w_lo" else 0)))

    def is_wide(n):
        return any(a <= n < a + k and (n - a) % 3 < 2 for a, k in split_runs)
    mod = nc.dram_tensor("modulation", (2, N_MOD), F32, kind="Internal").ap() if mod_in is None else mod_in

    with ctx:
        m0 = ExitStack()
        w_lo = buf("w_lo", 128, R, UNIT, dt=F32R, ctx=m0)
        m0.close()
        merged = buf("merged", 128, DT, S)
        ring = buf("ring", 128, R, UNIT)
        xs = buf("xs", 128, 2, D)
        xT = buf("xT", 128, DT, S)
        rowbc = buf("rowbc", 128, 5, D)
        ident = buf("ident", 128, 128)
        ones256 = buf("ones256", 128, S)
        ones = ones256[:, 0:128]
        lamb = buf("lamb", 128, S)
        cols = buf("cols", 128, 128)
        causal_neg = buf("causal_neg", 128, 128)
        causal_01 = buf("causal_01", 128, 128)
        rope = buf("rope", 128, 2, 2, 8)
        eps_ln = buf("eps_ln", 128, 2)
        st = buf("st", 128, 64)
        P = ctx.enter_context(nc.psum_tensor("P", [128, 8, 512], F32))

        m0 = ExitStack()
        masks = buf("masks", 128, 6, 128, ctx=m0)
        tri64 = buf("tri64", 128, 128, ctx=m0)
        blk64 = buf("blk64", 128, 128, ctx=m0)
        tri16 = buf("tri16", 128, 128, ctx=m0)
        suffix = buf("suffix", 128, 128, ctx=m0)
        mask3 = buf("mask3", 128, 384, ctx=m0)
        neg3 = buf("neg3", 128, 384, ctx=m0)
        parity = buf("parity", 128, 2, ctx=m0)
        small = buf("small", 128, 128, ctx=m0)
        wsm = buf("wsm", 128, DT, 24, ctx=m0)
        lrT = buf("lrT", 16, S, ctx=m0)
        wup = buf("wup", 16, 512, ctx=m0)
        yT = [buf(f"yT{b}", 128, 4, S, ctx=m0) for b in range(4)]
        sg = buf("sg", 128, 2, S, ctx=m0)
        tmpm = buf("tmpm", 128, S, ctx=m0)
        qkv = buf("qkv", 128, 12, S, ctx=m0)
        gate_b = buf("gate_b", 128, 4, S, ctx=m0)
        gate_d = buf("gate_d", 128, 4, S, ctx=m0)
        m1 = ExitStack()
        sb_q = buf("sb_q", 128, 4, S, ctx=m1)
        sb_k = buf("sb_k", 128, 4, S, ctx=m1)
        sb_v = buf("sb_v", 128, 2, 512, ctx=m1)
        gl_q = buf("gl_q", 128, 4, S, ctx=m1)
        gl_k = buf("gl_k", 128, 4, S, ctx=m1)
        gl_v = buf("gl_v", 128, 2, 512, ctx=m1)
        m2 = ExitStack()
        rowst = buf("rowst", 128, 128, ctx=m2)
        a_pad = buf("a_pad", 128, 4, S + 3, ctx=m2)
        qkv_pad = buf("qkv_pad", 128, 12, S + 3, ctx=m2)
        wbd = buf("wbd", 128, 2, 4, 128, ctx=m2)
        a_x = buf("a_x", 128, 4, S, ctx=m2)
        a_r = buf("a_r", 128, 4, S, ctx=m2)
        a_i, a_t, nsq = yT[1], yT[3], merged
        m2.close()
        m2 = ExitStack()
        c_zs = buf("c_zs", 128, 2, 384, ctx=m2)
        c_e = buf("c_e", 128, 2, 384, ctx=m2)
        c_sp = buf("c_sp", 128, 2, 384, ctx=m2)
        c_w = buf("c_w", 128, 2, 384, ctx=m2)
        m2.close()
        m2 = ExitStack()
        d_B = buf("d_B", 128, 4 * S, ctx=m2)
        d_y = buf("d_y", 128, 4 * S, ctx=m2)
        d_e = buf("d_e", 128, 4 * S, ctx=m2)
        d_reset = buf("d_reset", 128, 4 * S, ctx=m2)
        d_gl = buf("d_gl", 128, 4, 16, ctx=m2)
        d_kd = buf("d_kd", 128, 4, S, ctx=m2)
        d_at = buf("d_at", 128, 8, 128, ctx=m2)
        d_kn = buf("d_kn", 128, 2, 8, 128, ctx=m2)
        d_S = d_B[:, :].rearrange("p (a b) -> p a b", b=512)
        m2.close()
        m1.close()
        m1 = ExitStack()
        b_r1 = buf("b_r1", 128, 8, 128, ctx=m1)
        b_r2 = buf("b_r2", 128, 8, 128, ctx=m1)
        b_dm = buf("b_dm", 128, 8, 128, ctx=m1)
        b_eg = buf("b_eg", 128, 8, 128, ctx=m1)
        b_N = buf("b_N", 128, 8, 128, ctx=m1)
        b_at = buf("b_at", 128, 8, 128, ctx=m1)
        b_X = buf("b_X", 128, 8, 128, ctx=m1)
        b_XT = buf("b_XT", 128, 8, 128, ctx=m1)
        b_kbg = buf("b_kbg", 128, 8, 128, ctx=m1)
        b_kd = buf("b_kd", 128, 8, 128, ctx=m1)
        b_vb = buf("b_vb", 128, 8, 128, ctx=m1)
        b_vn = buf("b_vn", 128, 4, 128, ctx=m1)
        b_S = buf("b_S", 128, 4, 128, ctx=m1)
        b_Nl, b_Y, b_u, b_wT, b_qd, b_sq = b_r1, b_r2, b_r1, b_dm, b_eg, b_X
        m1.close()
        m0.close()

        m0 = ExitStack()
        hid = buf("hid", 128, 2, S, ctx=m0)
        hid_hi = buf("hid_hi", 128, 4, S, dt=F32R, ctx=m0)
        hid_lo = buf("hid_lo", 128, 4, S, dt=F32R, ctx=m0)
        x_hi = buf("x_hi", 128, DT, S, dt=F32R, ctx=m0)
        x_lo = buf("x_lo", 128, DT, S, dt=F32R, ctx=m0)
        silu = buf("silu", 128, 2, S, ctx=m0)
        adac = buf("adac", 128, 2 * N_COLS, ctx=m0)
        adab = buf("adab", N_COLS, 2, 128, ctx=m0)
        modr = buf("modr", N_COLS, 2, 128, ctx=m0)
        m1 = ExitStack()
        w_hi = buf("w_hi", 128, R, UNIT, dt=F32R, ctx=m1)
        ada = buf("ada", 128, 3, DT // 2, CH, ctx=m1)
        acc = buf("acc", 128, 3, CH, ctx=m1)
        wr = buf("wr", 128, DT, 16, ctx=m1)
        rt = buf("rt", 128, 16, 32, ctx=m1)
        sc = buf("sc", 128, 32, ctx=m1)
        comb = buf("comb", 128, 32, ctx=m1)
        m1.close()
        m1 = ExitStack()
        proj = buf("proj", 128, 2, DIFF_IN, ctx=m1)
        qT = buf("qT", 128, 8, S, ctx=m1)
        kT = buf("kT", 128, 8, S, ctx=m1)
        oT = buf("oT", 128, 8, S, ctx=m1)
        dup = buf("dup", 128, 2, 128, ctx=m1)
        keep = buf("keep", 128, 2, S, ctx=m1)
        big = buf("big", 128, 4, S, ctx=m1)
        pr = buf("pr", 128, 4, S, ctx=m1)
        pT = buf("pT", 128, 2, 4, 128, ctx=m1)
        h = buf("h", 128, 2, D, ctx=m1)
        m1.close()
        m0.close()
        qiT = proj[:, 0, 2048:3072].rearrange("p (a b) -> p a b", b=S)
        score = h[:, 0, 0:256]
        rl = h[:, 0, 256:512]
        wk = h[:, 0, 512:1024].rearrange("p (a b) -> p a b", b=S)
        sq_o = h[:, :, :].rearrange("p a b -> p (a b)")

        block = ctx.enter_context(nc.Block())

        AFTER = ((3, 4), (5,), (6, 7), (8,))
        HALVES = ((0,), (1, 2), (3,), (4, 5))
        LAST_AFTER = ((3,), (4, 5))
        unprimed = {n for n in (2, 4, 5, 7) if n == first or n in (4, 7)}

        def halves(bank0):
            return P[:, bank0:bank0 + 2, :].rearrange("p b (h s) -> p (b h) s", s=S)

        @block.sync
        def _(sp):
            sp.dma_start(xs[:, :, :], A["x"][0].rearrange("(i p) d -> p i d", p=128)).then_inc(sem("x_here"), 16)
            passed, after_unit = Counter(), []
            for n in range(end_unit - first_unit):
                used = "wide_used" if is_wide(first_unit + n) else "unit_used"
                passed[used] += 1
                after_unit.append((used, passed[used]))
            for n, (src, m, k, p) in enumerate(loads[first_unit:end_unit]):
                if n >= R:
                    for used, count in sorted({after_unit[n - R], after_unit[n - R + (n - R + 1 in split_no and n % R < R - 1)]}):
                        sp.wait_ge(sem(used), count)
                sp.dma_start(ring[0:p, n % R, 0:m * k].rearrange("p (m k) -> p m k", k=k), src)\
                  .then_inc(sem("unit%d" % (n % R)), 16)
            sp.wait_ge(sem("x_final"), 1)
            sp.dma_start(out[0].rearrange("(i p) d -> p i d", p=128), xs[:, :, :]).then_inc(sem("stored"), 16)
            sp.wait_ge(sem("stored"), 16)

        @block.gpsimd
        def _(pool):
            g = Line(pool, sem, "pool")

            def select(ap, pattern, base, mult, op=ALU.is_ge, fill=0.0):
                g.done(pool.affine_select(out=ap, in_=ap, compare_op=op, fill=fill, base=base, pattern=pattern,
                                          channel_multiplier=mult))

            def load(dst, src, name, **kw):
                pool.dma_start(dst, src, **kw).then_inc(sem(name), 16)

            g.done(pool.memset(ident[:, :], 0.0))
            g.done(pool.memset(ones256[:, :], 1.0))
            select(ident[:, :], [[-1, 128]], 0, 1, ALU.not_equal, 1.0)
            g.done(pool.memset(eps_ln[:, 0:1], LN_EPS))
            g.done(pool.memset(eps_ln[:, 1:2], EPS))
            g.done(pool.memset(causal_01[:, :], 1.0))
            select(causal_01[:, :], [[-1, 128]], 0, 1)
            g.done(pool.tensor_scalar(causal_neg[:, :], causal_01[:, :], -1.0, BIG, ALU.add, ALU.mult))
            g.mark("consts")
            if first == 0:
                g.tell(pool.memset(a_pad[:, :, 0:3], 0.0), "pads")
                g.tell(pool.memset(qkv_pad[:, :, 0:3], 0.0), "pads")
            load(lamb[:, :], A["diff_lambda_2"][0].rearrange("a b -> (a b)").partition_broadcast(128), "lam_here")
            load(st[:, 60:62].bitcast(I32), A["positions_2"][0].rearrange("(i p) -> p i", p=128), "pos_here",
                 allow_slow_non_contiguous=True)
            v = A["conv_a_w"][0], A["gdn_conv_w"][0]
            g.done(pool.memset(rowst[:, :], 0.0))
            tiles = [(V_CONV_A, v[0].rearrange("w (t p) -> w t p", p=128).rearrange("w t p -> (w t) p"), 16),
                     (V_CONV_B, v[1].rearrange("w (t p) -> w t p", p=128).rearrange("w t p -> (w t) p"), 48)]
            for c, name, n in ((V_CONV_AB, "conv_a_b", 4), (V_BA, "rg_b_a", 4), (V_BX, "rg_b_x", 4),
                               (V_LAM, "rg_lambda", 4), (V_BGLA, "gla_b_gate", 4), (V_NB, "gdn_norm_w", 1),
                               (V_ND, "gla_norm_w", 1), (V_SUB, "diff_subln_2", 1), (V_C, "c_2", 8)):
                tiles.append((c, A[name][0].rearrange("(t p) -> t p", p=128), n))
            for c, src, n in tiles:
                load(rowst[c:c + n, :], src, "rows_here")
            if first == 0:
                load(wsm[:, :, 0:8], A["w_in"][0][:, C_BETA:C_BETA + 8].rearrange("(t p) n -> p t n", p=128), "small_here")
                load(wsm[:, :, 8:24], A["w_in"][0][:, C_LR:C_LR + 16].rearrange("(t p) n -> p t n", p=128), "small_here")
                load(small[:, 0:4], A["gdn_dt_bias"][0].partition_broadcast(128), "small_here")
                load(small[:, 4:8], A["gdn_a_log"][0].partition_broadcast(128), "small_here")
                load(wup[:, :], A["gla_w_gate_up"][0], "wup_here")
                g.done(pool.memset(wbd[:, :, :, :], 0.0))
                for k, name in enumerate(("rg_w_a", "rg_w_x")):
                    w = A[name][0].rearrange("(t e) i j -> e i t j", e=2)
                    for e in range(2):
                        load(wbd[64 * e:64 * e + 64, k, :, 64 * e:64 * e + 64], w[e], "wbd_here")
                for k, name in enumerate(("ln1_g", "ln1_b", "ln2_g", "ln2_b")):
                    load(rowbc[:, k, :], A[name][0].partition_broadcast(128), "ln_here")
                for m, w in ((blk64, 64), (tri64, 64), (tri16, 16)):
                    g.done(pool.memset(m[:, :], 1.0))
                    v = m[:, :].rearrange("p (a b) -> p a b", b=w)
                    select(v, [[-w, 128 // w], [0, w]], 0, 1)
                    select(v, [[w, 128 // w], [0, w]], w - 1, -1)
                for m in (tri64, tri16):
                    select(m[:, :], [[1, 128]], 0, -1)
                g.done(pool.memset(suffix[:, :], 1.0))
                select(suffix[:, :], [[-1, 128]], 0, 1)
                g.done(pool.memset(mask3[:, :], 1.0))
                for b in (0, 2):
                    select(mask3[:, 128 * b:128 * b + 128], [[1, 128]], 0, -1, ALU.is_gt)
                g.done(pool.tensor_scalar(neg3[:, :], mask3[:, :], -1.0, BIG, ALU.add, ALU.mult))
                g.done(pool.memset(masks[:, :, :], 0.0))
                for lv in range(6):
                    b = 1 << lv
                    v = masks[:, lv, :].rearrange("p (n two b) -> p n two b", two=2, b=b)[:, :, 1, :]
                    g.done(pool.memset(v, 1.0))
                    select(v, [[-2 * b, 64 // b], [0, b]], 0, 1)
                    select(v, [[2 * b, 64 // b], [0, b]], b - 1, -1)
                g.done(pool.memset(small[:, 64:72], 1.0))
                for b in range(4):
                    select(small[:, 64 + b:65 + b], [[0, 1]], -32 * b, 1)
                    select(small[:, 64 + b:65 + b], [[0, 1]], 32 * b + 15, -1)
                g.done(pool.tensor_tensor(small[:, 64:66], small[:, 64:66], small[:, 66:68], ALU.add))
                g.done(pool.tensor_tensor(parity[:, 0:1], small[:, 64:65], small[:, 65:66], ALU.add))
                g.done(pool.tensor_scalar(parity[:, 1:2], parity[:, 0:1], -1.0, -1.0, ALU.add, ALU.mult))
                g.mark("masks")

            if first <= 1 <= last:
                if first == 1:
                    for k, name in ((2, "ln2_g"), (3, "ln2_b")):
                        load(rowbc[:, k, :], A[name][0].partition_broadcast(128), "ln_here")
                    for k in range(2):
                        load(rowbc[:, k, :], A["ln1_g"][0].partition_broadcast(128), "ln_here")
                else:
                    pool.wait_ge(sem("mixed"), 1)
                load(wr[:, :, :], A["w_router"].rearrange("(t p) n -> p t n", p=128), "wr_here")
                load(rt[:, 15, 0:16], A["router_bias"].partition_broadcast(128), "wr_here")
                load(adab[:, :, :], A["ada_b_2"].rearrange("l (p q) -> p l q", q=128), "wr_here")

                def half_chunk(layer, r, i, used=None):
                    if used is not None:
                        pool.wait_ge(sem("ada_half"), used)
                    src = A["ada_w_2"][layer].rearrange("(t p) n -> p t n", p=128)
                    half = i % 2 * (DT // 2)
                    pool.dma_start(ada[:, i % 3, :, :],
                                   src[:, half:half + DT // 2, bass.ds(r * (3 * CH) + i // 2 * CH, CH)])\
                        .then_inc(sem("ada%d" % (i % 3)), 16)

                def low(j, r=0):
                    n = starts[1] - first_unit + j
                    pool.wait_ge(sem("w_hi"), r * 12 + 2 * (split_no[n] + 1))
                    lo_wait(pool, n - 1, r)
                    pool.tensor_tensor(w_lo[:, n % R, :], ring[:, n % R, :], w_hi[:, n % R, :].bitcast(F32),
                                       ALU.subtract).then_inc(sem("w_lo_pool"), 1)

                def expert(layer, r, e, next_layer, next_r):
                    half_chunk(layer, r, 3, e * 6 + 1)
                    low(5, e)
                    half_chunk(layer, r, 4, e * 6 + 2)
                    half_chunk(layer, r, 5, e * 6 + 3)
                    if next_layer is not None:
                        half_chunk(next_layer, next_r, 0, e * 6 + 4)
                    low(8, e)
                    if next_layer is not None:
                        half_chunk(next_layer, next_r, 1, e * 6 + 5)
                        half_chunk(next_layer, next_r, 2, e * 6 + 6)

                for i in range(3):
                    half_chunk(0, 0, i)
                low(2)
                per_layer = EXPERTS // 2
                with pool.Fori(0, per_layer - 1) as r:
                    expert(0, r, r, 0, r + 1)
                expert(0, per_layer - 1, per_layer - 1, 1, 0)
                with pool.Fori(0, per_layer - 1) as r:
                    expert(1, r, r + per_layer, 1, r + 1)
                expert(1, per_layer - 1, EXPERTS - 1, None, None)
                g.see("modr")
                pool.dma_start(mod.rearrange("l (p q) -> p l q", q=128), modr[:, :, :]).then_inc(sem("mod_stored"), 16)
                pool.wait_ge(sem("mod_stored"), 16)

            def mod_row(layer, k):
                return mod[layer][k * D:k * D + D]

            for n in range(max(first - 2, 0), max(last - 1, 0)):
                layer, sub = n // 3, n % 3
                if first <= 1 or n > first - 2:
                    g.see("pre_free")
                load(rowbc[:, 0, :], A["pre_norm_2"][layer][sub].partition_broadcast(128), "pre_here")
                load(rowbc[:, 1, :], mod_row(layer, 3 * sub + 1).partition_broadcast(128), "pre_here")
                load(rowbc[:, 2, :], mod_row(layer, 3 * sub).partition_broadcast(128), "pre_here")
                if n > max(first - 2, 0):
                    g.see("post_free")
                load(rowbc[:, 3, :], A["post_norm_2"][layer][sub].partition_broadcast(128), "post_here")
                load(rowbc[:, 4, :], mod_row(layer, 3 * sub + 2).partition_broadcast(128), "post_here")

        @block.tensor
        def _(pe):
            t = Line(pe, sem, "pe")
            unit = [0]

            def take(ahead=0):
                n = unit[0]
                unit[0] += 1
                pe.wait_ge(sem("unit%d" % (n % R)), 16 * (n // R + 1))
                return ring[:, n % R, :]

            def mm(o, l, r, start=True, stop=True, **kw):
                return pe.matmul(o, l, r, start=start, stop=stop, **kw)

            def mm3(o, l, r, start, stop):
                mm(o, l[0], r[0], start, False)
                mm(o, l[0], r[1], False, False)
                return mm(o, l[1], r[0], False, stop)

            def turn_x(src):
                for i in range(2):
                    for b in range(2):
                        for k in range(4):
                            c = 4 * b + k
                            last_t = pe.transpose(P[:, 4 + 2 * i + b, k * 128:k * 128 + 128],
                                                  src[:, i, c * 128:c * 128 + 128], ident[:, :])
                        t.tell(last_t, "xt_psum%d" % b)
                t.see("xt_dve", 2)
                t.see("xt_act", 2)

            def square_out(lhs, tiles=8):
                for u in range(4):
                    w = take().rearrange("p (m n) -> p m n", n=D)
                    for k in range(2):
                        for i in range(2):
                            for c in range(2):
                                x = mm(P[:, 4 + 2 * i + c, :], lhs(2 * u + k, i), w[:, k, c * 512:c * 512 + 512],
                                       start=(u + k == 0), stop=(2 * u + k == 7))
                    if u < 3:
                        t.tell(x, "unit_used")
                return x

            def tile_cm(w, c, n=128):
                k = t.sent["proj"]
                if k >= 2:
                    pe.wait_ge(sem("proj_out"), k - 1)
                for d in range(DT):
                    x = mm(P[:, k % 2, 0:S], w[:, d, c:c + 128], xT[:, d, :], start=d == 0, stop=d == DT - 1)
                t.tell(x, "proj")
                return x

            def tiles_tm(w, n=256):
                for i in range(2):
                    k = t.sent["proj"]
                    if k >= 2:
                        pe.wait_ge(sem("proj_out"), k - 1)
                    for d in range(DT):
                        x = mm(P[:, k % 2, 0:n], xT[:, d, i * 128:i * 128 + 128], w[:, d, :],
                               start=d == 0, stop=d == DT - 1)
                    t.tell(x, "proj")
                return x

            def cm_units(n):
                for _ in range(n):
                    w = take().rearrange("p (m n) -> p m n", n=256)
                    for c in range(2):
                        tile_cm(w, c * 128)

            def tm_units(n, width=256):
                for _ in range(n):
                    w = take()[:, 0:DT * width].rearrange("p (m n) -> p m n", n=width)
                    tiles_tm(w, width)

            def p_cols():
                pe.wait_ge(sem("rows_here"), 16 * 11)
                t.tell(pe.transpose(P[:, 7, 0:128], rowst[:, :], ident[:, :]), "cols_psum")
                t.see("cols_ready")

            def p_small():
                pe.wait_ge(sem("small_here"), 64)
                for i in range(2):
                    for d in range(DT):
                        mm(P[:, 2, 8 * i:8 * i + 8], xT[:, d, i * 128:i * 128 + 128], wsm[:, d, 0:8],
                           start=d == 0, stop=d == DT - 1)
                for d in range(DT):
                    x = mm(P[0:16, 3, 0:S], wsm[:, d, 8:24], xT[:, d, :], start=d == 0, stop=d == DT - 1)
                t.tell(x, "small_psum")

            def p_proj(which, u):
                if which in "cd" and u in (4, 5):
                    tm_units(1)
                else:
                    cm_units(1)

            def p_a_gates():
                pe.wait_ge(sem("wbd_here"), 64)
                t.see("masks")
                t.see("a_x")
                t.see("small_free")
                for g in range(2):
                    for c in range(4):
                        x = mm(P[:, 2 + 2 * g + c // 2, (c % 2) * S:(c % 2) * S + S], wbd[:, g, c, :], a_x[:, c, :])
                    t.tell(x, "a_ri")

            def p_b_norm():
                t.see("b_sq")
                for c in range(4):
                    x = mm(P[:, 4 + c, :], ones, nsq[:, 2 * c:2 * c + 2, :].rearrange("p a b -> p (a b)"))
                t.tell(x, "b_ss")

            def p_c_z(hp):
                if hp == 0:
                    t.see("a_done")
                    t.see("b_rs")
                    pe.wait_ge(sem("proj_out"), t.sent["proj"])
                for s in range(2):
                    r = slice(64 * s, 64 * s + 64)
                    mm(P[:, 2 + s, 0:S], sb_k[r, hp, 0:128], sb_q[r, hp, :])
                    x = mm(P[:, 2 + s, S:384], sb_k[r, hp, 128:S], sb_q[r, hp, 128:S])
                t.tell(x, "c_z")

            def p_c_cum(hp):
                t.see("c_sp")
                for s in range(2):
                    mm(P[:, 4 + s, 0:384], suffix[:, :], c_sp[:, s, :])
                    x = mm(P[:, 4 + s, 128:S], ones[:, :], c_sp[:, s, S:384], start=False, skip_group_check=True)
                t.tell(x, "c_cum")

            def p_c_out(hp):
                t.see("c_w")
                if hp >= 2:
                    pe.wait_ge(sem("y2"), hp - 1)
                for s in range(2):
                    r = slice(64 * s, 64 * s + 64)
                    c = (2 * hp + s) * 64
                    mm(P[r, 6 + hp % 2, 0:S], sb_v[:, 0, c:c + 64], c_w[:, s, 0:S])
                    x = mm(P[r, 6 + hp % 2, 128:S], sb_v[:, 1, c:c + 64], c_w[:, s, S:384], start=False,
                           skip_group_check=True)
                t.tell(x, "c_o")

            def p_d_gate():
                pe.wait_ge(sem("wup_here"), 16)
                for c in range(4):
                    x = mm(P[:, 2 + c // 2, (c % 2) * S:(c % 2) * S + S], wup[:, c * 128:c * 128 + 128], lrT[:, :])
                t.tell(x, "d_psum")

            def p_d_attn():
                t.see("d_q")
                pe.wait_ge(sem("y2"), 4)
                for i in range(2):
                    for hh in range(4):
                        r = slice(i * 128, i * 128 + 128)
                        x = mm(P[:, 4 + i, hh * 128:hh * 128 + 128], gl_k[:, hh, r], gl_q[:, hh, r])
                t.tell(x, "d_psum")
                for i in range(2):
                    for hh in range(4):
                        x = pe.transpose(P[:, 6 + i, hh * 128:hh * 128 + 128], d_kd[:, hh, i * 128:i * 128 + 128], ident[:, :])
                t.tell(x, "d_psum")

            def p_d_intra():
                t.see("d_am")
                for hh in range(4):
                    for i in range(2):
                        o = (hh % 2) * S + i * 128
                        mm(P[:, 4 + hh // 2, o:o + 128], gl_v[:, i, hh * 128:hh * 128 + 128], d_at[:, 4 * i + hh, :],
                           start=(hh % 2 == 0 and i == 0), skip_group_check=True)

            def p_d_chunk(c):
                if c < 15:
                    if c >= 2:
                        pe.wait_ge(sem("d_S"), c - 1)
                    i, b = c // 8, (c % 8) // 2
                    r = slice(32 * b, 32 * b + 32)
                    for hh in range(4):
                        x = mm(P[:, 2 + c % 2, hh * 128:hh * 128 + 128], d_kn[r, c % 2, 4 * i + hh, :],
                               gl_v[r, i, hh * 128:hh * 128 + 128])
                    t.tell(x, "d_psum")
                if c >= 1:
                    pe.wait_ge(sem("d_S"), c)
                    for hh in range(4):
                        o = (hh % 2) * S + c * 16
                        x = mm(P[:, 4 + hh // 2, o:o + 16], d_S[:, (c - 1) % 2, hh * 128:hh * 128 + 128],
                               gl_q[:, hh, c * 16:c * 16 + 16], start=False, skip_group_check=True)
                    t.tell(x, "d_I")

            def norm_sum(bank, name_in, name_out, sq):
                t.see(name_in)
                for b in range(2):
                    x = mm(P[:, bank + b, :], ones[:, :], sq[:, b * 512:b * 512 + 512])
                t.tell(x, name_out)

            def p_d_end():
                norm_sum(6, "d_sq", "d_ss", d_e)

            def p_b_rows():
                t.see("b_dve")
                pe.wait_ge(sem("y3"), 1)
                for i in range(2):
                    mm(P[:, 2 + i, :], ones[:, :], b_r1[:, 4 * i:4 * i + 4, :].rearrange("p a b -> p (a b)"))
                    mm(P[:, 4 + i, :], ones[:, :], b_r2[:, 4 * i:4 * i + 4, :].rearrange("p a b -> p (a b)"))
                for i in range(2):
                    gi = small[:, 24 + 4 * i:28 + 4 * i]
                    mm(P[:, 6, 4 * i:4 * i + 4], tri64[:, :], gi)
                    mm(P[:, 6, 8 + 4 * i:12 + 4 * i], blk64[:, :], gi)
                    for s in range(2):
                        r = slice(64 * s, 64 * s + 64)
                        x = mm(P[:, 6 + s, 16 + 4 * i:20 + 4 * i], ones[r, :], small[r, 24 + 4 * i:28 + 4 * i])
                t.tell(x, "b_rows")

            def p_b_decay():
                pass

            def p_b_kk():
                t.see("b_dve")
                for i in range(2):
                    r = slice(i * 128, i * 128 + 128)
                    for hh in range(4):
                        mm(P[:, 2 + i, hh * 128:hh * 128 + 128], qkv[:, 4 + hh, r], qkv[:, 4 + hh, r])
                        x = mm(P[:, 6 + i, hh * 128:hh * 128 + 128], qkv[:, 4 + hh, r], qkv[:, hh, r])
                t.tell(x, "b_kk")

            def p_b_nat():
                t.see("b_dve")
                for i in range(2):
                    r = slice(i * 128, i * 128 + 128)
                    for hh in range(4):
                        o = slice(hh * 128, hh * 128 + 128)
                        pe.transpose(P[:, 2 + i, o], qkv[:, 4 + hh, r], ident[:, :])
                        pe.transpose(P[:, 4 + i, o], qkv[:, 8 + hh, r], ident[:, :])
                        x = pe.transpose(P[:, 6 + i, o], b_XT[:, 4 * i + hh, :], ident[:, :])
                t.tell(x, "b_nat")

            def p_b_y(lv):
                t.see("b_dve")
                for u in range(8):
                    x = mm(P[:, 2 + u // 4, (u % 4) * 128:(u % 4) * 128 + 128], b_Nl[:, u, :], b_X[:, u, :])
                t.tell(x, "b_Yp")

            def p_b_xy(lv):
                t.see("b_Y")
                for u in range(8):
                    o = slice((u % 4) * 128, (u % 4) * 128 + 128)
                    mm(P[:, 4 + u // 4, o], b_XT[:, u, :], b_Y[:, u, :])
                    x = mm(P[:, 6 + u // 4, o], b_Y[:, u, :], b_XT[:, u, :])
                t.tell(x, "b_XY")

            def p_b_uw():
                t.see("b_dve")
                for u in range(8):
                    o = slice((u % 4) * 128, (u % 4) * 128 + 128)
                    mm(P[:, 2 + u // 4, o], b_XT[:, u, :], b_vb[:, u, :])
                    x = mm(P[:, 4 + u // 4, o], b_kbg[:, u, :], b_XT[:, u, :])
                t.tell(x, "b_uw")

            def p_b_w(c):
                if c == 0:
                    t.see("b_dve")
                    return
                i, b = c // 2, 64 * (c % 2)
                t.see("b_dve")
                for hh in range(4):
                    x = mm(P[b:b + 64, 2, hh * 128:hh * 128 + 128], b_wT[:, 4 * i + hh, b:b + 64], b_S[:, hh, :])
                t.tell(x, "b_wS")

            def p_b_o(c):
                i, b = c // 2, 64 * (c % 2)
                r = slice(b, b + 64)
                t.see("b_dve")
                for hh in range(4):
                    u = 4 * i + hh
                    o = P[:, 6 + hh // 2, (hh % 2) * S + c * 64:(hh % 2) * S + c * 64 + 64]
                    if c:
                        mm(o, b_S[:, hh, :], b_qd[:, u, r], stop=False)
                    x = mm(o, b_vn[r, hh, :], b_at[r, u, r], start=not c)
                if c < 3:
                    for hh in range(4):
                        x = mm(P[:, 3, hh * 128:hh * 128 + 128], b_kd[r, 4 * i + hh, :], b_vn[r, hh, :])
                t.tell(x, "b_o")

            def p_b_end():
                norm_sum(2, "b_sq2", "b_ss2", b_sq[:, :, :].rearrange("p a b -> p (a b)"))

            held = {}

            def p_merge(k):
                n, d = BRANCH_ORDER[k // DT], k % DT
                if d == 0:
                    pe.wait_ge(sem("y%d" % n), 4 if n == 2 else 1)
                if k == 0:
                    pe.wait_ge(sem("proj_out"), t.sent["proj"])
                if d % 4 == 0:
                    held["w"] = take().rearrange("p (m n) -> p m n", n=512)
                if d % 2 == 0:
                    held["g"] = take().rearrange("p (m n) -> p m n", n=256)
                if k >= 2:
                    pe.wait_ge(sem("merged"), k - 1)
                for c in range(DT):
                    mm(P[:, k % 2, 0:S], held["g"][:, c, (d % 2) * 128:(d % 2) * 128 + 128], xT[:, c, :],
                           start=c == 0, stop=c == DT - 1)
                for c in range(4):
                    x = mm(P[:, k % 2, S:2 * S], held["w"][:, c, (d % 4) * 128:(d % 4) * 128 + 128], yT[n][:, c, :],
                           start=c == 0, stop=c == 3)
                t.tell(x, "branch_psum")

            pe_steps = {"a_mult": lambda: None, "a_scan": lambda: None, "angles": lambda: None, "cols": p_cols, "small": p_small, "proj": p_proj, "a_conv": lambda: None, "a_gates": p_a_gates,
                        "b_conv": lambda: None, "b_norm": p_b_norm, "c_z": p_c_z, "c_cum": p_c_cum, "c_out": p_c_out,
                        "d_gate": p_d_gate, "d_attn": p_d_attn, "d_intra": p_d_intra, "d_chunk": p_d_chunk,
                        "d_end": p_d_end, "b_rows": p_b_rows, "b_decay": p_b_decay, "b_kk": p_b_kk, "b_nat": p_b_nat,
                        "b_y": p_b_y, "b_xy": p_b_xy, "b_uw": p_b_uw, "b_w": p_b_w, "b_o": p_b_o, "b_end": p_b_end,
                        "merge": p_merge}

            def first_mixer():
                turn_x(xs)
                for step in STEPS:
                    pe_steps[step[0]](*step[1:])
                pe.wait_ge(sem("merged"), 4 * DT)
                t.see("b_read")
                t.tell(square_out(lambda k, i: merged[:, k, i * 128:i * 128 + 128]), "mixer_out")

            def gate_up(f, w, gate, up, col, read):
                if read is not None:
                    pe.wait_ge(sem("hid"), read)
                for k, src in enumerate((gate, up)):
                    for d in range(DT):
                        x = mm3(P[0:w, f % 2, k * S:k * S + S], [part[:, d, col:col + w] for part in src],
                                (x_hi[:, d, :], x_lo[:, d, :]), start=d == 0, stop=d == DT - 1)
                return x

            def down(f, w, wd, row, ready, start, stop):
                pe.wait_ge(sem("hid"), ready)
                for i in range(2):
                    for c in range(2):
                        x = mm3(P[:, 4 + 2 * i + c, :], [part[0:w, f, i * 128:i * 128 + 128] for part in (hid_hi, hid_lo)],
                                [part[0:w, row, c * 512:c * 512 + 512] for part in wd], start=start, stop=stop)
                return x

            def unit_at(n0, j, r, wide=256):
                lo_wait(pe, n0 + j, r)
                return [w[:, (n0 + j) % R, 0:(DT * wide if wide != D else UNIT)].rearrange("p (m n) -> p m n", n=wide)
                        for w in (w_hi, w_lo)]

            def four_tiles(n0, r, h0, first_tile, fresh, before_first_down=None, also={}, waits=False):
                wide = [None, None]
                for f in range(4):
                    c = f // 2
                    if f % 2 == 0:
                        wide = unit_at(n0, 3 * c, r), unit_at(n0, 3 * c + 1, r)
                    x = gate_up(f, 128, wide[0], wide[1], (f % 2) * 128,
                                None if first_tile and f < 2 and not waits else r * 4 + (h0 + f - 1))
                    x.then_inc(sem("gu"), 1)
                    if f == 0:
                        if not first_tile:
                            last_down(n0 - R, r, h0 - 4, fresh)
                    if f in also:
                        also[f]()
                    if f == 0:
                        continue
                    g = f - 1
                    if g == 0 and before_first_down is not None:
                        before_first_down()
                    wd = unit_at(n0, 3 * (g // 2) + 2, r, D)
                    x = down(g, 128, wd, g % 2, r * 4 + (h0 + g + 1), start=(g == 0 and (fresh or first_tile)), stop=False)
                    if f == 2:
                        x.then_inc(sem("unit_used"), 1)

            def last_down(n0, r, h0, stop):
                wd = unit_at(n0, 5, r, D)
                x = down(3, 128, wd, 1, r * 4 + (h0 + 4), start=False, stop=stop)
                x.then_inc(sem("expert_out" if stop else "unit_used"), 1)

            def ada_sum(j, r):
                pe.wait_ge(sem("ada_half"), r * 6 + (2 * j + 2))
                for q in range(3):
                    x = mm(P[:, 2, bass.ds(r * 9 + (3 * j + q), 1)], acc[:, j, q * 128:q * 128 + 128], ones[:, 0:1])
                x.then_inc(sem("ada_read"), 1)

            def experts():
                turn_x(xs)
                pe.wait_ge(sem("wr_here"), 48)
                for i in range(2):
                    for d in range(DT):
                        x = mm(P[:, 3, 16 * i:16 * i + 16], xT[:, d, i * 128:i * 128 + 128], wr[:, d, :],
                               start=d == 0, stop=d == DT - 1)
                t.tell(x, "route_psum")
                t.see("x_lo")
                n0 = unit[0]
                four_tiles(n0, 0, 0, True, True, also={3: lambda: ada_sum(0, 0)})
                with pe.Fori(0, EXPERTS - 1) as r:
                    def y_read():
                        pe.wait_ge(sem("y_added"), r + 1)
                    four_tiles(n0 + 6, r, 4, False, True, y_read,
                               {0: lambda: ada_sum(1, r), 2: lambda: ada_sum(2, r), 3: lambda: ada_sum(0, r + 1)})
                last_down(n0 + 6 * 15, 0, 4 * 15, True)
                ada_sum(1, EXPERTS - 1)
                ada_sum(2, EXPERTS - 1)
                unit[0] += 6 * EXPERTS
                t.see("adac")
                for l in range(2):
                    x = pe.transpose(P[0:N_COLS, 3, l * 128:l * 128 + 128], adac[:, l * N_COLS:(l + 1) * N_COLS], ident[:, :])
                t.tell(x, "modt")

            tiles_before = [4 * EXPERTS if first <= 1 else 0]

            def ffn():
                n0, h0 = unit[0], tiles_before[0]
                t.see("x_lo")
                four_tiles(n0, 0, h0, True, False, waits=h0 > 0)
                with pe.Fori(0, 4) as r:
                    four_tiles(n0 + 6, r, h0 + 4, False, False)
                m, k0 = n0 + 30, h0 + 20
                wide = unit_at(m, 0, 0), unit_at(m, 1, 0)
                gate_up(0, 128, wide[0], wide[1], 0, k0 - 1).then_inc(sem("gu"), 1)
                last_down(m - R, 0, k0 - 4, False)
                gate_up(1, 128, wide[0], wide[1], 128, k0).then_inc(sem("gu"), 1)
                down(0, 128, unit_at(m, 2, 0, D), 0, k0 + 1, False, False)
                t.tell(down(1, 128, unit_at(m, 2, 0, D), 1, k0 + 2, False, True), "out")
                unit[0] += 3 * FF_GROUPS
                tiles_before[0] += 22

            def turns(pieces):
                for k in range(0, len(pieces), 4):
                    q = t.sent["turn"]
                    if q >= 2:
                        pe.wait_ge(sem("turned"), q - 1)
                    part = pieces[k:k + 4]
                    for m, src in enumerate(part):
                        x = pe.transpose(P[:, 2 + q % 2, m * 128:m * 128 + 128], src, ident[:, :])
                    t.tell(x, "turn")

            def sparse():
                turn_x(h)
                for u in range(7):
                    tm_units(1, 256 if u < 6 else 200)
                t.see("roped")
                for i in range(2):
                    turns([proj[:, i, 128 * k:128 * k + 128] for k in range(8)])
                    turns([proj[:, i, 1152 + 128 * k:1280 + 128 * k] for k in range(4)])
                t.see("dup")
                for i in range(2):
                    turns([dup[:, i, :], dup2[:, i, :]])
                pe.wait_ge(sem("turned"), t.sent["turn"])
                n = 0
                for i in range(2):
                    kw = 128 * (i + 1)
                    for hh in range(8):
                        r = slice(64 * (hh % 2), 64 * (hh % 2) + 64)
                        if n >= 2:
                            pe.wait_ge(sem("idx_relu"), n - 1)
                        x = mm(P[:, n % 2, 0:kw], qiT[r, hh // 2, i * 128:i * 128 + 128], kT[r, 1, 0:kw])
                        t.tell(x, "idx")
                        n += 1
                units = [(i, hg) for i in range(2) for hg in range(4)]

                def scores(n):
                    i, hg = units[n]
                    kw = 128 * (i + 1)
                    if n >= 1:
                        pe.wait_ge(sem("s_read"), n)
                    else:
                        pe.wait_ge(sem("idx_relu"), 16)
                    for k in range(4):
                        hh = 4 * hg + k
                        r = slice(64 * (hh % 2), 64 * (hh % 2) + 64)
                        x = mm(P[:, k % 2, (k // 2) * S:(k // 2) * S + kw], qT[r, hh // 2, i * 128:i * 128 + 128],
                               kT[r, 0, 0:kw])
                    t.tell(x, "s_psum")
                scores(0)
                for n, (i, hg) in enumerate(units):
                    if n + 1 < len(units):
                        scores(n + 1)
                    t.see("p_ready")
                    for j in range(i + 1):
                        q = t.sent["pt"]
                        if q >= 2:
                            pe.wait_ge(sem("pt_out"), q - 1)
                        for k in range(4):
                            x = pe.transpose(P[:, 2 + q % 2, k * 128:k * 128 + 128], pr[:, k, j * 128:j * 128 + 128], ident[:, :])
                        t.tell(x, "pt")
                    pe.wait_ge(sem("pt_out"), t.sent["pt"])
                    if n >= 2:
                        pe.wait_ge(sem("o_out"), n - 1)
                    for s in range(2):
                        for j in range(i + 1):
                            x = mm(P[64 * s:64 * s + 64, 4 + n % 2, 0:S], proj[:, j, 1088:1152], pT[:, j, 2 * s:2 * s + 2, :],
                                   start=j == 0, stop=j == i)
                    t.tell(x, "o_psum")
                pe.wait_ge(sem("o_out"), len(units))
                t.tell(square_out(lambda k, i: oT[:, k, i * 128:i * 128 + 128]), "out")

            dup2 = big[:, 0, :].rearrange("p (a b) -> p a b", b=128)

            def differential():
                turn_x(h)
                tm_units(12)
                t.see("roped")
                for i in range(2):
                    turns([proj[:, i, 128 * k:128 * k + 128] for k in range(16)])
                pe.wait_ge(sem("turned"), t.sent["turn"])
                units = [(i, hg) for i in range(2) for hg in range(4)]
                base_s = t.sent["s_psum"]

                def scores(n):
                    i, hg = units[n]
                    kw = 128 * (i + 1)
                    if n >= 1:
                        pe.wait_ge(sem("s_read"), base_s + n)
                    else:
                        pe.wait_ge(sem("proj_out"), t.sent["proj"])
                    for k in range(4):
                        hh, c = 2 * hg + k // 2, k % 2
                        r = slice(64 * (hh % 2), 64 * (hh % 2) + 64)
                        tile = (8 * c + hh) // 2
                        x = mm(P[:, k // 2, (k % 2) * S:(k % 2) * S + kw], qT[r, tile, i * 128:i * 128 + 128],
                               kT[r, tile, 0:kw])
                    t.tell(x, "s_psum")
                scores(0)
                for n, (i, hg) in enumerate(units):
                    if n + 1 < len(units):
                        scores(n + 1)
                    t.see("p_ready")
                    q = t.sent["pt"]
                    if q >= 2:
                        pe.wait_ge(sem("pt_out"), q - 1)
                    for k in range(2):
                        for j in range(i + 1):
                            x = pe.transpose(P[:, 2 + q % 2, (2 * k + j) * 128:(2 * k + j) * 128 + 128],
                                             pr[:, k, j * 128:j * 128 + 128], ident[:, :])
                    t.tell(x, "pt")
                    pe.wait_ge(sem("pt_out"), t.sent["pt"])
                    for k in range(2):
                        hh = 2 * hg + k
                        for j in range(i + 1):
                            x = mm(P[:, 4 + hh // 2, (hh % 2) * S + i * 128:(hh % 2) * S + i * 128 + 128],
                                   proj[:, j, 2048 + hh * 128:2048 + hh * 128 + 128], pT[:, k // 2, 2 * (k % 2) + j, :],
                                   start=j == 0, stop=j == i)
                    t.tell(x, "o_psum")
                t.see("o_sq")
                for b in range(4):
                    x = mm(P[:, b, :], ones[:, :], sq_o[:, b * 512:b * 512 + 512])
                t.tell(x, "o_ss")
                t.see("o_normed")
                t.tell(square_out(lambda k, i: oT[:, k, i * 128:i * 128 + 128]), "out")

            t.see("consts")
            pe.wait_ge(sem("x_here"), 16)
            if first > 0:
                p_cols()
            if first == 0:
                first_mixer()
            if first <= 1 <= last:
                if first == 0:
                    t.see("x_ready")
                experts()
                t.see("modr_read")
            for n in range(max(first, 2), last + 1):
                t.see("h_ready")
                sub = (n - 2) % 3
                if sub != 1:
                    turn_x(h)
                    ffn()
                elif n == 3:
                    sparse()
                else:
                    differential()

        @block.scalar
        def _(act):
            a = Line(act, sem, "act")

            def f(o, i, fn, name=None, **kw):
                a.done(act.activation(o, i, fn, **kw), name)

            def rsqrt(o, i, scale, eps, name=None):
                f(o, i, ACT.Ln, scale=scale, bias=eps)
                f(o, o, ACT.Exp, name, scale=-0.5)

            def take_xT():
                for i in range(2):
                    a.see("xt_psum1")
                    f(xT[:, 4:8, i * 128:i * 128 + 128], P[:, 5 + 2 * i, :].rearrange("p (a b) -> p a b", b=128), ACT.Copy, "xt_act")

            def high_xT():
                f(x_hi[:, 4:8, :], xT[:, 4:8, :], ACT.Copy, "x_hi")

            def high(n0, js, r=0):
                for j in js:
                    if n0 + j in split_no:
                        slot, half = (n0 + j) % R, UNIT // 2
                        act.wait_ge(sem("unit%d" % slot), r * 16 + 16 * ((n0 + j) // R + 1))
                        for c in (0, half):
                            act.activation(w_hi[:, slot, c:c + half], ring[:, slot, c:c + half],
                                           ACT.Copy).then_inc(sem("w_hi"), 1)

            def out_tile(dst, fn=ACT.Copy, scale=1.0, width=S):
                a.see("proj")
                k = a.sent["proj_out"]
                f(dst, P[:, k % 2, 0:width], fn, "proj_out", scale=scale)
                if k % 2:
                    a.mark("unit_used")

            def a_angles():
                a.see("angles")
                f(rope[:, :, :, :], rope[:, :, :, :], ACT.Sin)

            def a_cols():
                a.see("cols_ready")

            def a_small():
                a.see("small_psum")
                f(small[:, 16:24].rearrange("p (i k) -> p i k", k=4), P[:, 2, 0:16].rearrange("p (i k) -> p i k", k=8)[:, :, 0:4],
                  ACT.Sigmoid, "beta")
                f(lrT[:, :], P[0:16, 3, 0:S], ACT.Copy, "lrT")
                a.see("sp_in")
                f(small[:, 44:56], small[:, 44:56], ACT.Exp)
                f(small[:, 8:12], small[:, 4:8], ACT.Exp, "sp_e")

            def a_proj(which, u):
                if which == "a" and u == 0:
                    a.see("pads", 2)
                for c in (2 * u, 2 * u + 1):
                    if which == "a":
                        out_tile(a_pad[:, c, 3:S + 3])
                    elif which == "b" and c < 12:
                        out_tile(qkv_pad[:, c, 3:S + 3])
                    elif which == "b":
                        out_tile(gate_b[:, c - 12, :], ACT.Silu)
                    else:
                        q, k, v = (sb_q, sb_k, sb_v) if which == "c" else (gl_q, gl_k, gl_v)
                        if c < 4:
                            out_tile(q[:, c, :], scale=64 ** -0.5 if which == "c" else 128 ** -0.5)
                        elif c < 8:
                            out_tile(k[:, c - 4, :])
                        elif c < 12:
                            out_tile(v[:, c % 2, (c - 8) // 2 * S:(c - 8) // 2 * S + S])
                        else:
                            out_tile(gate_d[:, c - 12, :], ACT.Silu)

            def a_a_gates():
                for g, (dst, bias) in enumerate(((a_r, V_BA), (a_i, V_BX))):
                    a.see("a_ri")
                    for c in range(4):
                        f(dst[:, c, :], P[:, 2 + 2 * g + c // 2, (c % 2) * S:(c % 2) * S + S], ACT.Sigmoid,
                          "a_act" if c == 3 else None, bias=cols[:, bias + c:bias + c + 1])

            def a_a_mult():
                a.see("a_dve")
                f(a_t[:, :, :], a_r[:, :, :], ACT.Tanh)
                f(a_r[:, :, :], a_r[:, :, :], ACT.Exp, "a_act")

            def a_a_scan():
                a.see("a_dve")
                f(a_t[:, :, :], a_t[:, :, :], ACT.Sqrt, "a_act")

            def a_b_conv():
                a.see("b_conv")
                f(qkv[:, :, :], qkv[:, :, :], ACT.Silu)
                f(nsq[:, :, :], qkv[:, 0:8, :], ACT.Square, "b_sq")

            def a_b_norm():
                a.see("b_ss")
                rsqrt(nsq[:, :, :], P[:, 4:8, :], 1.0, eps_ln[:, 1:2], "b_rs")

            def a_c_z(hp):
                a.see("c_z")
                if hp == 0:
                    a.see("a_done")
                    a.see("b_normed")
                f(c_zs[:, :, :], P[:, 2:4, 0:384], ACT.Copy, "c_act")
                a.see("c_dve")
                f(c_e[:, :, :], c_e[:, :, :], ACT.Exp)
                f(c_e[:, :, :], c_e[:, :, :], ACT.Ln, "c_act", bias=1.0)

            def a_c_cum(hp):
                a.see("c_dve")
                f(c_w[:, :, :], c_w[:, :, :], ACT.Exp, "c_w")

            def a_c_out(hp):
                a.see("c_o")
                f(yT[2][:, hp, :], P[:, 6 + hp % 2, 0:S], ACT.Copy, "y2")

            def a_d_gate():
                a.see("d_dve")
                f(d_e[:, :], d_e[:, :], ACT.Exp)
                f(d_e[:, :], d_e[:, :], ACT.Ln, "d_act", bias=1.0)
                a.see("d_dve")
                f(d_y[:, :], d_B[:, :], ACT.Exp, scale=-1 / 16)
                f(d_gl[:, :, :], d_B[:, :].rearrange("p (h c k) -> p h c k", h=4, k=16)[:, :, :, 15], ACT.Exp, scale=-1 / 16)
                f(d_e[:, :], d_B[:, :], ACT.Exp, "d_act", scale=1 / 16)
                a.see("d_dve")
                f(d_kd[:, :, :].rearrange("p a b -> p (a b)"), d_kd[:, :, :].rearrange("p a b -> p (a b)"), ACT.Exp,
                  "d_act", scale=-1 / 16)

            def a_d_end():
                a.see("d_I", 15)
                f(d_e[:, :], P[:, 4:6, :].rearrange("p a b -> p (a b)"), ACT.Square, "d_sq")
                a.see("d_ss")
                rsqrt(d_e[:, :], P[:, 6:8, :].rearrange("p a b -> p (a b)"), 1 / 128, eps_ln[:, 1:2], "d_act")

            def a_b_decay():
                a.see("b_st")
                f(small[:, 72:104], small[:, 72:104], ACT.Exp, "b_act")
                f(b_eg[:, :, :], P[:, 2:4, :], ACT.Exp)
                a.see("b_dif")
                f(b_dm[:, :, :], b_dm[:, :, :], ACT.Exp, "b_act")

            def a_b_nat():
                a.see("b_nat")
                f(b_X[:, :, :], P[:, 6:8, :], ACT.Copy, "b_act")

            def a_b_y(lv):
                a.see("b_Yp")
                f(b_Y[:, :, :], P[:, 2:4, :], ACT.Copy, "b_Y")

            def a_b_uw():
                a.see("b_uw")
                f(b_u[:, :, :], P[:, 2:4, :], ACT.Copy)
                f(b_wT[:, :, :], P[:, 4:6, :], ACT.Copy, "b_act")

            def a_b_end():
                a.see("b_o", 4)
                f(b_sq[:, :, :], P[:, 6:8, :], ACT.Square, "b_sq2")
                a.see("b_ss2")
                rsqrt(b_sq[:, :, :], P[:, 2:4, :], 1 / 128, eps_ln[:, 1:2], "b_act")

            def a_merge(k):
                if k >= 2:
                    act.wait_ge(sem("merged"), k - 1)
                a.see("branch_psum")
                f(sg[:, k % 2, :], P[:, k % 2, 0:S], ACT.Sigmoid, "sg")

            nothing = lambda *x: None
            act_steps = {"a_mult": a_a_mult, "a_scan": a_a_scan, "angles": a_angles, "cols": a_cols, "small": a_small, "proj": a_proj, "a_conv": nothing, "a_gates": a_a_gates, "b_conv": a_b_conv,
                         "b_norm": a_b_norm, "c_z": a_c_z, "c_cum": a_c_cum, "c_out": a_c_out, "d_gate": a_d_gate,
                         "d_attn": nothing, "d_intra": nothing, "d_chunk": nothing, "d_end": a_d_end, "b_rows": nothing,
                         "b_decay": a_b_decay, "b_kk": nothing, "b_nat": a_b_nat, "b_y": a_b_y, "b_xy": nothing,
                         "b_uw": a_b_uw, "b_w": nothing, "b_o": nothing, "b_end": a_b_end, "merge": a_merge}

            def layer_norm_rs():
                a.see("var")
                rsqrt(st[:, 4:6], st[:, 4:6], 1.0, eps_ln[:, 0:1], "rs")

            def silus(n0, tiles=4, r=0, h0=0, free=True, after=AFTER):
                for k in range(tiles):
                    if free or k >= 2:
                        act.wait_ge(sem("hid"), r * 4 + (h0 + k - 1))
                    act.wait_ge(sem("gu"), r * 4 + (h0 + k + 1))
                    if k % 2:
                        act.sem_inc(sem("wide_used"), 2)
                    act.activation(silu[:, k % 2, :], P[:, k % 2, 0:S], ACT.Silu).then_inc(sem("silu"), 1)
                    high(n0, after[k], r)

            tiles, unit = [0], [starts[max(first, 1)] - first_unit]

            def a_experts():
                take_xT()
                high_xT()
                a.see("route_psum")
                f(sc[:, :], P[:, 3, 0:32], ACT.Sigmoid, "sc")
                f(cols[:, V_C:V_C + 8], cols[:, V_C:V_C + 8], ACT.Silu, "cond")
                high(unit[0], (0, 1, 2))
                silus(unit[0], free=False)
                with act.Fori(0, EXPERTS - 1) as r:
                    silus(unit[0] + 6, r=r, h0=4)
                tiles[0] += 4 * EXPERTS
                unit[0] += 6 * EXPERTS
                layer_norm_rs()

            def before(n):
                for i in range(2):
                    f(h[:, 0, :], xs[:, i, :], ACT.Square, accum_out=st[:, 8 + i:9 + i])
                rsqrt(st[:, 8:10], st[:, 8:10], 1 / D, eps_ln[:, 1:2], "rs_in")

            def after(n):
                a.see("out")
                a.mark("unit_used")
                for b in range(4):
                    f(h[:, 0, 0:512], P[:, 4 + b, :], ACT.Square, "y_ss" if b == 3 else None, accum_out=st[:, 12 + b:13 + b])
                a.see("y_sum")
                rsqrt(st[:, 16:18], st[:, 16:18], 1 / D, eps_ln[:, 1:2], "y_rs")

            def a_ffn():
                high_xT()
                h0, n0 = tiles[0], unit[0]
                silus(n0, h0=h0, free=h0 > 0)
                with act.Fori(0, 4) as r:
                    silus(n0 + 6, r=r, h0=h0 + 4)
                silus(n0 + 30, 2, h0=h0 + 20, after=LAST_AFTER)
                tiles[0] += 22
                unit[0] += 3 * FF_GROUPS

            def turned(dsts):
                for dst in dsts:
                    a.see("turn")
                    k = a.sent["turned"]
                    n = dst.shape[1]
                    f(dst, P[:, 2 + k % 2, 0:n * 128].rearrange("p (a b) -> p a b", b=128), ACT.Copy, "turned")

            def softmax_exps(n, i):
                kw = 128 * (i + 1)
                a.see("nmax")
                for k in range(4):
                    f(big[:, k, 0:kw], big[:, k, 0:kw], ACT.Exp, "exps" if k == 3 else None,
                      bias=st[:, 24 + k:25 + k], accum_out=st[:, 28 + k:29 + k])

            def a_sparse():
                for u in range(7):
                    w = 256 if u < 6 else 200
                    for i in range(2):
                        out_tile(proj[:, i, u * 256:u * 256 + w], width=w)
                for i in range(2):
                    r = slice(i * 128, i * 128 + 128)
                    turned([qT[:, 0:4, r], qT[:, 4:8, r], qiT[:, 0:4, r]])
                for i in range(2):
                    turned([kT[:, 0:2, i * 128:i * 128 + 128]])
                n = 0
                for i in range(2):
                    kw = 128 * (i + 1)
                    for hh in range(8):
                        a.see("idx")
                        if n >= 2:
                            act.wait_ge(sem("idx_add"), n - 1)
                        f(wk[:, n % 2, 0:kw], P[:, n % 2, 0:kw], ACT.Relu, "idx_relu")
                        n += 1
                for n in range(8):
                    i, hg = n // 4, n % 4
                    softmax_exps(n, i)
                    for j in range(i + 1):
                        a.see("pt")
                        f(pT[:, j, :, :], P[:, 2 + a.sent["pt_out"] % 2, :].rearrange("p (a b) -> p a b", b=128), ACT.Copy, "pt_out")
                    a.see("o_psum")
                    f(oT[:, 2 * hg:2 * hg + 2, i * 128:i * 128 + 128],
                      P[:, 4 + n % 2, 0:S].rearrange("p (a b) -> p a b", b=128), ACT.Copy, "o_out")

            def a_differential():
                for u in range(12):
                    for i in range(2):
                        out_tile(proj[:, i, u * 256:u * 256 + 256])
                for i in range(2):
                    r = slice(i * 128, i * 128 + 128)
                    turned([qT[:, 0:4, r], qT[:, 4:8, r], kT[:, 0:4, r], kT[:, 4:8, r]])
                for n in range(8):
                    i, hg = n // 4, n % 4
                    softmax_exps(n, i)
                    a.see("pt")
                    src = P[:, 2 + a.sent["pt_out"] % 2, :].rearrange("p (k j b) -> p k j b", k=2, j=2)
                    f(pT[:, 0, :, :].rearrange("p (k j) b -> p k j b", j=2)[:, :, 0:i + 1, :], src[:, :, 0:i + 1, :], ACT.Copy, "pt_out")
                a.see("o_psum", 8)
                f(sq_o[:, :], P[:, 4:8, :].rearrange("p a b -> p (a b)"), ACT.Square, "o_sq")
                a.see("o_ss")
                rsqrt(sq_o[:, :], P[:, 0:4, :].rearrange("p a b -> p (a b)"), 1 / 128, eps_ln[:, 1:2], "o_rs")

            a.see("consts")
            if first > 0:
                a_angles()
                a_cols()
            if first == 0:
                take_xT()
                for step in STEPS:
                    act_steps[step[0]](*step[1:])
                layer_norm_rs()
            if first > 0:
                act.wait_ge(sem("x_here"), 16)
            if first <= 1 <= last:
                a_experts()
            for n in range(max(first, 2), last + 1):
                if n > first:
                    a.see("x_ready2")
                before(n)
                if n in unprimed:
                    high(unit[0], (0, 1, 2))
                take_xT()
                sub = (n - 2) % 3
                if sub != 1:
                    a_ffn()
                elif n == 3:
                    a_sparse()
                else:
                    a.see("lam_in")
                    f(st[:, 56:58], st[:, 56:58], ACT.Exp, "lam_exp")
                    a_differential()
                unit[0] += (0 if sub != 1 else 11 if n == 3 else 16)
                after(n)

        @block.vector
        def _(dve):
            v = Line(dve, sem, "dve")

            def tt(o, x, y, op, name=None):
                v.done(dve.tensor_tensor(o, x, y, op), name)

            def ts(o, x, s1, s2=None, op0=ALU.mult, op1=None, name=None):
                v.done(dve.tensor_scalar(o, x, s1, s2, op0, op1) if s2 is not None else
                       dve.tensor_scalar(o, x, s1, None, op0), name)

            def stt(o, x, s, y, op0, op1, name=None):
                v.done(dve.scalar_tensor_tensor(out=o, in0=x, scalar=s, in1=y, op0=op0, op1=op1), name)

            def copy(o, x, name=None):
                v.done(dve.tensor_copy(o, x), name)

            def recip(o, x, name=None):
                v.done(dve.reciprocal(o, x), name)

            def over(ap, n):
                return ap.unsqueeze(1).to_broadcast([128, n, ap.shape[1]])

            def along(ap, n):
                return ap.unsqueeze(2).to_broadcast([128, ap.shape[1], n])

            def take_xT():
                for i in range(2):
                    v.see("xt_psum0")
                    copy(xT[:, 0:4, i * 128:i * 128 + 128], P[:, 4 + 2 * i, :].rearrange("p (a b) -> p a b", b=128), "xt_dve")

            def low_xT():
                copy(x_hi[:, 0:4, :], xT[:, 0:4, :])
                v.see("x_hi")
                tt(x_lo[:, :, :], xT[:, :, :], x_hi[:, :, :].bitcast(F32), ALU.subtract, "x_lo")

            def low(n0, js, r=0):
                for j in js:
                    n = n0 + j
                    if n in split_no and lo_at[n][0] == "w_lo":
                        slot, half = n % R, UNIT // 2
                        for q, c in enumerate((0, half)):
                            if n - 1 in split_no and slot > 0:
                                lo_wait(dve, n - 1, r, back=1 - q)
                            dve.wait_ge(sem("w_hi"), r * 12 + (2 * split_no[n] + q + 1))
                            dve.tensor_tensor(w_lo[:, slot, c:c + half], ring[:, slot, c:c + half],
                                              w_hi[:, slot, c:c + half].bitcast(F32), ALU.subtract).then_inc(sem("w_lo"), 1)

            def rope_angles():
                dve.wait_ge(sem("pos_here"), 16)
                copy(st[:, 58:60], st[:, 60:62].bitcast(I32))
                for k in range(8):
                    v.done(dve.memset(st[:, 32 + k:33 + k], float(np.float32(500000.0 ** (-k / 8)))))
                for i in range(2):
                    for c in range(2):
                        ts(rope[:, i, c, :], st[:, 32:40], st[:, 58 + i:59 + i])
                rv = rope[:, :, :, :].rearrange("p i c k -> p c i k")
                turn = 2 * math.pi
                magic = 1.5 * 2.0 ** 23
                c1 = float(np.float32(6.28125))
                c2 = float(np.float32(int((turn - c1) * 2 ** 21) / 2 ** 21))
                c3 = float(np.float32(turn - c1 - c2))
                for c in range(2):
                    k = big_k[:, c, :].rearrange("p (i k) -> p i k", k=8)
                    ts(k, rv[:, c], 1 / turn, 0.25 * c, ALU.mult, ALU.add)
                    ts(k, k, magic, None, ALU.add)
                    ts(k, k, magic, None, ALU.subtract)
                    for cc in (c1, c2, c3):
                        stt(rv[:, c], k, -cc, rv[:, c], ALU.mult, ALU.add)
                    if c:
                        ts(rv[:, c], rv[:, c], math.pi / 2, None, ALU.add)
                    ts(rv[:, c], rv[:, c], 3.1415925, -3.1415925, ALU.min, ALU.max, "angles" if c else None)

            big_k = st[:, 0:32].rearrange("p (c k) -> p c k", k=16)

            def v_cols():
                v.see("cols_psum")
                copy(cols[:, :], P[:, 7, 0:128], "cols_ready")

            def v_small():
                dve.wait_ge(sem("small_here"), 64)
                z, e, s, s2, q = (small[:, k:k + 12] for k in (32, 44, 72, 84, 96))
                ts(z[:, 0:4], cols[:, V_LAM:V_LAM + 4], -1.0)
                v.see("beta")
                tt(z[:, 4:12].rearrange("p (i k) -> p i k", k=4), P[:, 2, 0:16].rearrange("p (i k) -> p i k", k=8)[:, :, 4:8],
                   over(small[:, 0:4], 2), ALU.add)
                stt(e, z, -1.0, z, ALU.mult, ALU.min, "sp_in")
                v.see("sp_e")
                ts(s, e, 2.0, None, ALU.add)
                recip(s, s)
                tt(s, s, e, ALU.mult)
                tt(s2, s, s, ALU.mult)
                ts(q, s2, 1 / 17)
                for k in (15, 13, 11, 9, 7, 5, 3):
                    stt(q, q, 1 / k, s2, ALU.add, ALU.mult)
                ts(q, q, 1.0, 2.0, ALU.add, ALU.mult)
                tt(q, q, s, ALU.mult)
                stt(q, z, 0.0, q, ALU.max, ALU.add)
                ts(small[:, 12:16], q[:, 0:4], -8.0)
                stt(small[:, 24:32].rearrange("p (i k) -> p i k", k=4), q[:, 4:12].rearrange("p (i k) -> p i k", k=4), -1.0,
                    over(small[:, 8:12], 2), ALU.mult, ALU.mult, "small_free")

            def conv(dst, src, w0, stride, c, bias=None):
                tap = lambda w: cols[:, w0 + w * stride + c:w0 + w * stride + c + 1]
                if bias is None:
                    ts(dst, src[:, c, 0:S], tap(0))
                else:
                    ts(dst, src[:, c, 0:S], tap(0), bias, ALU.mult, ALU.add)
                for w in range(1, 4):
                    stt(dst, src[:, c, w:w + S], tap(w), dst, ALU.mult, ALU.add)

            def v_a_conv():
                dve.wait_ge(sem("proj_out"), 4)
                for c in range(4):
                    conv(a_x[:, c, :], a_pad, V_CONV_A, 4, c, cols[:, V_CONV_AB + c:V_CONV_AB + c + 1])
                v.mark("a_x")

            def v_a_gates():
                v.see("masks")
                v.see("a_act", 2)
                for c in range(4):
                    ts(a_r[:, c, :], a_r[:, c, :], small[:, 12 + c:13 + c], name="a_dve" if c == 3 else None)

            def v_a_mult():
                v.see("a_act")
                ts(nsq[:, 0:4, :], a_t[:, :, :], -1.0, 1.0, ALU.mult, ALU.add)
                recip(nsq[:, 0:4, :], nsq[:, 0:4, :])
                stt(a_t[:, :, :], a_t[:, :, :], -2.0, nsq[:, 0:4, :], ALU.mult, ALU.mult, "a_dve")

            def v_a_scan():
                v.see("a_act")
                v.done(dve.memset(a_t[:, :, 0:1], 1.0))
                tt(a_t[:, :, :], a_t[:, :, :], a_i[:, :, :], ALU.mult)
                tt(a_t[:, :, :], a_t[:, :, :], a_x[:, :, :], ALU.mult)
                for c in range(4):
                    v.done(dve.tensor_tensor_scan(yT[0][:, c, :], a_r[:, c, :], a_t[:, c, :], 0.0, ALU.mult, ALU.add),
                           "y0" if c == 3 else None)
                v.mark("a_done")

            def v_b_conv():
                dve.wait_ge(sem("proj_out"), 16)
                for c in range(12):
                    conv(qkv[:, c, :], qkv_pad, V_CONV_B, 12, c)
                v.mark("b_conv")

            def v_b_norm():
                v.see("b_rs")
                stt(qkv[:, 0:4, :], qkv[:, 0:4, :], 128 ** -0.5, nsq[:, 0:4, :], ALU.mult, ALU.mult)
                tt(qkv[:, 4:8, :], qkv[:, 4:8, :], nsq[:, 4:8, :], ALU.mult, "b_normed")

            def v_c_z(hp):
                v.see("c_act")
                stt(c_e[:, :, :], c_zs[:, :, :], -1.0, c_zs[:, :, :], ALU.mult, ALU.min, "c_dve")
                v.see("c_act")
                stt(c_sp[:, :, :], c_zs[:, :, :], 0.0, c_e[:, :, :], ALU.max, ALU.add)
                tt(c_sp[:, :, :], c_sp[:, :, :], over(mask3[:, :], 2), ALU.mult, "c_sp")

            def v_c_cum(hp):
                v.see("c_cum")
                if hp:
                    dve.wait_ge(sem("c_o"), hp)
                stt(c_w[:, :, :], P[:, 4:6, 0:384], -1.0, c_zs[:, :, :], ALU.mult, ALU.add)
                stt(c_w[:, :, :], c_w[:, :, :], 0.0, over(neg3[:, :], 2), ALU.min, ALU.add, "c_dve")

            def v_d_gate():
                dve.wait_ge(sem("c_o"), 4)
                v.done(dve.memset(d_reset[:, :], 1.0))
                v.done(dve.memset(d_reset[:, 0::16], 0.0))
                v.see("d_psum")
                for c in range(4):
                    ts(d_y[:, c * S:c * S + S], P[:, 2 + c // 2, (c % 2) * S:(c % 2) * S + S],
                       cols[:, V_BGLA + c:V_BGLA + c + 1], -1.0, ALU.add, ALU.mult)
                stt(d_e[:, :], d_y[:, :], -1.0, d_y[:, :], ALU.mult, ALU.min, "d_dve")
                v.see("d_act")
                stt(d_e[:, :], d_y[:, :], 0.0, d_e[:, :], ALU.max, ALU.add)
                v.done(dve.tensor_tensor_scan(d_B[:, :], d_reset[:, :], d_e[:, :], 0.0, ALU.mult, ALU.add), "d_dve")
                B4 = d_B[:, :].rearrange("p (c k) -> p c k", k=16)
                tt(d_kd[:, :, :].rearrange("p h (c k) -> p (h c) k", k=16), B4[:, :, 15:16].to_broadcast([128, 64, 16]), B4, ALU.subtract, "d_dve")
                v.see("d_act")
                q4, k4 = (x[:, :, :].rearrange("p a b -> p (a b)") for x in (gl_q, gl_k))
                v.see("d_act")
                tt(d_kd[:, :, :].rearrange("p a b -> p (a b)"), d_kd[:, :, :].rearrange("p a b -> p (a b)"), k4, ALU.mult)
                tt(q4, q4, d_y[:, :], ALU.mult)
                tt(k4, k4, d_e[:, :], ALU.mult, "d_q")

            def v_d_attn():
                v.see("d_psum")
                tt(d_at[:, :, :], P[:, 4:6, :].rearrange("p i (h s) -> p (i h) s", s=128), over(tri16[:, :], 8), ALU.mult)
                v.see("d_psum")
                for e in range(2):
                    ts(d_kn[:, e, :, :], P[:, 6:8, :].rearrange("p i (h s) -> p (i h) s", s=128), parity[:, e:e + 1],
                       name="d_am" if e else None)

            def v_d_chunk(c):
                if c == 15:
                    return
                v.see("d_psum")
                if c >= 2:
                    dve.wait_ge(sem("d_I"), c - 1)
                if c == 0:
                    copy(d_S[:, 0, :], P[:, 2, :], "d_S")
                    return
                for hh in range(4):
                    r = slice(hh * 128, hh * 128 + 128)
                    stt(d_S[:, c % 2, r], d_S[:, (c - 1) % 2, r], d_gl[:, hh, c:c + 1], P[:, 2 + c % 2, r],
                        ALU.mult, ALU.add, "d_S" if hh == 3 else None)

            def branch_end(rs, bank, scale_col, gate, y, name):
                tt(rs, rs, P[:, bank:bank + 2, :].rearrange("p a b -> p (a b)"), ALU.mult)
                stt(y[:, :, :].rearrange("p a b -> p (a b)"), rs, cols[:, scale_col:scale_col + 1],
                    gate[:, :, :].rearrange("p a b -> p (a b)"), ALU.mult, ALU.mult, name)

            def v_d_end():
                v.see("d_act")
                branch_end(d_e[:, :], 4, V_ND, gate_d, yT[3], "y3")

            def v_b_rows():
                for i in range(2):
                    for hh in range(4):
                        c = 4 * i + hh
                        ts(b_r1[:, c, :], tri64[:, :], small[:, 24 + c:25 + c])
                        ts(b_r2[:, c, :], ident[:, :], small[:, 16 + c:17 + c], name="b_dve" if c == 7 else None)

            def v_b_decay():
                v.see("b_rows")
                copy(small[:, 72:88], P[:, 6, 0:16])
                for s in range(2):
                    copy(small[:, 88:104].rearrange("p (i s k) -> p i s k", s=2, k=4)[:, :, s, :],
                         P[:, 6 + s, 16:24].rearrange("p (i k) -> p i k", k=4))
                for u in range(8):
                    ts(b_dm[:, u, :], P[:, 2 + u // 4, (u % 4) * 128:(u % 4) * 128 + 128], small[:, 72 + u:73 + u], 0.0,
                       ALU.subtract, ALU.min, name="b_dif" if u == 7 else None)
                tt(small[:, 80:88], small[:, 80:88], small[:, 72:80], ALU.subtract, "b_st")
                v.see("b_act")
                tt(small[:, 104:112], small[:, 72:80], small[:, 16:24], ALU.mult)
                v.see("b_act")
                tt(b_dm[:, :, :], b_dm[:, :, :], over(tri64[:, :], 8), ALU.mult)
                tt(b_r1[:, :, :], b_dm[:, :, :], P[:, 4:6, :].rearrange("p i (h s) -> p (i h) s", s=128), ALU.mult, "b_dve")

            def v_b_kk():
                v.see("b_kk")
                tt(b_N[:, :, :], b_r1[:, :, :], P[:, 2:4, :].rearrange("p i (h s) -> p (i h) s", s=128), ALU.mult)
                tt(b_at[:, :, :], b_dm[:, :, :], P[:, 6:8, :].rearrange("p i (h s) -> p (i h) s", s=128), ALU.mult)
                tt(b_XT[:, :, :], b_N[:, :, :], over(masks[:, 0, :], 8), ALU.mult)
                tt(b_XT[:, :, :], over(ident[:, :], 8), b_XT[:, :, :], ALU.subtract, "b_dve")

            def v_b_nat():
                v.see("b_nat")
                kp = P[:, 2:4, :].rearrange("p i (h s) -> p (i h) s", s=128)
                vp = P[:, 4:6, :].rearrange("p i (h s) -> p (i h) s", s=128)
                tt(b_kbg[:, :, :], kp, along(small[:, 104:112], 128), ALU.mult)
                tt(b_kd[:, :, :], kp, along(small[:, 80:88], 128), ALU.mult)
                tt(b_vb[:, :, :], vp, along(small[:, 16:24], 128), ALU.mult)
                v.see("b_act")

            def v_b_y(lv):
                tt(b_Nl[:, :, :], b_N[:, :, :], over(masks[:, lv, :], 8), ALU.mult, "b_dve")

            def v_b_xy(lv):
                v.see("b_XY")
                if lv < 5:
                    tt(b_X[:, :, :], b_X[:, :, :], P[:, 4:6, :].rearrange("p i (h s) -> p (i h) s", s=128), ALU.subtract)
                tt(b_XT[:, :, :], b_XT[:, :, :], P[:, 6:8, :].rearrange("p i (h s) -> p (i h) s", s=128), ALU.subtract,
                   "b_dve" if lv == 5 else None)

            def v_b_uw():
                for i in range(2):
                    tt(b_qd[:, 4 * i:4 * i + 4, :], qkv[:, 0:4, i * 128:i * 128 + 128], b_eg[:, 4 * i:4 * i + 4, :], ALU.mult)
                v.see("b_act")
                v.mark("b_dve")

            def v_b_w(c):
                i, b = c // 2, 64 * (c % 2)
                r = slice(b, b + 64)
                if c == 0:
                    copy(b_vn[r, :, :], b_u[r, 0:4, :], "b_dve")
                    return
                v.see("b_wS")
                tt(b_vn[r, :, :], b_u[r, 4 * i:4 * i + 4, :], P[r, 2, :].rearrange("p (h s) -> p h s", s=128), ALU.subtract, "b_dve")

            def v_b_o(c):
                v.see("b_o")
                if c == 3:
                    return
                if c == 0:
                    copy(b_S[:, :, :], P[:, 3, :].rearrange("p (h s) -> p h s", s=128), "b_dve")
                    return
                tt(b_S[:, :, :], b_S[:, :, :], along(small[:, 88 + 4 * c:92 + 4 * c], 128), ALU.mult)
                tt(b_S[:, :, :], b_S[:, :, :], P[:, 3, :].rearrange("p (h s) -> p h s", s=128), ALU.add, "b_dve")

            def v_b_end():
                v.see("b_act")
                branch_end(b_sq[:, :, :].rearrange("p a b -> p (a b)"), 6, V_NB, gate_b, yT[1], "y1")
                v.mark("b_read")

            def v_merge(k):
                d = k % DT
                v.see("sg")
                if d % 4 == 3:
                    v.mark("unit_used", 3)
                p = P[:, k % 2, S:2 * S]
                if k < DT:
                    tt(merged[:, d, :], sg[:, k % 2, :], p, ALU.mult, "merged")
                else:
                    tt(tmpm[:, :], sg[:, k % 2, :], p, ALU.mult)
                    tt(merged[:, d, :], merged[:, d, :], tmpm[:, :], ALU.add, "merged")

            nothing = lambda *x: None
            dve_steps = {"a_mult": v_a_mult, "a_scan": v_a_scan, "angles": rope_angles, "cols": v_cols, "small": v_small, "proj": nothing, "a_conv": v_a_conv, "a_gates": v_a_gates, "b_conv": v_b_conv,
                         "b_norm": v_b_norm, "c_z": v_c_z, "c_cum": v_c_cum, "c_out": nothing, "d_gate": v_d_gate,
                         "d_attn": v_d_attn, "d_intra": nothing, "d_chunk": v_d_chunk, "d_end": v_d_end,
                         "b_rows": v_b_rows, "b_decay": v_b_decay, "b_kk": v_b_kk, "b_nat": v_b_nat, "b_y": v_b_y,
                         "b_xy": v_b_xy, "b_uw": v_b_uw, "b_w": v_b_w, "b_o": v_b_o, "b_end": v_b_end, "merge": v_merge}

            def layer_norm(g, b, name):
                for i in range(2):
                    for c in range(2):
                        v.done(dve.bn_stats(st[:, 20 + 6 * c:26 + 6 * c], xs[:, i, c * 512:c * 512 + 512]))
                    v.done(dve.bn_aggr(st[:, 2 * i:2 * i + 2], st[:, 20:32].rearrange("p (c k) -> p c k", k=6)))
                for i in range(2):
                    copy(st[:, 4 + i:5 + i], st[:, 2 * i + 1:2 * i + 2], "var" if i else None)
                v.see("rs")
                for i in range(2):
                    ts(xs[:, i, :], xs[:, i, :], st[:, 2 * i:2 * i + 1], st[:, 4 + i:5 + i], ALU.subtract, ALU.mult)
                tt(xs[:, :, :], xs[:, :, :], over(rowbc[:, g, :], 2), ALU.mult)
                tt(xs[:, :, :], xs[:, :, :], over(rowbc[:, b, :], 2), ALU.add, name)

            def route():
                s = lambda k: rt[:, k, :]
                g4 = lambda ap: ap.rearrange("p (i g e) -> p i g e", i=2, e=4)
                v.see("sc")
                tt(s(0).rearrange("p (i e) -> p i e", i=2), sc[:, :].rearrange("p (i e) -> p i e", i=2), over(rt[:, 15, 0:16], 2), ALU.add)
                b4 = g4(s(0)).rearrange("p i g e -> p (i g) e")
                gs, pair = s(1)[:, 0:8], s(2)[:, 0:8]
                first_pair = True
                for x in range(4):
                    for y in range(x + 1, 4):
                        tt((gs if first_pair else pair).unsqueeze(2), b4[:, :, x:x + 1], b4[:, :, y:y + 1], ALU.add)
                        if not first_pair:
                            tt(gs, gs, pair, ALU.max)
                        first_pair = False

                def first_best(vals, n, dst, cum):
                    v3 = vals.rearrange("p (i n) -> p i n", i=2)
                    d3 = dst.rearrange("p (i n) -> p i n", i=2)
                    v.done(dve.tensor_reduce(s(3)[:, 0:2], v3, AX.X, ALU.max))
                    tt(d3, v3, along(s(3)[:, 0:2], n), ALU.is_equal)
                    for i in range(2):
                        v.done(dve.tensor_tensor_scan(cum[:, i * n:i * n + n], ones[:, 0:n], dst[:, i * n:i * n + n], 0.0,
                                                      ALU.mult, ALU.add))
                    stt(dst, cum, 1.0, dst, ALU.is_equal, ALU.mult)

                yield
                first_best(gs, 4, s(4)[:, 0:8], s(5)[:, 0:8])
                ts(s(6)[:, 0:8], s(4)[:, 0:8], -1.0, BIG, ALU.add, ALU.mult)
                tt(s(7).rearrange("p (g e) -> p g e", e=4), b4, along(s(6)[:, 0:8], 4), ALU.add)
                yield
                first_best(s(7), 16, s(8), s(9))
                stt(s(7), s(8), -BIG, s(7), ALU.mult, ALU.add)
                yield
                first_best(s(7), 16, s(10), s(9))
                tt(s(8), s(8), s(10), ALU.add)
                tt(s(8), s(8), sc[:, :], ALU.mult)
                v.done(dve.tensor_reduce(s(3)[:, 0:2], s(8).rearrange("p (i n) -> p i n", i=2), AX.X, ALU.add))
                recip(s(3)[:, 0:2], s(3)[:, 0:2])
                tt(comb[:, :].rearrange("p (i n) -> p i n", i=2), s(8).rearrange("p (i n) -> p i n", i=2), along(s(3)[:, 0:2], 16), ALU.mult)
                ts(xs[:, :, :], xs[:, :, :], DN_ALPHA)

            def hidden(k, r, h0, done=0):
                n = 2 * (h0 + k)
                for lo_or_hi in (hid_hi, hid_lo) if done else ():
                    ts(lo_or_hi[0:done, k, :], ones256[0:done, :], 0.0)
                x, hi = hid[done:128, k % 2, :], hid_hi[done:128, k, :]
                dve.wait_ge(sem("silu"), r * 4 + (h0 + k + 1))
                dve.tensor_tensor(x, silu[done:128, k % 2, :], P[done:128, k % 2, S:2 * S], ALU.mult).then_inc(sem("hid_part"), 1)
                dve.wait_ge(sem("hid_part"), r * 8 + (n + 1))
                dve.tensor_copy(hi, x).then_inc(sem("hid_part"), 1)
                dve.wait_ge(sem("hid_part"), r * 8 + (n + 2))
                dve.tensor_tensor(hid_lo[done:128, k, :], x, hi.bitcast(F32), ALU.subtract).then_inc(sem("hid"), 1)

            def ada_halves(halves, r, prior=True):
                for i in halves:
                    j = i // 2
                    dve.wait_ge(sem("ada%d" % (i % 3)), r * 32 + 16 * (i // 3 + 1))
                    if i % 2 == 0 and prior:
                        dve.wait_ge(sem("ada_read"), r * 3 + (j - 2))
                    for d in range(4):
                        w, c = ada[:, i % 3, d, :], cols[:, V_C + 4 * (i % 2) + d:V_C + 4 * (i % 2) + d + 1]
                        if i % 2 == 0 and d == 0:
                            x = dve.tensor_scalar(acc[:, j, :], w, c, None, ALU.mult)
                        else:
                            if d == 0:
                                dve.wait_ge(sem("ada_half"), r * 6 + i)
                            else:
                                dve.wait_ge(sem("ada_step"), r * 18 + (3 * i + d))
                            x = dve.scalar_tensor_tensor(out=acc[:, j, :], in0=w, scalar=c, in1=acc[:, j, :],
                                                         op0=ALU.mult, op1=ALU.add)
                        x.then_inc(sem("ada_step" if d < 3 else "ada_half"), 1)

            def add_expert(e, r):
                dve.wait_ge(sem("expert_out"), r)
                dve.sem_inc(sem("unit_used"), 1)
                dve.wait_ge(sem("y_added"), r - 1)
                for b in range(4):
                    i, c = b // 2, b % 2
                    x = dve.scalar_tensor_tensor(out=xs[:, i, c * 512:c * 512 + 512], in0=P[:, 4 + b, :],
                                                 scalar=comb[:, bass.ds(e + 16 * i, 1)], in1=xs[:, i, c * 512:c * 512 + 512],
                                                 op0=ALU.mult, op1=ALU.add)
                x.then_inc(sem("y_added"), 1)

            tiles, unit = [0], [starts[max(first, 1)] - first_unit]

            def v_experts():
                take_xT()
                low_xT()
                n0 = unit[0]
                low(n0, (0, 1, 2))
                routing = route()
                v.see("cond")
                for k in range(4):
                    hidden(k, 0, 0)
                    low(n0, AFTER[k])
                    next(routing, None)
                    ada_halves(HALVES[k], 0, False)
                with dve.Fori(0, EXPERTS - 1) as r:
                    hidden(0, r, 4)
                    add_expert(r, r + 1)
                    low(n0 + 6, AFTER[0], r)
                    ada_halves(HALVES[0], r + 1)
                    for k in range(1, 4):
                        hidden(k, r, 4)
                        low(n0 + 6, AFTER[k], r)
                        ada_halves(HALVES[k], r + 1)
                unit[0] += 6 * EXPERTS
                add_expert(EXPERTS - 1, EXPERTS)
                dve.wait_ge(sem("y_added"), EXPERTS)
                tiles[0] += 4 * EXPERTS
                dve.wait_ge(sem("ada_read"), 3 * EXPERTS)
                copy(adac[:, :], P[:, 2, 0:2 * N_COLS], "adac")
                v.see("modt")
                for l in range(2):
                    tt(modr[:, l, :], P[0:N_COLS, 3, l * 128:l * 128 + 128], adab[:, l, :], ALU.add, "modr" if l else None)
                v.mark("modr_read")
                layer_norm(2, 3, "x_final" if last == 1 else "x_ready2")
                v.mark("pre_free")

            def before(n):
                k = n - max(first, 2)
                dve.wait_ge(sem("pre_here"), 48 * (k + 1))
                stt(rowbc[:, 1, :], rowbc[:, 1, :], 1.0, rowbc[:, 0, :], ALU.add, ALU.mult)
                v.see("rs_in")
                for i in range(2):
                    stt(h[:, i, :], xs[:, i, :], st[:, 8 + i:9 + i], rowbc[:, 1, :], ALU.mult, ALU.mult)
                tt(h[:, :, :], h[:, :, :], over(rowbc[:, 2, :], 2), ALU.add, "h_ready")
                v.mark("pre_free")
                if n in unprimed:
                    low(unit[0], (0,))
                take_xT()
                if (n - 2) % 3 != 1:
                    low_xT()
                if n in unprimed:
                    low(unit[0], (1, 2))
                dve.wait_ge(sem("post_here"), 32 * (k + 1))
                stt(rowbc[:, 4, :], rowbc[:, 4, :], 1.0 if (n - 2) % 3 == 1 else 0.5, rowbc[:, 3, :], ALU.mult, ALU.mult)

            def after(n):
                v.see("y_ss")
                v.done(dve.tensor_reduce(st[:, 16:18], st[:, 12:16].rearrange("p (i c) -> p i c", c=2), AX.X, ALU.add), "y_sum")
                v.see("y_rs")
                for b in range(4):
                    i, c = b // 2, slice((b % 2) * 512, (b % 2) * 512 + 512)
                    stt(h[:, i, c], P[:, 4 + b, :], st[:, 16 + i:17 + i], rowbc[:, 4, c], ALU.mult, ALU.mult)
                tt(xs[:, :, :], xs[:, :, :], h[:, :, :], ALU.add, "x_final" if n == last else "x_ready2")
                if n < last:
                    v.mark("post_free")

            def v_ffn():
                h0, n0 = tiles[0], unit[0]
                for k in range(4):
                    hidden(k, 0, h0)
                    low(n0, AFTER[k])
                with dve.Fori(0, 4) as r:
                    for k in range(4):
                        hidden(k, r, h0 + 4)
                        low(n0 + 6, AFTER[k], r)
                for k in range(2):
                    hidden(k, 0, h0 + 20, 0 if k else FF_DONE)
                    low(n0 + 30, LAST_AFTER[k])
                tiles[0] += 22
                unit[0] += 3 * FF_GROUPS

            def apply_rope(i, c0, heads):
                x = proj[:, i, c0:c0 + 64 * heads].rearrange("p (h d) -> p h d", d=64)
                x1, x2 = x[:, :, 0:8], x[:, :, 8:16]
                w = [big[:, k, 0:8 * heads].rearrange("p (h d) -> p h d", d=8) for k in range(4)]
                sin, cos = over(rope[:, i, 0, :], heads), over(rope[:, i, 1, :], heads)
                tt(w[0], x1, cos, ALU.mult)
                tt(w[1], x2, sin, ALU.mult)
                tt(w[2], x2, cos, ALU.mult)
                tt(w[3], x1, sin, ALU.mult)
                tt(x1, w[0], w[1], ALU.subtract)
                tt(x2, w[2], w[3], ALU.add)

            def probs_rows(i, mask):
                kw = 128 * (i + 1)
                v.see("s_psum")
                s4 = halves(0)[:, :, 0:kw]
                stt(big[:, :, 0:kw], s4, 64 ** -0.5, over(mask, 4), ALU.mult, ALU.add, "s_read")
                v.done(dve.tensor_reduce(st[:, 24:28], big[:, :, 0:kw], AX.X, ALU.max))
                ts(st[:, 24:28], st[:, 24:28], -1.0, name="nmax")
                v.see("exps")
                recip(st[:, 28:32], st[:, 28:32])

            def v_sparse():
                dve.wait_ge(sem("proj_out"), proj_before[0] + 14)
                proj_before[0] += 14
                for i in range(2):
                    apply_rope(i, 0, 17)
                    apply_rope(i, 1152, 9)
                v.mark("roped")
                for i in range(2):
                    for e in range(2):
                        copy(dup[:, i, 64 * e:64 * e + 64], proj[:, i, 1024:1088])
                        copy(big[:, 0, 128 * i + 64 * e:128 * i + 64 * e + 64], proj[:, i, 1664:1728],
                             "dup" if i + e == 2 else None)
                n = 0
                for i in range(2):
                    kw = 128 * (i + 1)
                    w8 = st[:, 40:48]
                    ts(w8, proj[:, i, 1728:1736], float(np.float32(8 ** -0.5 * 64 ** -0.5)))
                    for hh in range(8):
                        v.see("idx_relu")
                        if hh == 0:
                            ts(score[:, 0:kw], wk[:, n % 2, 0:kw], w8[:, 0:1], name="idx_add")
                        else:
                            stt(score[:, 0:kw], wk[:, n % 2, 0:kw], w8[:, hh:hh + 1], score[:, 0:kw], ALU.mult, ALU.add, "idx_add")
                        n += 1
                    d0 = 128 * i
                    tt(score[:, d0:d0 + 128], score[:, d0:d0 + 128], causal_neg[:, :], ALU.add)
                    best = st[:, 48:56]
                    src = score[:, 0:kw]
                    for k in range(TOPK // 8):
                        v.done(dve.max(best, src))
                        if k < TOPK // 8 - 1:
                            v.done(dve.match_replace(rl[:, 0:kw], best, src, -3e38))
                            src = rl[:, 0:kw]
                    thr = best[:, 7:8]
                    m = keep[:, i, 0:kw]
                    more, same, cum = big[:, 1, 0:kw], big[:, 2, 0:kw], big[:, 3, 0:kw]
                    ts(more, score[:, 0:kw], thr, None, ALU.is_gt)
                    ts(same, score[:, 0:kw], thr, None, ALU.is_equal)
                    v.done(dve.tensor_reduce(st[:, 32:33], more, AX.X, ALU.add))
                    ts(st[:, 32:33], st[:, 32:33], -1.0, float(TOPK), ALU.mult, ALU.add)
                    v.done(dve.tensor_tensor_scan(cum, ones256[:, 0:kw], same, 0.0, ALU.mult, ALU.add))
                    stt(m, cum, st[:, 32:33], same, ALU.is_le, ALU.mult)
                    tt(m, m, more, ALU.add)
                    ts(m, m, -1.0, BIG, ALU.add, ALU.mult)
                    tt(keep[:, i, d0:d0 + 128], keep[:, i, d0:d0 + 128], causal_neg[:, :], ALU.add)
                for n in range(8):
                    i, hg = n // 4, n % 4
                    kw = 128 * (i + 1)
                    probs_rows(i, keep[:, i, 0:kw])
                    if n >= 1:
                        dve.wait_ge(sem("pt"), pt_count(n))
                    tt(pr[:, :, 0:kw], big[:, :, 0:kw], along(st[:, 28:32], kw), ALU.mult, "p_ready")

            def pt_count(n):
                return n if n <= 4 else 4 + 2 * (n - 4)

            proj_before = [48 if first == 0 else 0]

            def v_differential():
                n_pt = 12 if first <= 3 else 0
                dve.wait_ge(sem("lam_here"), 16)
                lam = lamb[:, :].rearrange("p (a b c) -> p a b c", a=2, b=2)
                tt(oT[:, 1, 0:128].rearrange("p (a c) -> p a c", a=2), lam[:, :, 0, :], lam[:, :, 1, :], ALU.mult)
                v.done(dve.tensor_reduce(st[:, 56:58], oT[:, 1, 0:128].rearrange("p (a c) -> p a c", a=2), AX.X, ALU.add), "lam_in")
                v.see("lam_exp")
                tt(st[:, 58:59], st[:, 56:57], st[:, 57:58], ALU.subtract)
                ts(st[:, 58:59], st[:, 58:59], LAM_INIT, None, ALU.add)
                dve.wait_ge(sem("proj_out"), proj_before[0] + 24)
                for i in range(2):
                    apply_rope(i, 0, 32)
                v.mark("roped")
                v.done(dve.memset(keep[:, 1, 0:128], 0.0))
                copy(keep[:, 1, 128:256], causal_neg[:, :])
                for n in range(8):
                    i, hg = n // 4, n % 4
                    kw = 128 * (i + 1)
                    probs_rows(i, keep[:, 1, 128:256] if i == 0 else keep[:, 1, :])
                    ts(st[:, 29:32:2], st[:, 29:32:2], st[:, 58:59])
                    if n >= 1:
                        dve.wait_ge(sem("pt"), n_pt + n)
                    for k in range(2):
                        ts(big[:, 2 * k + 1, 0:kw], big[:, 2 * k + 1, 0:kw], st[:, 29 + 2 * k:30 + 2 * k])
                        stt(pr[:, k, 0:kw], big[:, 2 * k, 0:kw], st[:, 28 + 2 * k:29 + 2 * k], big[:, 2 * k + 1, 0:kw],
                            ALU.mult, ALU.subtract, "p_ready" if k else None)
                ts(st[:, 59:60], cols[:, V_SUB:V_SUB + 1], 1.0 - LAM_INIT)
                v.see("o_rs")
                stt(oT[:, :, :].rearrange("p a b -> p (a b)"), sq_o[:, :], st[:, 59:60], P[:, 4:8, :].rearrange("p a b -> p (a b)"),
                    ALU.mult, ALU.mult, "o_normed")

            v.see("consts")
            if first > 0:
                rope_angles()
                v_cols()
            if first == 0:
                take_xT()
                for step in STEPS:
                    dve_steps[step[0]](*step[1:])
                v.see("mixer_out")
                v.mark("unit_used")
                for b in range(4):
                    i, c = b // 2, slice((b % 2) * 512, (b % 2) * 512 + 512)
                    stt(xs[:, i, c], xs[:, i, c], DN_ALPHA, P[:, 4 + b, :], ALU.mult, ALU.add)
                dve.wait_ge(sem("ln_here"), 64)
                layer_norm(0, 1, "x_final" if last == 0 else "x_ready")
                v.mark("mixed")
            if first > 0:
                dve.wait_ge(sem("x_here"), 16)
            if first <= 1 <= last:
                v_experts()
            for n in range(max(first, 2), last + 1):
                before(n)
                sub = (n - 2) % 3
                if sub != 1:
                    v_ffn()
                elif n == 3:
                    v_sparse()
                else:
                    v_differential()
                unit[0] += (0 if sub != 1 else 11 if n == 3 else 16)
                after(n)


def kernel(**inputs):
    import concourse.bacc as bacc
    from concourse.bass_utils import run_bass_kernel_spmd

    nc = bacc.Bacc("TRN2", target_bir_lowering=False, num_devices=1)
    arrays, aps = {}, {}
    for name, a in inputs.items():
        a = np.ascontiguousarray(a)
        arrays["in_" + name] = a
        aps[name] = nc.dram_tensor("in_" + name, a.shape, mybir.dt.from_np(a.dtype), kind="ExternalInput").ap()
    out = nc.dram_tensor("out", (1, S, D), F32, kind="ExternalOutput").ap()
    build(nc, aps, out)
    return run_bass_kernel_spmd(nc, [arrays], core_ids=[0]).results[0]["out"]
```

```python
import math
from collections import Counter
from contextlib import ExitStack

import numpy as np

import concourse.bass as bass
from concourse import mybir

F32 = mybir.dt.float32
I32 = mybir.dt.int32
F32R = mybir.dt.float32r
ALU = mybir.AluOpType
ACT = mybir.ActivationFunctionType
AX = mybir.AxisListType

S = 256
D = 1024
DT = D // 128
LRU, BRANCH, HEADS = 512, 512, 4
EXPERTS, D_EXPERT = 16, 512
D_FF = 2752
A_IN, DIFF_IN = 1736, 3072
TOPK = 64
DN_ALPHA = 2 ** 0.25
LN_EPS, EPS = 1e-5, 1e-6
BIG = 1e30
LAM_INIT = 0.8 - 0.6 * math.exp(-0.3 * 1)

R = 6
UNIT = 2048
N_MOD = 9 * D
CH = 2 * N_MOD // EXPERTS // 3
N_COLS = N_MOD // 128
FF_GROUPS = (D_FF + 255) // 256
FF_DONE = 256 * FF_GROUPS - D_FF

C_A, C_GDN, C_BETA, C_GATE_B, C_SB, C_GLA, C_LR, C_GATE_D, C_MERGE = (
    0, 512, 2048, 2056, 2568, 4104, 5640, 5656, 6168)
V_CONV_A, V_CONV_AB, V_BA, V_BX, V_LAM, V_BGLA, V_NB, V_ND, V_SUB, V_CONV_B, V_C = (
    0, 16, 20, 24, 28, 32, 36, 37, 38, 40, 88)

BRANCH_ORDER = [0, 2, 3, 1]

PROJ_UNITS = {"a": 2, "b": 8, "c": 6, "d": 8}
STEPS = [("proj", w, u) for w in "abcd" for u in range(PROJ_UNITS[w])]


def _put(after, steps):
    k = STEPS.index(after) + 1
    STEPS[k:k] = steps


_put(("proj", "a", 1), [("cols",), ("small",), ("a_conv",)])
_put(("proj", "b", 3), [("angles",)])
_put(("proj", "b", 7), [("a_gates",)])
_put(("proj", "c", 0), [("a_mult",)])
_put(("proj", "c", 1), [("a_scan",)])
_put(("proj", "c", 5), [("b_conv",)])
_put(("proj", "d", 3), [("b_norm",)])


def _weave(steps, tiles):
    out, put = [], 0
    for n, s in enumerate(steps):
        out.append(s)
        while put < len(tiles) and put * len(steps) < (n + 1) * len(tiles):
            out.append(tiles[put])
            put += 1
    return out + tiles[put:]


_MERGE = [("merge", k) for k in range(4 * DT)]
for hp in range(4):
    STEPS += [("c_z", hp), _MERGE[2 * hp], ("c_cum", hp), _MERGE[2 * hp + 1], ("c_out", hp)]
STEPS += [("d_gate",), _MERGE[8], _MERGE[9], ("d_attn",), _MERGE[10], ("d_intra",)]
STEPS += _weave([("d_chunk", c) for c in range(16)], _MERGE[11:14])
STEPS += [("d_end",), _MERGE[14], _MERGE[15], ("b_rows",), ("b_decay",), _MERGE[16], _MERGE[17], ("b_kk",), _MERGE[18],
          ("b_nat",), _MERGE[19]]
STEPS += _weave([(s, lv) for lv in range(1, 6) for s in ("b_y", "b_xy")]
                + [("b_uw",)] + [(s, c) for c in range(4) for s in ("b_w", "b_o")] + [("b_end",)],
                _MERGE[20:22])
STEPS += _MERGE[22:32]


def weight_loads(A):
    out = []

    def cols(w, c0, n):
        for c in range(c0, c0 + n, 256):
            m = min(256, n)
            c = min(c, c0 + n - m)
            out.append((w[:, c:c + m].rearrange("(t p) n -> p t n", p=128), w.shape[0] // 128, m, 128))

    def rows(w, r0, n):
        m = max(n // 128, 1)
        p = min(n, 128)
        out.append((w[r0:r0 + n, :].rearrange("(t p) n -> p t n", p=p), m, w.shape[1], p))

    def square(w):
        for r in range(0, D, 256):
            rows(w, r, 256)

    w_in, w_branch = A["w_in"][0], A["w_branch"][0]
    for c, n in ((C_A, 512), (C_GDN, 1536), (C_GATE_B, 512), (C_SB, 1536), (C_GLA, 1536), (C_GATE_D, 512)):
        cols(w_in, c, n)
    for b in BRANCH_ORDER:
        for half in range(2):
            out.append((w_branch[b][:, half * 512:half * 512 + 512].rearrange("(t p) n -> p t n", p=128),
                        4, 512, 128))
            cols(w_in, C_MERGE + b * D + half * 512, 512)
    square(A["w_out"][0])
    marks = {"moe": len(out)}
    for e in range(EXPERTS):
        for c in range(0, D_EXPERT, 256):
            cols(A["w_gate"][0][e], c, 256)
            cols(A["w_up"][0][e], c, 256)
            rows(A["w_down"][0][e], c, 256)
    for layer in range(2):
        for half in range(2):
            if half:
                mix = "dsa" if layer == 0 else "diff"
                marks["attention", layer] = len(out)
                cols(A[mix + "_w_in_2"][0], 0, A_IN if layer == 0 else DIFF_IN)
                square(A[mix + "_w_out_2"][0])
            marks[layer, half] = len(out)
            g, u, d = (A["ffn_w_%s_2" % k][layer][half] for k in ("gate", "up", "down"))
            for c in range(0, D_FF, 256):
                c = min(c, D_FF - 256)
                cols(g, c, 256)
                cols(u, c, 256)
                rows(d, c, 256)
    return out, marks


class Line:

    def __init__(self, eng, sem, own):
        self.eng, self.sem, self.own = eng, sem, own
        self.sent, self.seen = Counter(), Counter()

    def done(self, ins, name=None):
        name = name or self.own
        self.sent[name] += 1
        ins.then_inc(self.sem(name), 1)
        self.eng.wait_ge(self.sem(name), self.sent[name])

    def tell(self, ins, name, n=1):
        self.sent[name] += n
        ins.then_inc(self.sem(name), n)

    def see(self, name, k=1):
        self.seen[name] += k
        self.eng.wait_ge(self.sem(name), self.seen[name])

    def mark(self, name, n=1):
        self.sent[name] += n
        self.eng.sem_inc(self.sem(name), n)


def build(nc, A, out):
    ctx = ExitStack()
    sems = {}

    def sem(name):
        if name not in sems:
            sems[name] = ctx.enter_context(nc.semaphore("s_" + name))
        return sems[name]

    def buf(name, *shape, dt=F32, ctx=ctx):
        return ctx.enter_context(nc.sbuf_tensor(name, list(shape), dt))

    loads, marks = weight_loads(A)
    moe = marks["moe"]
    split_no = {}
    split_runs = [(moe, 6 * EXPERTS)] + [(marks[l, h], 3 * FF_GROUPS) for l in range(2) for h in range(2)]
    attention_runs = [(marks["attention", 0], -(-A_IN // 256)), (marks["attention", 1], DIFF_IN // 256)]
    for n in range(len(loads)):
        if any(a <= n < a + k for a, k in split_runs + attention_runs):
            split_no[n] = len(split_no)

    lo_at, count = {}, Counter()
    for n in split_no:
        name = "w_lo_pool" if n < moe + 6 * EXPERTS + 3 and (n - moe) % 3 == 2 else "w_lo"
        count[name] += 1 if name == "w_lo_pool" else 2
        lo_at[n] = name, count[name]

    def lo_wait(eng, n, r=0, back=0):
        name, c = lo_at[n]
        eng.wait_ge(sem(name), r * (2 if name == "w_lo_pool" else 8 if n < moe + 6 * EXPERTS else 12) + (c - (back if name == "w_lo" else 0)))

    def is_wide(n):
        return any(a <= n < a + k and (n - a) % 3 < 2 for a, k in split_runs)

    mod = nc.dram_tensor("modulation", (2, N_MOD), F32, kind="Internal").ap()

    with ctx:
        m0 = ExitStack()
        w_lo = buf("w_lo", 128, R, UNIT, dt=F32R, ctx=m0)
        m0.close()
        merged = buf("merged", 128, DT, S)
        ring = buf("ring", 128, R, UNIT)
        xs = buf("xs", 128, 2, D)
        xT = buf("xT", 128, DT, S)
        rowbc = buf("rowbc", 128, 4, D)
        ident = buf("ident", 128, 128)
        ones256 = buf("ones256", 128, S)
        ones = ones256[:, 0:128]
        lamb = buf("lamb", 128, S)
        cols = buf("cols", 128, 128)
        causal_neg = buf("causal_neg", 128, 128)
        causal_01 = buf("causal_01", 128, 128)
        rope = buf("rope", 128, 2, 2, 8)
        eps_ln = buf("eps_ln", 128, 2)
        st = buf("st", 128, 64)
        P = ctx.enter_context(nc.psum_tensor("P", [128, 8, 512], F32))

        m0 = ExitStack()
        masks = buf("masks", 128, 6, 128, ctx=m0)
        tri64 = buf("tri64", 128, 128, ctx=m0)
        blk64 = buf("blk64", 128, 128, ctx=m0)
        tri16 = buf("tri16", 128, 128, ctx=m0)
        suffix = buf("suffix", 128, 128, ctx=m0)
        mask3 = buf("mask3", 128, 384, ctx=m0)
        neg3 = buf("neg3", 128, 384, ctx=m0)
        parity = buf("parity", 128, 2, ctx=m0)
        small = buf("small", 128, 128, ctx=m0)
        wsm = buf("wsm", 128, DT, 24, ctx=m0)
        lrT = buf("lrT", 16, S, ctx=m0)
        wup = buf("wup", 16, 512, ctx=m0)
        yT = [buf(f"yT{b}", 128, 4, S, ctx=m0) for b in range(4)]
        sg = buf("sg", 128, 2, S, ctx=m0)
        tmpm = buf("tmpm", 128, S, ctx=m0)
        qkv = buf("qkv", 128, 12, S, ctx=m0)
        gate_b = buf("gate_b", 128, 4, S, ctx=m0)
        gate_d = buf("gate_d", 128, 4, S, ctx=m0)
        m1 = ExitStack()
        sb_q = buf("sb_q", 128, 4, S, ctx=m1)
        sb_k = buf("sb_k", 128, 4, S, ctx=m1)
        sb_v = buf("sb_v", 128, 2, 512, ctx=m1)
        gl_q = buf("gl_q", 128, 4, S, ctx=m1)
        gl_k = buf("gl_k", 128, 4, S, ctx=m1)
        gl_v = buf("gl_v", 128, 2, 512, ctx=m1)
        m2 = ExitStack()
        rowst = buf("rowst", 128, 128, ctx=m2)
        a_pad = buf("a_pad", 128, 4, S + 3, ctx=m2)
        qkv_pad = buf("qkv_pad", 128, 12, S + 3, ctx=m2)
        wbd = buf("wbd", 128, 2, 4, 128, ctx=m2)
        a_x = buf("a_x", 128, 4, S, ctx=m2)
        a_r = buf("a_r", 128, 4, S, ctx=m2)
        a_i, a_t, nsq = yT[1], yT[3], merged
        m2.close()
        m2 = ExitStack()
        c_zs = buf("c_zs", 128, 2, 384, ctx=m2)
        c_e = buf("c_e", 128, 2, 384, ctx=m2)
        c_sp = buf("c_sp", 128, 2, 384, ctx=m2)
        c_w = buf("c_w", 128, 2, 384, ctx=m2)
        m2.close()
        m2 = ExitStack()
        d_B = buf("d_B", 128, 4 * S, ctx=m2)
        d_y = buf("d_y", 128, 4 * S, ctx=m2)
        d_e = buf("d_e", 128, 4 * S, ctx=m2)
        d_reset = buf("d_reset", 128, 4 * S, ctx=m2)
        d_gl = buf("d_gl", 128, 4, 16, ctx=m2)
        d_kd = buf("d_kd", 128, 4, S, ctx=m2)
        d_at = buf("d_at", 128, 8, 128, ctx=m2)
        d_kn = buf("d_kn", 128, 2, 8, 128, ctx=m2)
        d_S = d_B[:, :].rearrange("p (a b) -> p a b", b=512)
        m2.close()
        m1.close()
        m1 = ExitStack()
        b_r1 = buf("b_r1", 128, 8, 128, ctx=m1)
        b_r2 = buf("b_r2", 128, 8, 128, ctx=m1)
        b_dm = buf("b_dm", 128, 8, 128, ctx=m1)
        b_eg = buf("b_eg", 128, 8, 128, ctx=m1)
        b_N = buf("b_N", 128, 8, 128, ctx=m1)
        b_at = buf("b_at", 128, 8, 128, ctx=m1)
        b_X = buf("b_X", 128, 8, 128, ctx=m1)
        b_XT = buf("b_XT", 128, 8, 128, ctx=m1)
        b_kbg = buf("b_kbg", 128, 8, 128, ctx=m1)
        b_kd = buf("b_kd", 128, 8, 128, ctx=m1)
        b_vb = buf("b_vb", 128, 8, 128, ctx=m1)
        b_vn = buf("b_vn", 128, 4, 128, ctx=m1)
        b_S = buf("b_S", 128, 4, 128, ctx=m1)
        b_Nl, b_Y, b_u, b_wT, b_qd, b_sq = b_r1, b_r2, b_r1, b_dm, b_eg, b_X
        m1.close()
        m0.close()

        m0 = ExitStack()
        hid = buf("hid", 128, 2, S, ctx=m0)
        hid_hi = buf("hid_hi", 128, 4, S, dt=F32R, ctx=m0)
        hid_lo = buf("hid_lo", 128, 4, S, dt=F32R, ctx=m0)
        x_hi = buf("x_hi", 128, DT, S, dt=F32R, ctx=m0)
        x_lo = buf("x_lo", 128, DT, S, dt=F32R, ctx=m0)
        silu = buf("silu", 128, 2, S, ctx=m0)
        adac = buf("adac", 128, 2 * N_COLS, ctx=m0)
        adab = buf("adab", N_COLS, 2, 128, ctx=m0)
        modr = buf("modr", N_COLS, 2, 128, ctx=m0)
        normr = buf("normr", 6 * DT, 128, ctx=m0)
        modc = buf("modc", 128, 6, 3, DT, ctx=m0)
        x_scale = buf("x_scale", 128, 6, DT, ctx=m0)
        m1 = ExitStack()
        w_hi = buf("w_hi", 128, R, UNIT, dt=F32R, ctx=m1)
        ada = buf("ada", 128, 3, DT // 2, CH, ctx=m1)
        acc = buf("acc", 128, 3, CH, ctx=m1)
        wr = buf("wr", 128, DT, 16, ctx=m1)
        rt = buf("rt", 128, 16, 32, ctx=m1)
        sc = buf("sc", 128, 32, ctx=m1)
        comb = buf("comb", 128, 32, ctx=m1)
        m1.close()
        m1 = ExitStack()
        m2 = ExitStack()
        qT = buf("qT", 128, 8, S, ctx=m2)
        kT = buf("kT", 128, 8, S, ctx=m2)
        oT = buf("oT", 128, 8, S, ctx=m2)
        dup = buf("dup", 128, 2, 128, ctx=m2)
        keep = buf("keep", 128, 2, S, ctx=m2)
        big = buf("big", 128, 4, S, ctx=m2)
        pr = buf("pr", 128, 4, S, ctx=m2)
        pT = buf("pT", 128, 2, 4, 128, ctx=m2)
        m2.close()
        m2 = ExitStack()
        buf("w_hi_again", 128, R, UNIT, ctx=m2)
        proj = buf("proj", 128, 2, DIFF_IN, ctx=m2)
        h = buf("h", 128, 2, D, ctx=m2)
        m2.close()
        m0.close()
        xT_rows = xT[:, :, :].rearrange("p (i t) s -> p i (t s)", i=2)
        qiT = proj[:, 0, 2048:3072].rearrange("p (a b) -> p a b", b=S)
        score = h[:, 0, 0:256]
        rl = h[:, 0, 256:512]
        wk = h[:, 0, 512:1024].rearrange("p (a b) -> p a b", b=S)
        sq_o = h[:, :, :].rearrange("p a b -> p (a b)")

        block = ctx.enter_context(nc.Block())

        AFTER = ((3, 4), (5,), (6, 7), (8,))
        HALVES = ((0,), (1, 2), (3,), (4, 5))
        LAST_AFTER = ((3,), ())
        SUBLAYERS = (("ffn", ()), ("sparse", (1, 2)), ("ffn", (0, 1, 2)), ("ffn", (1, 2)), ("differential", (1, 2)),
                     ("ffn", (0, 1, 2)))
        SPARSE_WIDTHS = [256] * (A_IN // 256) + [A_IN % 256]
        ATTENTION_UNITS = {"sparse": -(-A_IN // 256) + D // 256, "differential": DIFF_IN // 256 + D // 256, "ffn": 0}

        def halves(bank0):
            return P[:, bank0:bank0 + 2, :].rearrange("p b (h s) -> p (b h) s", s=S)

        @block.sync
        def _(sp):
            sp.dma_start(xs[:, :, :], A["x"][0].rearrange("(i p) d -> p i d", p=128)).then_inc(sem("x_here"), 16)
            passed, after_unit = Counter(), []
            for n in range(len(loads)):
                used = "wide_used" if is_wide(n) else "unit_used"
                passed[used] += 1
                after_unit.append((used, passed[used]))
            for n, (src, m, k, p) in enumerate(loads):
                if n >= R:
                    for used, count in sorted({after_unit[n - R], after_unit[n - R + (n - R + 1 in split_no and n % R < R - 1)]}):
                        sp.wait_ge(sem(used), count)
                sp.dma_start(ring[0:p, n % R, 0:m * k].rearrange("p (m k) -> p m k", k=k), src)\
                  .then_inc(sem("unit%d" % (n % R)), 16)
            for i in range(2):
                sp.wait_ge(sem("x_final"), i + 1)
                sp.dma_start(out[0][i * 128:i * 128 + 128, :], xs[:, i, :]).then_inc(sem("stored"), 16)
            sp.wait_ge(sem("stored"), 32)

        @block.gpsimd
        def _(pool):
            g = Line(pool, sem, "pool")

            def select(ap, pattern, base, mult, op=ALU.is_ge, fill=0.0):
                g.done(pool.affine_select(out=ap, in_=ap, compare_op=op, fill=fill, base=base, pattern=pattern,
                                          channel_multiplier=mult))

            def load(dst, src, name, **kw):
                pool.dma_start(dst, src, **kw).then_inc(sem(name), 16)

            g.done(pool.memset(ident[:, :], 0.0))
            g.done(pool.memset(ones256[:, :], 1.0))
            select(ident[:, :], [[-1, 128]], 0, 1, ALU.not_equal, 1.0)
            g.done(pool.memset(eps_ln[:, 0:1], LN_EPS))
            g.done(pool.memset(eps_ln[:, 1:2], EPS))
            g.done(pool.memset(causal_01[:, :], 1.0))
            select(causal_01[:, :], [[-1, 128]], 0, 1)
            g.done(pool.tensor_scalar(causal_neg[:, :], causal_01[:, :], -1.0, BIG, ALU.add, ALU.mult))
            g.mark("consts")
            g.tell(pool.memset(a_pad[:, :, 0:3], 0.0), "pads")
            g.tell(pool.memset(qkv_pad[:, :, 0:3], 0.0), "pads")
            load(lamb[:, :], A["diff_lambda_2"][0].rearrange("a b -> (a b)").partition_broadcast(128), "lam_here")
            load(st[:, 60:62].bitcast(I32), A["positions_2"][0].rearrange("(i p) -> p i", p=128), "pos_here",
                 allow_slow_non_contiguous=True)
            v = A["conv_a_w"][0], A["gdn_conv_w"][0]
            g.done(pool.memset(rowst[:, :], 0.0))
            tiles = [(V_CONV_A, v[0].rearrange("w (t p) -> w t p", p=128).rearrange("w t p -> (w t) p"), 16),
                     (V_CONV_B, v[1].rearrange("w (t p) -> w t p", p=128).rearrange("w t p -> (w t) p"), 48)]
            for c, name, n in ((V_CONV_AB, "conv_a_b", 4), (V_BA, "rg_b_a", 4), (V_BX, "rg_b_x", 4),
                               (V_LAM, "rg_lambda", 4), (V_BGLA, "gla_b_gate", 4), (V_NB, "gdn_norm_w", 1),
                               (V_ND, "gla_norm_w", 1), (V_SUB, "diff_subln_2", 1), (V_C, "c_2", 8)):
                tiles.append((c, A[name][0].rearrange("(t p) -> t p", p=128), n))
            for c, src, n in tiles:
                load(rowst[c:c + n, :], src, "rows_here")
            load(wsm[:, :, 0:8], A["w_in"][0][:, C_BETA:C_BETA + 8].rearrange("(t p) n -> p t n", p=128), "small_here")
            load(wsm[:, :, 8:24], A["w_in"][0][:, C_LR:C_LR + 16].rearrange("(t p) n -> p t n", p=128), "small_here")
            load(small[:, 0:4], A["gdn_dt_bias"][0].partition_broadcast(128), "small_here")
            load(small[:, 4:8], A["gdn_a_log"][0].partition_broadcast(128), "small_here")
            load(wup[:, :], A["gla_w_gate_up"][0], "wup_here")
            g.done(pool.memset(wbd[:, :, :, :], 0.0))
            for k, name in enumerate(("rg_w_a", "rg_w_x")):
                w = A[name][0].rearrange("(t e) i j -> e i t j", e=2)
                for e in range(2):
                    load(wbd[64 * e:64 * e + 64, k, :, 64 * e:64 * e + 64], w[e], "wbd_here")
            for k, name in enumerate(("ln1_g", "ln1_b", "ln2_g", "ln2_b")):
                load(rowbc[:, k, :], A[name][0].partition_broadcast(128), "ln_here")
            for m, w in ((blk64, 64), (tri64, 64), (tri16, 16)):
                g.done(pool.memset(m[:, :], 1.0))
                v = m[:, :].rearrange("p (a b) -> p a b", b=w)
                select(v, [[-w, 128 // w], [0, w]], 0, 1)
                select(v, [[w, 128 // w], [0, w]], w - 1, -1)
            for m in (tri64, tri16):
                select(m[:, :], [[1, 128]], 0, -1)
            g.done(pool.memset(suffix[:, :], 1.0))
            select(suffix[:, :], [[-1, 128]], 0, 1)
            g.done(pool.memset(mask3[:, :], 1.0))
            for b in (0, 2):
                select(mask3[:, 128 * b:128 * b + 128], [[1, 128]], 0, -1, ALU.is_gt)
            g.done(pool.tensor_scalar(neg3[:, :], mask3[:, :], -1.0, BIG, ALU.add, ALU.mult))
            g.done(pool.memset(masks[:, :, :], 0.0))
            for lv in range(6):
                b = 1 << lv
                v = masks[:, lv, :].rearrange("p (n two b) -> p n two b", two=2, b=b)[:, :, 1, :]
                g.done(pool.memset(v, 1.0))
                select(v, [[-2 * b, 64 // b], [0, b]], 0, 1)
                select(v, [[2 * b, 64 // b], [0, b]], b - 1, -1)
            g.done(pool.memset(small[:, 64:72], 1.0))
            for b in range(4):
                select(small[:, 64 + b:65 + b], [[0, 1]], -32 * b, 1)
                select(small[:, 64 + b:65 + b], [[0, 1]], 32 * b + 15, -1)
            g.done(pool.tensor_tensor(small[:, 64:66], small[:, 64:66], small[:, 66:68], ALU.add))
            g.done(pool.tensor_tensor(parity[:, 0:1], small[:, 64:65], small[:, 65:66], ALU.add))
            g.done(pool.tensor_scalar(parity[:, 1:2], parity[:, 0:1], -1.0, -1.0, ALU.add, ALU.mult))
            g.mark("masks")

            pool.wait_ge(sem("mixed"), 1)
            load(normr[:, :], A["pre_norm_2"].rearrange("l s (t p) -> (l s t) p", p=128), "wr_here")
            load(wr[:, :, :], A["w_router"].rearrange("(t p) n -> p t n", p=128), "wr_here")
            load(rt[:, 15, 0:16], A["router_bias"].partition_broadcast(128), "wr_here")
            load(adab[:, :, :], A["ada_b_2"].rearrange("l (p q) -> p l q", q=128), "wr_here")

            def half_chunk(layer, r, i, used=None):
                if used is not None:
                    pool.wait_ge(sem("ada_half"), used)
                src = A["ada_w_2"][layer].rearrange("(t p) n -> p t n", p=128)
                half = i % 2 * (DT // 2)
                pool.dma_start(ada[:, i % 3, :, :],
                               src[:, half:half + DT // 2, bass.ds(r * (3 * CH) + i // 2 * CH, CH)])\
                    .then_inc(sem("ada%d" % (i % 3)), 16)

            def low(j, r=0):
                n = moe + j
                pool.wait_ge(sem("w_hi"), r * 12 + 2 * (split_no[n] + 1))
                lo_wait(pool, n - 1, r)
                pool.tensor_tensor(w_lo[:, n % R, :], ring[:, n % R, :], w_hi[:, n % R, :].bitcast(F32),
                                   ALU.subtract).then_inc(sem("w_lo_pool"), 1)

            def expert(layer, r, e, next_layer, next_r):
                half_chunk(layer, r, 3, e * 6 + 1)
                low(5, e)
                half_chunk(layer, r, 4, e * 6 + 2)
                half_chunk(layer, r, 5, e * 6 + 3)
                if next_layer is not None:
                    half_chunk(next_layer, next_r, 0, e * 6 + 4)
                low(8, e)
                if next_layer is not None:
                    half_chunk(next_layer, next_r, 1, e * 6 + 5)
                    half_chunk(next_layer, next_r, 2, e * 6 + 6)

            for i in range(3):
                half_chunk(0, 0, i)
            low(2)
            per_layer = EXPERTS // 2
            with pool.Fori(0, per_layer - 1) as r:
                expert(0, r, r, 0, r + 1)
            expert(0, per_layer - 1, per_layer - 1, 1, 0)
            with pool.Fori(0, per_layer - 1) as r:
                expert(1, r, r + per_layer, 1, r + 1)
            expert(1, per_layer - 1, EXPERTS - 1, None, None)
            g.see("modr")
            pool.dma_start(mod.rearrange("l (p q) -> p l q", q=128), modr[:, :, :]).then_inc(sem("mod_stored"), 16)
            pool.wait_ge(sem("mod_stored"), 16)

            def mod_row(layer, k):
                return mod[layer][k * D:k * D + D]

            for n in range(6):
                layer, sub = n // 3, n % 3
                g.see("post_free")
                load(rowbc[:, 0, :], A["post_norm_2"][layer][sub].partition_broadcast(128), "post_here")
                load(rowbc[:, 1, :], mod_row(layer, 3 * sub + 2).partition_broadcast(128), "post_here")

        @block.tensor
        def _(pe):
            t = Line(pe, sem, "pe")
            unit = [0]

            def take(ahead=0):
                n = unit[0]
                unit[0] += 1
                pe.wait_ge(sem("unit%d" % (n % R)), 16 * (n // R + 1))
                return ring[:, n % R, :]

            def mm(o, l, r, start=True, stop=True, **kw):
                return pe.matmul(o, l, r, start=start, stop=stop, **kw)

            def mm3(o, l, r, start, stop):
                mm(o, l[0], r[0], start, False)
                mm(o, l[0], r[1], False, False)
                return mm(o, l[1], r[0], False, stop)

            def turn_x(ready=None, src=xs):
                for i in range(2):
                    if ready:
                        t.see(ready)
                    for b in range(2):
                        for k in range(4):
                            o = P[:, 4 + 2 * b + i, k * 128:k * 128 + 128]
                            x = pe.transpose(o, src[:, i, (4 * b + k) * 128:(4 * b + k + 1) * 128], ident[:, :])
                        t.tell(x, "xt_psum%d" % b)
                t.see("xt_dve")
                t.see("xt_act")

            def square_out(lhs, tiles=8):
                for u in range(4):
                    w = take().rearrange("p (m n) -> p m n", n=D)
                    for k in range(2):
                        for i in range(2):
                            for c in range(2):
                                x = mm(P[:, 4 + 2 * i + c, :], lhs(2 * u + k, i), w[:, k, c * 512:c * 512 + 512],
                                       start=(u + k == 0), stop=(2 * u + k == 7))
                    if u < 3:
                        t.tell(x, "unit_used")
                return x

            def tile_cm(w, c, n=128):
                k = t.sent["proj"]
                if k >= 2:
                    pe.wait_ge(sem("proj_out"), k - 1)
                for d in range(DT):
                    x = mm(P[:, k % 2, 0:S], w[:, d, c:c + 128], xT[:, d, :], start=d == 0, stop=d == DT - 1)
                t.tell(x, "proj")
                return x

            def tiles_tm(w, n=256):
                for i in range(2):
                    k = t.sent["proj"]
                    if k >= 2:
                        pe.wait_ge(sem("proj_out"), k - 1)
                    for d in range(DT):
                        x = mm(P[:, k % 2, 0:n], xT[:, d, i * 128:i * 128 + 128], w[:, d, :],
                               start=d == 0, stop=d == DT - 1)
                    t.tell(x, "proj")
                return x

            def cm_units(n):
                for _ in range(n):
                    w = take().rearrange("p (m n) -> p m n", n=256)
                    for c in range(2):
                        tile_cm(w, c * 128)

            def tm_unit():
                tiles_tm(take().rearrange("p (m n) -> p m n", n=256))

            def p_cols():
                pe.wait_ge(sem("rows_here"), 16 * 11)
                t.tell(pe.transpose(P[:, 7, 0:128], rowst[:, :], ident[:, :]), "cols_psum")
                t.see("cols_ready")

            def p_small():
                pe.wait_ge(sem("small_here"), 64)
                for i in range(2):
                    for d in range(DT):
                        mm(P[:, 2, 8 * i:8 * i + 8], xT[:, d, i * 128:i * 128 + 128], wsm[:, d, 0:8],
                           start=d == 0, stop=d == DT - 1)
                for d in range(DT):
                    x = mm(P[0:16, 3, 0:S], wsm[:, d, 8:24], xT[:, d, :], start=d == 0, stop=d == DT - 1)
                t.tell(x, "small_psum")

            def p_proj(which, u):
                if which in "cd" and u in (4, 5):
                    tm_unit()
                else:
                    cm_units(1)

            def p_a_gates():
                pe.wait_ge(sem("wbd_here"), 64)
                t.see("masks")
                t.see("a_x")
                t.see("small_free")
                for g in range(2):
                    for c in range(4):
                        x = mm(P[:, 2 + 2 * g + c // 2, (c % 2) * S:(c % 2) * S + S], wbd[:, g, c, :], a_x[:, c, :])
                    t.tell(x, "a_ri")

            def p_b_norm():
                t.see("b_sq")
                for c in range(4):
                    x = mm(P[:, 4 + c, :], ones, nsq[:, 2 * c:2 * c + 2, :].rearrange("p a b -> p (a b)"))
                t.tell(x, "b_ss")

            def p_c_z(hp):
                if hp == 0:
                    t.see("a_done")
                    t.see("b_rs")
                    pe.wait_ge(sem("proj_out"), t.sent["proj"])
                for s in range(2):
                    r = slice(64 * s, 64 * s + 64)
                    mm(P[:, 2 + s, 0:S], sb_k[r, hp, 0:128], sb_q[r, hp, :])
                    x = mm(P[:, 2 + s, S:384], sb_k[r, hp, 128:S], sb_q[r, hp, 128:S])
                t.tell(x, "c_z")

            def p_c_cum(hp):
                t.see("c_sp")
                for s in range(2):
                    mm(P[:, 4 + s, 0:384], suffix[:, :], c_sp[:, s, :])
                    x = mm(P[:, 4 + s, 128:S], ones[:, :], c_sp[:, s, S:384], start=False, skip_group_check=True)
                t.tell(x, "c_cum")

            def p_c_out(hp):
                t.see("c_w")
                if hp >= 2:
                    pe.wait_ge(sem("y2"), hp - 1)
                for s in range(2):
                    r = slice(64 * s, 64 * s + 64)
                    c = (2 * hp + s) * 64
                    mm(P[r, 6 + hp % 2, 0:S], sb_v[:, 0, c:c + 64], c_w[:, s, 0:S])
                    x = mm(P[r, 6 + hp % 2, 128:S], sb_v[:, 1, c:c + 64], c_w[:, s, S:384], start=False,
                           skip_group_check=True)
                t.tell(x, "c_o")

            def p_d_gate():
                pe.wait_ge(sem("wup_here"), 16)
                for c in range(4):
                    x = mm(P[:, 2 + c // 2, (c % 2) * S:(c % 2) * S + S], wup[:, c * 128:c * 128 + 128], lrT[:, :])
                t.tell(x, "d_psum")

            def p_d_attn():
                t.see("d_q")
                pe.wait_ge(sem("y2"), 4)
                for i in range(2):
                    for hh in range(4):
                        r = slice(i * 128, i * 128 + 128)
                        x = mm(P[:, 4 + i, hh * 128:hh * 128 + 128], gl_k[:, hh, r], gl_q[:, hh, r])
                t.tell(x, "d_psum")
                for i in range(2):
                    for hh in range(4):
                        x = pe.transpose(P[:, 6 + i, hh * 128:hh * 128 + 128], d_kd[:, hh, i * 128:i * 128 + 128], ident[:, :])
                t.tell(x, "d_psum")

            def p_d_intra():
                t.see("d_am")
                for hh in range(4):
                    for i in range(2):
                        o = (hh % 2) * S + i * 128
                        mm(P[:, 4 + hh // 2, o:o + 128], gl_v[:, i, hh * 128:hh * 128 + 128], d_at[:, 4 * i + hh, :],
                           start=(hh % 2 == 0 and i == 0), skip_group_check=True)

            def p_d_chunk(c):
                if c < 15:
                    if c >= 2:
                        pe.wait_ge(sem("d_S"), c - 1)
                    i, b = c // 8, (c % 8) // 2
                    r = slice(32 * b, 32 * b + 32)
                    for hh in range(4):
                        x = mm(P[:, 2 + c % 2, hh * 128:hh * 128 + 128], d_kn[r, c % 2, 4 * i + hh, :],
                               gl_v[r, i, hh * 128:hh * 128 + 128])
                    t.tell(x, "d_psum")
                if c >= 1:
                    pe.wait_ge(sem("d_S"), c)
                    for hh in range(4):
                        o = (hh % 2) * S + c * 16
                        x = mm(P[:, 4 + hh // 2, o:o + 16], d_S[:, (c - 1) % 2, hh * 128:hh * 128 + 128],
                               gl_q[:, hh, c * 16:c * 16 + 16], start=False, skip_group_check=True)
                    t.tell(x, "d_I")

            def norm_sum(bank, name_in, name_out, sq):
                t.see(name_in)
                for b in range(2):
                    x = mm(P[:, bank + b, :], ones[:, :], sq[:, b * 512:b * 512 + 512])
                t.tell(x, name_out)

            def p_d_end():
                norm_sum(6, "d_sq", "d_ss", d_e)

            def p_b_rows():
                t.see("b_dve")
                pe.wait_ge(sem("y3"), 1)
                for i in range(2):
                    mm(P[:, 2 + i, :], ones[:, :], b_r1[:, 4 * i:4 * i + 4, :].rearrange("p a b -> p (a b)"))
                    mm(P[:, 4 + i, :], ones[:, :], b_r2[:, 4 * i:4 * i + 4, :].rearrange("p a b -> p (a b)"))
                for i in range(2):
                    gi = small[:, 24 + 4 * i:28 + 4 * i]
                    mm(P[:, 6, 4 * i:4 * i + 4], tri64[:, :], gi)
                    mm(P[:, 6, 8 + 4 * i:12 + 4 * i], blk64[:, :], gi)
                    for s in range(2):
                        r = slice(64 * s, 64 * s + 64)
                        x = mm(P[:, 6 + s, 16 + 4 * i:20 + 4 * i], ones[r, :], small[r, 24 + 4 * i:28 + 4 * i])
                t.tell(x, "b_rows")

            def p_b_kk():
                t.see("b_dve")
                for i in range(2):
                    r = slice(i * 128, i * 128 + 128)
                    for hh in range(4):
                        mm(P[:, 2 + i, hh * 128:hh * 128 + 128], qkv[:, 4 + hh, r], qkv[:, 4 + hh, r])
                        x = mm(P[:, 6 + i, hh * 128:hh * 128 + 128], qkv[:, 4 + hh, r], qkv[:, hh, r])
                t.tell(x, "b_kk")

            def p_b_nat():
                t.see("b_dve")
                for i in range(2):
                    r = slice(i * 128, i * 128 + 128)
                    for hh in range(4):
                        o = slice(hh * 128, hh * 128 + 128)
                        pe.transpose(P[:, 2 + i, o], qkv[:, 4 + hh, r], ident[:, :])
                        pe.transpose(P[:, 4 + i, o], qkv[:, 8 + hh, r], ident[:, :])
                        x = pe.transpose(P[:, 6 + i, o], b_XT[:, 4 * i + hh, :], ident[:, :])
                t.tell(x, "b_nat")

            def p_b_y(lv):
                t.see("b_dve")
                for u in range(8):
                    x = mm(P[:, 2 + u // 4, (u % 4) * 128:(u % 4) * 128 + 128], b_Nl[:, u, :], b_X[:, u, :])
                t.tell(x, "b_Yp")

            def p_b_xy(lv):
                t.see("b_Y")
                for u in range(8):
                    o = slice((u % 4) * 128, (u % 4) * 128 + 128)
                    mm(P[:, 4 + u // 4, o], b_XT[:, u, :], b_Y[:, u, :])
                    x = mm(P[:, 6 + u // 4, o], b_Y[:, u, :], b_XT[:, u, :])
                t.tell(x, "b_XY")

            def p_b_uw():
                t.see("b_dve")
                for u in range(8):
                    o = slice((u % 4) * 128, (u % 4) * 128 + 128)
                    mm(P[:, 2 + u // 4, o], b_XT[:, u, :], b_vb[:, u, :])
                    x = mm(P[:, 4 + u // 4, o], b_kbg[:, u, :], b_XT[:, u, :])
                t.tell(x, "b_uw")

            def p_b_w(c):
                if c == 0:
                    t.see("b_dve")
                    return
                i, b = c // 2, 64 * (c % 2)
                t.see("b_dve")
                for hh in range(4):
                    x = mm(P[b:b + 64, 2, hh * 128:hh * 128 + 128], b_wT[:, 4 * i + hh, b:b + 64], b_S[:, hh, :])
                t.tell(x, "b_wS")

            def p_b_o(c):
                i, b = c // 2, 64 * (c % 2)
                r = slice(b, b + 64)
                t.see("b_dve")
                for hh in range(4):
                    u = 4 * i + hh
                    o = P[:, 6 + hh // 2, (hh % 2) * S + c * 64:(hh % 2) * S + c * 64 + 64]
                    if c:
                        mm(o, b_S[:, hh, :], b_qd[:, u, r], stop=False)
                    x = mm(o, b_vn[r, hh, :], b_at[r, u, r], start=not c)
                if c < 3:
                    for hh in range(4):
                        x = mm(P[:, 3, hh * 128:hh * 128 + 128], b_kd[r, 4 * i + hh, :], b_vn[r, hh, :])
                t.tell(x, "b_o")

            def p_b_end():
                norm_sum(2, "b_sq2", "b_ss2", b_sq[:, :, :].rearrange("p a b -> p (a b)"))

            held = {}

            def p_merge(k):
                n, d = BRANCH_ORDER[k // DT], k % DT
                if d == 0:
                    pe.wait_ge(sem("y%d" % n), 4 if n == 2 else 1)
                if k == 0:
                    pe.wait_ge(sem("proj_out"), t.sent["proj"])
                if d % 4 == 0:
                    held["w"] = take().rearrange("p (m n) -> p m n", n=512)
                if d % 2 == 0:
                    held["g"] = take().rearrange("p (m n) -> p m n", n=256)
                if k >= 2:
                    pe.wait_ge(sem("merged"), k - 1)
                for c in range(DT):
                    mm(P[:, k % 2, 0:S], held["g"][:, c, (d % 2) * 128:(d % 2) * 128 + 128], xT[:, c, :],
                           start=c == 0, stop=c == DT - 1)
                for c in range(4):
                    x = mm(P[:, k % 2, S:2 * S], held["w"][:, c, (d % 4) * 128:(d % 4) * 128 + 128], yT[n][:, c, :],
                           start=c == 0, stop=c == 3)
                t.tell(x, "branch_psum")

            pe_steps = {"cols": p_cols, "small": p_small, "proj": p_proj, "a_gates": p_a_gates, "b_norm": p_b_norm,
                        "c_z": p_c_z, "c_cum": p_c_cum, "c_out": p_c_out, "d_gate": p_d_gate, "d_attn": p_d_attn,
                        "d_intra": p_d_intra, "d_chunk": p_d_chunk, "d_end": p_d_end, "b_rows": p_b_rows,
                        "b_kk": p_b_kk, "b_nat": p_b_nat, "b_y": p_b_y, "b_xy": p_b_xy, "b_uw": p_b_uw, "b_w": p_b_w,
                        "b_o": p_b_o, "b_end": p_b_end, "merge": p_merge}

            def first_mixer():
                turn_x()
                for step, *which in STEPS:
                    if step in pe_steps:
                        pe_steps[step](*which)
                pe.wait_ge(sem("merged"), 4 * DT)
                t.see("b_read")
                t.tell(square_out(lambda k, i: merged[:, k, i * 128:i * 128 + 128]), "mixer_out")

            def x_arrives(d):
                if d % 4 == 0:
                    t.see("x_lo")

            def gate_up(f, w, gate, up, col, read, new_x=False):
                if read is not None:
                    pe.wait_ge(sem("hid"), read)
                for k, src in enumerate((gate, up)):
                    for d in range(DT):
                        if new_x and k == 0:
                            x_arrives(d)
                        x = mm3(P[0:w, f % 2, k * S:k * S + S], [part[:, d, col:col + w] for part in src],
                                (x_hi[:, d, :], x_lo[:, d, :]), start=d == 0, stop=d == DT - 1)
                return x

            def down(f, w, wd, row, ready, start, stop):
                pe.wait_ge(sem("hid"), ready)
                for i in range(2):
                    for c in range(2):
                        x = mm3(P[:, 4 + 2 * i + c, :], [part[0:w, f, i * 128:i * 128 + 128] for part in (hid_hi, hid_lo)],
                                [part[0:w, row, c * 512:c * 512 + 512] for part in wd], start=start, stop=stop)
                return x

            def unit_at(n0, j, r, wide=256):
                lo_wait(pe, n0 + j, r)
                return [w[:, (n0 + j) % R, 0:(DT * wide if wide != D else UNIT)].rearrange("p (m n) -> p m n", n=wide)
                        for w in (w_hi, w_lo)]

            def four_tiles(n0, r, h0, first_tile, fresh, before_first_down=None, also={}, waits=False):
                wide = [None, None]
                for f in range(4):
                    c = f // 2
                    if f % 2 == 0:
                        wide = unit_at(n0, 3 * c, r), unit_at(n0, 3 * c + 1, r)
                    x = gate_up(f, 128, wide[0], wide[1], (f % 2) * 128,
                                None if first_tile and f < 2 and not waits else r * 4 + (h0 + f - 1),
                                new_x=first_tile and f == 0)
                    x.then_inc(sem("gu"), 1)
                    if f == 0:
                        if not first_tile:
                            last_down(n0 - R, r, h0 - 4, fresh)
                    if f in also:
                        also[f]()
                    if f == 0:
                        continue
                    g = f - 1
                    if g == 0 and before_first_down is not None:
                        before_first_down()
                    wd = unit_at(n0, 3 * (g // 2) + 2, r, D)
                    x = down(g, 128, wd, g % 2, r * 4 + (h0 + g + 1), start=(g == 0 and (fresh or first_tile)), stop=False)
                    if f == 2:
                        x.then_inc(sem("unit_used"), 1)

            def last_down(n0, r, h0, stop):
                wd = unit_at(n0, 5, r, D)
                x = down(3, 128, wd, 1, r * 4 + (h0 + 4), start=False, stop=stop)
                x.then_inc(sem("expert_out" if stop else "unit_used"), 1)

            def ada_sum(j, r):
                pe.wait_ge(sem("ada_half"), r * 6 + (2 * j + 2))
                for q in range(3):
                    x = mm(P[:, 2, bass.ds(r * 9 + (3 * j + q), 1)], acc[:, j, q * 128:q * 128 + 128], ones[:, 0:1])
                x.then_inc(sem("ada_read"), 1)

            def experts():
                turn_x("x_ready")
                pe.wait_ge(sem("wr_here"), 64)
                for i in range(2):
                    for d in range(DT):
                        x = mm(P[:, 3, 16 * i:16 * i + 16], xT[:, d, i * 128:i * 128 + 128], wr[:, d, :],
                               start=d == 0, stop=d == DT - 1)
                t.tell(x, "route_psum")
                n0 = unit[0]
                four_tiles(n0, 0, 0, True, True, also={3: lambda: ada_sum(0, 0)})
                with pe.Fori(0, EXPERTS - 1) as r:
                    def y_read():
                        pe.wait_ge(sem("y_added"), r + 1)
                    four_tiles(n0 + 6, r, 4, False, True, y_read,
                               {0: lambda: ada_sum(1, r), 2: lambda: ada_sum(2, r), 3: lambda: ada_sum(0, r + 1)})
                last_down(n0 + 6 * 15, 0, 4 * 15, True)
                ada_sum(1, EXPERTS - 1)
                ada_sum(2, EXPERTS - 1)
                unit[0] += 6 * EXPERTS
                t.see("adac")
                for l in range(2):
                    x = pe.transpose(P[0:N_COLS, 3, l * 128:l * 128 + 128], adac[:, l * N_COLS:(l + 1) * N_COLS], ident[:, :])
                t.tell(x, "modt")
                t.see("modr_ready")
                for l in range(2):
                    pe.transpose(P[:, 3, l * N_COLS:(l + 1) * N_COLS], modr[:, l, :], ident[0:N_COLS, 0:N_COLS])
                t.tell(pe.transpose(P[:, 3, 2 * N_COLS:2 * N_COLS + 6 * DT], normr[:, :], ident[0:6 * DT, 0:6 * DT]), "modt")

            tiles_before = [4 * EXPERTS]

            def ffn():
                n0, h0 = unit[0], tiles_before[0]
                four_tiles(n0, 0, h0, True, False, waits=h0 > 0)
                with pe.Fori(0, 4) as r:
                    four_tiles(n0 + 6, r, h0 + 4, False, False)
                m, k0 = n0 + 30, h0 + 20
                wide = unit_at(m, 0, 0), unit_at(m, 1, 0)
                gate_up(0, 128, wide[0], wide[1], 0, k0 - 1).then_inc(sem("gu"), 1)
                last_down(m - R, 0, k0 - 4, False)
                gate_up(1, 128, wide[0], wide[1], 128, k0).then_inc(sem("gu"), 1)
                down(0, 128, unit_at(m, 2, 0, D), 0, k0 + 1, False, False)
                t.tell(down(1, 128, unit_at(m, 2, 0, D), 1, k0 + 2, False, True), "out")
                unit[0] += 3 * FF_GROUPS
                tiles_before[0] += 22

            def turns(pieces):
                for k in range(0, len(pieces), 4):
                    q = t.sent["turn"]
                    if q >= 2:
                        pe.wait_ge(sem("turned"), q - 1)
                    part = pieces[k:k + 4]
                    for m, src in enumerate(part):
                        x = pe.transpose(P[:, 2 + q % 2, m * 128:m * 128 + 128], src, ident[:, :])
                    t.tell(x, "turn")

            def project(widths):
                for u, width in enumerate(widths):
                    w = unit_at(unit[0], 0, 0)
                    unit[0] += 1
                    for i in range(2):
                        k = t.sent["proj"]
                        pe.wait_ge(sem("proj_out"), k - 1)
                        for d in range(DT):
                            if u == 0 and i == 0:
                                x_arrives(d)
                            x = mm3(P[:, k % 2, 0:width], [x[:, d, i * 128:i * 128 + 128] for x in (x_hi, x_lo)],
                                    [p[:, d, 256 - width:256] for p in w], start=d == 0, stop=d == DT - 1)
                        t.tell(x, "proj")

            def sparse():
                project(SPARSE_WIDTHS)
                t.see("roped")
                for i in range(2):
                    turns([proj[:, i, 128 * k:128 * k + 128] for k in range(8)])
                    turns([proj[:, i, 1152 + 128 * k:1280 + 128 * k] for k in range(4)])
                t.see("dup")
                for i in range(2):
                    turns([dup[:, i, :], dup2[:, i, :]])
                pe.wait_ge(sem("turned"), t.sent["turn"])
                n = 0
                for i in range(2):
                    kw = 128 * (i + 1)
                    for hh in range(8):
                        r = slice(64 * (hh % 2), 64 * (hh % 2) + 64)
                        if n >= 2:
                            pe.wait_ge(sem("idx_relu"), n - 1)
                        x = mm(P[:, n % 2, 0:kw], qiT[r, hh // 2, i * 128:i * 128 + 128], kT[r, 1, 0:kw])
                        t.tell(x, "idx")
                        n += 1
                units = [(i, hg) for i in range(2) for hg in range(4)]

                def scores(n):
                    i, hg = units[n]
                    kw = 128 * (i + 1)
                    if n >= 1:
                        pe.wait_ge(sem("s_read"), n)
                    else:
                        pe.wait_ge(sem("idx_relu"), 16)
                    for k in range(4):
                        hh = 4 * hg + k
                        r = slice(64 * (hh % 2), 64 * (hh % 2) + 64)
                        x = mm(P[:, k % 2, (k // 2) * S:(k // 2) * S + kw], qT[r, hh // 2, i * 128:i * 128 + 128],
                               kT[r, 0, 0:kw])
                    t.tell(x, "s_psum")
                scores(0)
                for n, (i, hg) in enumerate(units):
                    if n + 1 < len(units):
                        scores(n + 1)
                    t.see("p_ready")
                    for j in range(i + 1):
                        q = t.sent["pt"]
                        if q >= 2:
                            pe.wait_ge(sem("pt_out"), q - 1)
                        for k in range(4):
                            x = pe.transpose(P[:, 2 + q % 2, k * 128:k * 128 + 128], pr[:, k, j * 128:j * 128 + 128], ident[:, :])
                        t.tell(x, "pt")
                    pe.wait_ge(sem("pt_out"), t.sent["pt"])
                    if n >= 2:
                        pe.wait_ge(sem("o_out"), n - 1)
                    for s in range(2):
                        for j in range(i + 1):
                            x = mm(P[64 * s:64 * s + 64, 4 + n % 2, 0:S], proj[:, j, 1088:1152], pT[:, j, 2 * s:2 * s + 2, :],
                                   start=j == 0, stop=j == i)
                    t.tell(x, "o_psum")
                pe.wait_ge(sem("o_out"), len(units))
                t.tell(square_out(lambda k, i: oT[:, k, i * 128:i * 128 + 128]), "out")

            dup2 = big[:, 0, :].rearrange("p (a b) -> p a b", b=128)

            def differential():
                project([256] * (DIFF_IN // 256))
                t.see("roped")
                for i in range(2):
                    turns([proj[:, i, 128 * k:128 * k + 128] for k in range(16)])
                pe.wait_ge(sem("turned"), t.sent["turn"])
                units = [(i, hg) for i in range(2) for hg in range(4)]
                base_s = t.sent["s_psum"]

                def scores(n):
                    i, hg = units[n]
                    kw = 128 * (i + 1)
                    if n >= 1:
                        pe.wait_ge(sem("s_read"), base_s + n)
                    else:
                        pe.wait_ge(sem("proj_out"), t.sent["proj"])
                    for k in range(4):
                        hh, c = 2 * hg + k // 2, k % 2
                        r = slice(64 * (hh % 2), 64 * (hh % 2) + 64)
                        tile = (8 * c + hh) // 2
                        x = mm(P[:, k // 2, (k % 2) * S:(k % 2) * S + kw], qT[r, tile, i * 128:i * 128 + 128],
                               kT[r, tile, 0:kw])
                    t.tell(x, "s_psum")
                scores(0)
                for n, (i, hg) in enumerate(units):
                    if n + 1 < len(units):
                        scores(n + 1)
                    t.see("p_ready")
                    q = t.sent["pt"]
                    if q >= 2:
                        pe.wait_ge(sem("pt_out"), q - 1)
                    for k in range(2):
                        for j in range(i + 1):
                            x = pe.transpose(P[:, 2 + q % 2, (2 * k + j) * 128:(2 * k + j) * 128 + 128],
                                             pr[:, k, j * 128:j * 128 + 128], ident[:, :])
                    t.tell(x, "pt")
                    pe.wait_ge(sem("pt_out"), t.sent["pt"])
                    for k in range(2):
                        hh = 2 * hg + k
                        for j in range(i + 1):
                            x = mm(P[:, 4 + hh // 2, (hh % 2) * S + i * 128:(hh % 2) * S + i * 128 + 128],
                                   proj[:, j, 2048 + hh * 128:2048 + hh * 128 + 128], pT[:, k // 2, 2 * (k % 2) + j, :],
                                   start=j == 0, stop=j == i)
                    t.tell(x, "o_psum")
                t.see("o_sq")
                for b in range(4):
                    x = mm(P[:, b, :], ones[:, :], sq_o[:, b * 512:b * 512 + 512])
                t.tell(x, "o_ss")
                t.see("o_normed")
                t.tell(square_out(lambda k, i: oT[:, k, i * 128:i * 128 + 128]), "out")

            t.see("consts")
            pe.wait_ge(sem("x_here"), 16)
            first_mixer()
            experts()
            for kind, _ in SUBLAYERS:
                turn_x("h_ready", h)
                {"ffn": ffn, "sparse": sparse, "differential": differential}[kind]()

        @block.scalar
        def _(act):
            a = Line(act, sem, "act")

            def f(o, i, fn, name=None, **kw):
                a.done(act.activation(o, i, fn, **kw), name)

            def rsqrt(o, i, scale, eps, name=None):
                f(o, i, ACT.Ln, scale=scale, bias=eps)
                f(o, o, ACT.Exp, name, scale=-0.5)

            def take_xT(sub=None):
                a.see("xt_psum1", 2)
                for c in range(4, 8):
                    name = "xt_act" if c == 7 else None
                    src = P[:, 6:8, (c - 4) * 128:(c - 3) * 128]
                    dst = xT[:, c, :].rearrange("p (i s) -> p i s", i=2)
                    if sub is None:
                        f(dst, src, ACT.Copy, name)
                    else:
                        f(dst, src, ACT.Identity, name, scale=x_scale[:, sub, c:c + 1], bias=modc[:, sub, 0, c:c + 1])

            def high_xT():
                f(x_hi[:, 4:8, :], xT[:, 4:8, :], ACT.Copy, "x_hi")

            def high(n0, js, r=0):
                for j in js:
                    if n0 + j in split_no:
                        slot, half = (n0 + j) % R, UNIT // 2
                        act.wait_ge(sem("unit%d" % slot), r * 16 + 16 * ((n0 + j) // R + 1))
                        for c in (0, half):
                            act.activation(w_hi[:, slot, c:c + half], ring[:, slot, c:c + half],
                                           ACT.Copy).then_inc(sem("w_hi"), 1)

            def out_tile(dst, fn=ACT.Copy, scale=1.0, width=S):
                a.see("proj")
                k = a.sent["proj_out"]
                f(dst, P[:, k % 2, 0:width], fn, "proj_out", scale=scale)
                if k % 2:
                    a.mark("unit_used")

            def a_angles():
                a.see("angles")
                f(rope[:, :, :, :], rope[:, :, :, :], ACT.Sin)

            def a_cols():
                a.see("cols_ready")

            def a_small():
                a.see("small_psum")
                f(small[:, 16:24].rearrange("p (i k) -> p i k", k=4), P[:, 2, 0:16].rearrange("p (i k) -> p i k", k=8)[:, :, 0:4],
                  ACT.Sigmoid, "beta")
                f(lrT[:, :], P[0:16, 3, 0:S], ACT.Copy, "lrT")
                a.see("sp_in")
                f(small[:, 44:56], small[:, 44:56], ACT.Exp)
                f(small[:, 8:12], small[:, 4:8], ACT.Exp, "sp_e")

            def a_proj(which, u):
                if which == "a" and u == 0:
                    a.see("pads", 2)
                for c in (2 * u, 2 * u + 1):
                    if which == "a":
                        out_tile(a_pad[:, c, 3:S + 3])
                    elif which == "b" and c < 12:
                        out_tile(qkv_pad[:, c, 3:S + 3])
                    elif which == "b":
                        out_tile(gate_b[:, c - 12, :], ACT.Silu)
                    else:
                        q, k, v = (sb_q, sb_k, sb_v) if which == "c" else (gl_q, gl_k, gl_v)
                        if c < 4:
                            out_tile(q[:, c, :], scale=64 ** -0.5 if which == "c" else 128 ** -0.5)
                        elif c < 8:
                            out_tile(k[:, c - 4, :])
                        elif c < 12:
                            out_tile(v[:, c % 2, (c - 8) // 2 * S:(c - 8) // 2 * S + S])
                        else:
                            out_tile(gate_d[:, c - 12, :], ACT.Silu)

            def a_a_gates():
                for g, (dst, bias) in enumerate(((a_r, V_BA), (a_i, V_BX))):
                    a.see("a_ri")
                    for c in range(4):
                        f(dst[:, c, :], P[:, 2 + 2 * g + c // 2, (c % 2) * S:(c % 2) * S + S], ACT.Sigmoid,
                          "a_act" if c == 3 else None, bias=cols[:, bias + c:bias + c + 1])

            def a_a_mult():
                a.see("a_dve")
                f(a_t[:, :, :], a_r[:, :, :], ACT.Tanh)
                f(a_r[:, :, :], a_r[:, :, :], ACT.Exp, "a_act")

            def a_a_scan():
                a.see("a_dve")
                f(a_t[:, :, :], a_t[:, :, :], ACT.Sqrt, "a_act")

            def a_b_conv():
                a.see("b_conv")
                f(qkv[:, :, :], qkv[:, :, :], ACT.Silu)
                f(nsq[:, :, :], qkv[:, 0:8, :], ACT.Square, "b_sq")

            def a_b_norm():
                a.see("b_ss")
                rsqrt(nsq[:, :, :], P[:, 4:8, :], 1.0, eps_ln[:, 1:2], "b_rs")

            def a_c_z(hp):
                a.see("c_z")
                if hp == 0:
                    a.see("a_done")
                    a.see("b_normed")
                f(c_zs[:, :, :], P[:, 2:4, 0:384], ACT.Copy, "c_act")
                a.see("c_dve")
                f(c_e[:, :, :], c_e[:, :, :], ACT.Exp)
                f(c_e[:, :, :], c_e[:, :, :], ACT.Ln, "c_act", bias=1.0)

            def a_c_cum(hp):
                a.see("c_dve")
                f(c_w[:, :, :], c_w[:, :, :], ACT.Exp, "c_w")

            def a_c_out(hp):
                a.see("c_o")
                f(yT[2][:, hp, :], P[:, 6 + hp % 2, 0:S], ACT.Copy, "y2")

            def a_d_gate():
                a.see("d_dve")
                f(d_e[:, :], d_e[:, :], ACT.Exp)
                f(d_e[:, :], d_e[:, :], ACT.Ln, "d_act", bias=1.0)
                a.see("d_dve")
                f(d_y[:, :], d_B[:, :], ACT.Exp, scale=-1 / 16)
                f(d_gl[:, :, :], d_B[:, :].rearrange("p (h c k) -> p h c k", h=4, k=16)[:, :, :, 15], ACT.Exp, scale=-1 / 16)
                f(d_e[:, :], d_B[:, :], ACT.Exp, "d_act", scale=1 / 16)
                a.see("d_dve")
                f(d_kd[:, :, :].rearrange("p a b -> p (a b)"), d_kd[:, :, :].rearrange("p a b -> p (a b)"), ACT.Exp,
                  "d_act", scale=-1 / 16)

            def a_d_end():
                a.see("d_I", 15)
                f(d_e[:, :], P[:, 4:6, :].rearrange("p a b -> p (a b)"), ACT.Square, "d_sq")
                a.see("d_ss")
                rsqrt(d_e[:, :], P[:, 6:8, :].rearrange("p a b -> p (a b)"), 1 / 128, eps_ln[:, 1:2], "d_act")

            def a_b_decay():
                a.see("b_st")
                f(small[:, 72:104], small[:, 72:104], ACT.Exp, "b_act")
                f(b_eg[:, :, :], P[:, 2:4, :], ACT.Exp)
                a.see("b_dif")
                f(b_dm[:, :, :], b_dm[:, :, :], ACT.Exp, "b_act")

            def a_b_nat():
                a.see("b_nat")
                f(b_X[:, :, :], P[:, 6:8, :], ACT.Copy, "b_act")

            def a_b_y(lv):
                a.see("b_Yp")
                f(b_Y[:, :, :], P[:, 2:4, :], ACT.Copy, "b_Y")

            def a_b_uw():
                a.see("b_uw")
                f(b_u[:, :, :], P[:, 2:4, :], ACT.Copy)
                f(b_wT[:, :, :], P[:, 4:6, :], ACT.Copy, "b_act")

            def a_b_end():
                a.see("b_o", 4)
                f(b_sq[:, :, :], P[:, 6:8, :], ACT.Square, "b_sq2")
                a.see("b_ss2")
                rsqrt(b_sq[:, :, :], P[:, 2:4, :], 1 / 128, eps_ln[:, 1:2], "b_act")

            def a_merge(k):
                if k >= 2:
                    act.wait_ge(sem("merged"), k - 1)
                a.see("branch_psum")
                f(sg[:, k % 2, :], P[:, k % 2, 0:S], ACT.Sigmoid, "sg")

            act_steps = {"a_mult": a_a_mult, "a_scan": a_a_scan, "angles": a_angles, "cols": a_cols,
                         "small": a_small, "proj": a_proj, "a_gates": a_a_gates, "b_conv": a_b_conv,
                         "b_norm": a_b_norm, "c_z": a_c_z, "c_cum": a_c_cum, "c_out": a_c_out, "d_gate": a_d_gate,
                         "d_end": a_d_end, "b_decay": a_b_decay, "b_nat": a_b_nat, "b_y": a_b_y, "b_uw": a_b_uw,
                         "b_end": a_b_end, "merge": a_merge}

            def layer_norm_rs():
                a.see("var")
                f(st[:, 4:6], st[:, 4:6], ACT.Sqrt, "rs", bias=eps_ln[:, 0:1])

            def silus(n0, tiles=4, r=0, h0=0, free=True, after=AFTER):
                for k in range(tiles):
                    if free or k >= 2:
                        act.wait_ge(sem("hid"), r * 4 + (h0 + k - 1))
                    act.wait_ge(sem("gu"), r * 4 + (h0 + k + 1))
                    if k % 2:
                        act.sem_inc(sem("wide_used"), 2)
                    act.activation(silu[:, k % 2, :], P[:, k % 2, 0:S], ACT.Silu).then_inc(sem("silu"), 1)
                    high(n0, after[k], r)

            tiles, unit = [0], [moe]

            def a_experts():
                take_xT()
                high_xT()
                high(unit[0], (0, 1, 2))
                a.see("route_psum")
                f(sc[:, :], P[:, 3, 0:32], ACT.Sigmoid, "sc")
                f(cols[:, V_C:V_C + 8], cols[:, V_C:V_C + 8], ACT.Silu, "cond")
                silus(unit[0], free=False)
                with act.Fori(0, EXPERTS - 1) as r:
                    silus(unit[0] + 6, r=r, h0=4)
                tiles[0] += 4 * EXPERTS
                unit[0] += 6 * EXPERTS
                layer_norm_rs()

            def before():
                for i in range(2):
                    a.see("x_ready2")
                    f(xT_rows[:, i, :], xs[:, i, :], ACT.Square, accum_out=st[:, 8 + i:9 + i])
                    f(st[:, 8 + i:9 + i], st[:, 8 + i:9 + i], ACT.Sqrt, "rs_in", scale=1 / D, bias=eps_ln[:, 1:2])

            def after():
                a.see("out")
                a.mark("unit_used")
                for b in range(4):
                    f(xT_rows[:, 0, 0:512], P[:, 4 + b, :], ACT.Square, "y_ss", accum_out=st[:, 12 + b:13 + b])
                a.see("y_sum")
                f(st[:, 16:18], st[:, 16:18], ACT.Sqrt, "y_rs", scale=1 / D, bias=eps_ln[:, 1:2])

            def a_ffn():
                h0, n0 = tiles[0], unit[0]
                silus(n0, h0=h0, free=h0 > 0)
                with act.Fori(0, 4) as r:
                    silus(n0 + 6, r=r, h0=h0 + 4)
                silus(n0 + 30, 2, h0=h0 + 20, after=LAST_AFTER)
                tiles[0] += 22
                unit[0] += 3 * FF_GROUPS

            def turned(dsts):
                for dst in dsts:
                    a.see("turn")
                    k = a.sent["turned"]
                    n = dst.shape[1]
                    f(dst, P[:, 2 + k % 2, 0:n * 128].rearrange("p (a b) -> p a b", b=128), ACT.Copy, "turned")

            def softmax_exps(n, i):
                kw = 128 * (i + 1)
                a.see("nmax")
                for k in range(4):
                    f(big[:, k, 0:kw], big[:, k, 0:kw], ACT.Exp, "exps" if k == 3 else None,
                      bias=st[:, 24 + k:25 + k], accum_out=st[:, 28 + k:29 + k])

            def a_project(widths):
                for u, w in enumerate(widths):
                    if u + 3 < len(widths):
                        high(unit[0], (u + 3,))
                    for i in range(2):
                        out_tile(proj[:, i, u * 256:u * 256 + w], width=w)

            def a_sparse():
                a_project(SPARSE_WIDTHS)
                for i in range(2):
                    r = slice(i * 128, i * 128 + 128)
                    turned([qT[:, 0:4, r], qT[:, 4:8, r], qiT[:, 0:4, r]])
                for i in range(2):
                    turned([kT[:, 0:2, i * 128:i * 128 + 128]])
                n = 0
                for i in range(2):
                    kw = 128 * (i + 1)
                    for hh in range(8):
                        a.see("idx")
                        if n >= 2:
                            act.wait_ge(sem("idx_add"), n - 1)
                        f(wk[:, n % 2, 0:kw], P[:, n % 2, 0:kw], ACT.Relu, "idx_relu")
                        n += 1
                for n in range(8):
                    i, hg = n // 4, n % 4
                    softmax_exps(n, i)
                    for j in range(i + 1):
                        a.see("pt")
                        f(pT[:, j, :, :], P[:, 2 + a.sent["pt_out"] % 2, :].rearrange("p (a b) -> p a b", b=128), ACT.Copy, "pt_out")
                    a.see("o_psum")
                    f(oT[:, 2 * hg:2 * hg + 2, i * 128:i * 128 + 128],
                      P[:, 4 + n % 2, 0:S].rearrange("p (a b) -> p a b", b=128), ACT.Copy, "o_out")

            def a_differential():
                a_project([256] * (DIFF_IN // 256))
                a.see("lam_in")
                f(st[:, 56:58], st[:, 56:58], ACT.Exp, "lam_exp")
                for i in range(2):
                    r = slice(i * 128, i * 128 + 128)
                    turned([qT[:, 0:4, r], qT[:, 4:8, r], kT[:, 0:4, r], kT[:, 4:8, r]])
                for n in range(8):
                    i, hg = n // 4, n % 4
                    softmax_exps(n, i)
                    a.see("pt")
                    src = P[:, 2 + a.sent["pt_out"] % 2, :].rearrange("p (k j b) -> p k j b", k=2, j=2)
                    f(pT[:, 0, :, :].rearrange("p (k j) b -> p k j b", j=2)[:, :, 0:i + 1, :], src[:, :, 0:i + 1, :], ACT.Copy, "pt_out")
                a.see("o_psum", 8)
                f(sq_o[:, :], P[:, 4:8, :].rearrange("p a b -> p (a b)"), ACT.Square, "o_sq")
                a.see("o_ss")
                rsqrt(sq_o[:, :], P[:, 0:4, :].rearrange("p a b -> p (a b)"), 1 / 128, eps_ln[:, 1:2], "o_rs")

            a.see("consts")
            take_xT()
            for step, *which in STEPS:
                if step in act_steps:
                    act_steps[step](*which)
            layer_norm_rs()
            a_experts()
            for n, (kind, unsplit) in enumerate(SUBLAYERS):
                before()
                high(unit[0], unsplit)
                take_xT(n)
                high_xT()
                {"ffn": a_ffn, "sparse": a_sparse, "differential": a_differential}[kind]()
                unit[0] += ATTENTION_UNITS[kind]
                after()

        @block.vector
        def _(dve):
            v = Line(dve, sem, "dve")

            def tt(o, x, y, op, name=None):
                v.done(dve.tensor_tensor(o, x, y, op), name)

            def ts(o, x, s1, s2=None, op0=ALU.mult, op1=None, name=None):
                v.done(dve.tensor_scalar(o, x, s1, s2, op0, op1) if s2 is not None else
                       dve.tensor_scalar(o, x, s1, None, op0), name)

            def stt(o, x, s, y, op0, op1, name=None):
                v.done(dve.scalar_tensor_tensor(out=o, in0=x, scalar=s, in1=y, op0=op0, op1=op1), name)

            def copy(o, x, name=None):
                v.done(dve.tensor_copy(o, x), name)

            def recip(o, x, name=None):
                v.done(dve.reciprocal(o, x), name)

            def over(ap, n):
                return ap.unsqueeze(1).to_broadcast([128, n, ap.shape[1]])

            def along(ap, n):
                return ap.unsqueeze(2).to_broadcast([128, ap.shape[1], n])

            def take_xT(sub=None):
                v.see("xt_psum0", 2)
                for c in range(4):
                    name = "xt_dve" if c == 3 else None
                    src = P[:, 4:6, c * 128:(c + 1) * 128]
                    dst = xT[:, c, :].rearrange("p (i s) -> p i s", i=2)
                    if sub is None:
                        copy(dst, src, name)
                    else:
                        ts(dst, src, x_scale[:, sub, c:c + 1], modc[:, sub, 0, c:c + 1], ALU.mult, ALU.add, name)

            def low_xT():
                copy(x_hi[:, 0:4, :], xT[:, 0:4, :])
                for k in range(2):
                    c = slice(4 * k, 4 * k + 4)
                    if k:
                        v.see("x_hi")
                    tt(x_lo[:, c, :], xT[:, c, :], x_hi[:, c, :].bitcast(F32), ALU.subtract, "x_lo")

            def low(n0, js, r=0):
                for j in js:
                    n = n0 + j
                    if n in split_no and lo_at[n][0] == "w_lo":
                        slot, half = n % R, UNIT // 2
                        for q, c in enumerate((0, half)):
                            if n - 1 in split_no and slot > 0:
                                lo_wait(dve, n - 1, r, back=1 - q)
                            dve.wait_ge(sem("w_hi"), r * 12 + (2 * split_no[n] + q + 1))
                            dve.tensor_tensor(w_lo[:, slot, c:c + half], ring[:, slot, c:c + half],
                                              w_hi[:, slot, c:c + half].bitcast(F32), ALU.subtract).then_inc(sem("w_lo"), 1)

            def rope_angles():
                dve.wait_ge(sem("pos_here"), 16)
                copy(st[:, 58:60], st[:, 60:62].bitcast(I32))
                for k in range(8):
                    v.done(dve.memset(st[:, 32 + k:33 + k], float(np.float32(500000.0 ** (-k / 8)))))
                for i in range(2):
                    for c in range(2):
                        ts(rope[:, i, c, :], st[:, 32:40], st[:, 58 + i:59 + i])
                rv = rope[:, :, :, :].rearrange("p i c k -> p c i k")
                turn = 2 * math.pi
                magic = 1.5 * 2.0 ** 23
                c1 = float(np.float32(6.28125))
                c2 = float(np.float32(int((turn - c1) * 2 ** 21) / 2 ** 21))
                c3 = float(np.float32(turn - c1 - c2))
                for c in range(2):
                    k = big_k[:, c, :].rearrange("p (i k) -> p i k", k=8)
                    ts(k, rv[:, c], 1 / turn, 0.25 * c, ALU.mult, ALU.add)
                    ts(k, k, magic, None, ALU.add)
                    ts(k, k, magic, None, ALU.subtract)
                    for cc in (c1, c2, c3):
                        stt(rv[:, c], k, -cc, rv[:, c], ALU.mult, ALU.add)
                    if c:
                        ts(rv[:, c], rv[:, c], math.pi / 2, None, ALU.add)
                    ts(rv[:, c], rv[:, c], 3.1415925, -3.1415925, ALU.min, ALU.max, "angles" if c else None)

            big_k = st[:, 0:32].rearrange("p (c k) -> p c k", k=16)

            def v_cols():
                v.see("cols_psum")
                copy(cols[:, :], P[:, 7, 0:128], "cols_ready")

            def v_small():
                dve.wait_ge(sem("small_here"), 64)
                z, e, s, s2, q = (small[:, k:k + 12] for k in (32, 44, 72, 84, 96))
                ts(z[:, 0:4], cols[:, V_LAM:V_LAM + 4], -1.0)
                v.see("beta")
                tt(z[:, 4:12].rearrange("p (i k) -> p i k", k=4), P[:, 2, 0:16].rearrange("p (i k) -> p i k", k=8)[:, :, 4:8],
                   over(small[:, 0:4], 2), ALU.add)
                stt(e, z, -1.0, z, ALU.mult, ALU.min, "sp_in")
                v.see("sp_e")
                ts(s, e, 2.0, None, ALU.add)
                recip(s, s)
                tt(s, s, e, ALU.mult)
                tt(s2, s, s, ALU.mult)
                ts(q, s2, 1 / 17)
                for k in (15, 13, 11, 9, 7, 5, 3):
                    stt(q, q, 1 / k, s2, ALU.add, ALU.mult)
                ts(q, q, 1.0, 2.0, ALU.add, ALU.mult)
                tt(q, q, s, ALU.mult)
                stt(q, z, 0.0, q, ALU.max, ALU.add)
                ts(small[:, 12:16], q[:, 0:4], -8.0)
                stt(small[:, 24:32].rearrange("p (i k) -> p i k", k=4), q[:, 4:12].rearrange("p (i k) -> p i k", k=4), -1.0,
                    over(small[:, 8:12], 2), ALU.mult, ALU.mult, "small_free")

            def conv(dst, src, w0, stride, c, bias=None):
                tap = lambda w: cols[:, w0 + w * stride + c:w0 + w * stride + c + 1]
                if bias is None:
                    ts(dst, src[:, c, 0:S], tap(0))
                else:
                    ts(dst, src[:, c, 0:S], tap(0), bias, ALU.mult, ALU.add)
                for w in range(1, 4):
                    stt(dst, src[:, c, w:w + S], tap(w), dst, ALU.mult, ALU.add)

            def v_a_conv():
                dve.wait_ge(sem("proj_out"), 4)
                for c in range(4):
                    conv(a_x[:, c, :], a_pad, V_CONV_A, 4, c, cols[:, V_CONV_AB + c:V_CONV_AB + c + 1])
                v.mark("a_x")

            def v_a_gates():
                v.see("masks")
                v.see("a_act", 2)
                for c in range(4):
                    ts(a_r[:, c, :], a_r[:, c, :], small[:, 12 + c:13 + c], name="a_dve" if c == 3 else None)

            def v_a_mult():
                v.see("a_act")
                ts(nsq[:, 0:4, :], a_t[:, :, :], -1.0, 1.0, ALU.mult, ALU.add)
                recip(nsq[:, 0:4, :], nsq[:, 0:4, :])
                stt(a_t[:, :, :], a_t[:, :, :], -2.0, nsq[:, 0:4, :], ALU.mult, ALU.mult, "a_dve")

            def v_a_scan():
                v.see("a_act")
                v.done(dve.memset(a_t[:, :, 0:1], 1.0))
                tt(a_t[:, :, :], a_t[:, :, :], a_i[:, :, :], ALU.mult)
                tt(a_t[:, :, :], a_t[:, :, :], a_x[:, :, :], ALU.mult)
                for c in range(4):
                    v.done(dve.tensor_tensor_scan(yT[0][:, c, :], a_r[:, c, :], a_t[:, c, :], 0.0, ALU.mult, ALU.add),
                           "y0" if c == 3 else None)
                v.mark("a_done")

            def v_b_conv():
                dve.wait_ge(sem("proj_out"), 16)
                for c in range(12):
                    conv(qkv[:, c, :], qkv_pad, V_CONV_B, 12, c)
                v.mark("b_conv")

            def v_b_norm():
                v.see("b_rs")
                stt(qkv[:, 0:4, :], qkv[:, 0:4, :], 128 ** -0.5, nsq[:, 0:4, :], ALU.mult, ALU.mult)
                tt(qkv[:, 4:8, :], qkv[:, 4:8, :], nsq[:, 4:8, :], ALU.mult, "b_normed")

            def v_c_z(hp):
                v.see("c_act")
                stt(c_e[:, :, :], c_zs[:, :, :], -1.0, c_zs[:, :, :], ALU.mult, ALU.min, "c_dve")
                v.see("c_act")
                stt(c_sp[:, :, :], c_zs[:, :, :], 0.0, c_e[:, :, :], ALU.max, ALU.add)
                tt(c_sp[:, :, :], c_sp[:, :, :], over(mask3[:, :], 2), ALU.mult, "c_sp")

            def v_c_cum(hp):
                v.see("c_cum")
                if hp:
                    dve.wait_ge(sem("c_o"), hp)
                stt(c_w[:, :, :], P[:, 4:6, 0:384], -1.0, c_zs[:, :, :], ALU.mult, ALU.add)
                stt(c_w[:, :, :], c_w[:, :, :], 0.0, over(neg3[:, :], 2), ALU.min, ALU.add, "c_dve")

            def v_d_gate():
                dve.wait_ge(sem("c_o"), 4)
                v.done(dve.memset(d_reset[:, :], 1.0))
                v.done(dve.memset(d_reset[:, 0::16], 0.0))
                v.see("d_psum")
                for c in range(4):
                    ts(d_y[:, c * S:c * S + S], P[:, 2 + c // 2, (c % 2) * S:(c % 2) * S + S],
                       cols[:, V_BGLA + c:V_BGLA + c + 1], -1.0, ALU.add, ALU.mult)
                stt(d_e[:, :], d_y[:, :], -1.0, d_y[:, :], ALU.mult, ALU.min, "d_dve")
                v.see("d_act")
                stt(d_e[:, :], d_y[:, :], 0.0, d_e[:, :], ALU.max, ALU.add)
                v.done(dve.tensor_tensor_scan(d_B[:, :], d_reset[:, :], d_e[:, :], 0.0, ALU.mult, ALU.add), "d_dve")
                B4 = d_B[:, :].rearrange("p (c k) -> p c k", k=16)
                tt(d_kd[:, :, :].rearrange("p h (c k) -> p (h c) k", k=16), B4[:, :, 15:16].to_broadcast([128, 64, 16]), B4, ALU.subtract, "d_dve")
                v.see("d_act")
                q4, k4 = (x[:, :, :].rearrange("p a b -> p (a b)") for x in (gl_q, gl_k))
                v.see("d_act")
                tt(d_kd[:, :, :].rearrange("p a b -> p (a b)"), d_kd[:, :, :].rearrange("p a b -> p (a b)"), k4, ALU.mult)
                tt(q4, q4, d_y[:, :], ALU.mult)
                tt(k4, k4, d_e[:, :], ALU.mult, "d_q")

            def v_d_attn():
                v.see("d_psum")
                tt(d_at[:, :, :], P[:, 4:6, :].rearrange("p i (h s) -> p (i h) s", s=128), over(tri16[:, :], 8), ALU.mult)
                v.see("d_psum")
                for e in range(2):
                    ts(d_kn[:, e, :, :], P[:, 6:8, :].rearrange("p i (h s) -> p (i h) s", s=128), parity[:, e:e + 1],
                       name="d_am" if e else None)

            def v_d_chunk(c):
                if c == 15:
                    return
                v.see("d_psum")
                if c >= 2:
                    dve.wait_ge(sem("d_I"), c - 1)
                if c == 0:
                    copy(d_S[:, 0, :], P[:, 2, :], "d_S")
                    return
                for hh in range(4):
                    r = slice(hh * 128, hh * 128 + 128)
                    stt(d_S[:, c % 2, r], d_S[:, (c - 1) % 2, r], d_gl[:, hh, c:c + 1], P[:, 2 + c % 2, r],
                        ALU.mult, ALU.add, "d_S" if hh == 3 else None)

            def branch_end(rs, bank, scale_col, gate, y, name):
                tt(rs, rs, P[:, bank:bank + 2, :].rearrange("p a b -> p (a b)"), ALU.mult)
                stt(y[:, :, :].rearrange("p a b -> p (a b)"), rs, cols[:, scale_col:scale_col + 1],
                    gate[:, :, :].rearrange("p a b -> p (a b)"), ALU.mult, ALU.mult, name)

            def v_d_end():
                v.see("d_act")
                branch_end(d_e[:, :], 4, V_ND, gate_d, yT[3], "y3")

            def v_b_rows():
                for i in range(2):
                    for hh in range(4):
                        c = 4 * i + hh
                        ts(b_r1[:, c, :], tri64[:, :], small[:, 24 + c:25 + c])
                        ts(b_r2[:, c, :], ident[:, :], small[:, 16 + c:17 + c], name="b_dve" if c == 7 else None)

            def v_b_decay():
                v.see("b_rows")
                copy(small[:, 72:88], P[:, 6, 0:16])
                for s in range(2):
                    copy(small[:, 88:104].rearrange("p (i s k) -> p i s k", s=2, k=4)[:, :, s, :],
                         P[:, 6 + s, 16:24].rearrange("p (i k) -> p i k", k=4))
                for u in range(8):
                    ts(b_dm[:, u, :], P[:, 2 + u // 4, (u % 4) * 128:(u % 4) * 128 + 128], small[:, 72 + u:73 + u], 0.0,
                       ALU.subtract, ALU.min, name="b_dif" if u == 7 else None)
                tt(small[:, 80:88], small[:, 80:88], small[:, 72:80], ALU.subtract, "b_st")
                v.see("b_act")
                tt(small[:, 104:112], small[:, 72:80], small[:, 16:24], ALU.mult)
                v.see("b_act")
                tt(b_dm[:, :, :], b_dm[:, :, :], over(tri64[:, :], 8), ALU.mult)
                tt(b_r1[:, :, :], b_dm[:, :, :], P[:, 4:6, :].rearrange("p i (h s) -> p (i h) s", s=128), ALU.mult, "b_dve")

            def v_b_kk():
                v.see("b_kk")
                tt(b_N[:, :, :], b_r1[:, :, :], P[:, 2:4, :].rearrange("p i (h s) -> p (i h) s", s=128), ALU.mult)
                tt(b_at[:, :, :], b_dm[:, :, :], P[:, 6:8, :].rearrange("p i (h s) -> p (i h) s", s=128), ALU.mult)
                tt(b_XT[:, :, :], b_N[:, :, :], over(masks[:, 0, :], 8), ALU.mult)
                tt(b_XT[:, :, :], over(ident[:, :], 8), b_XT[:, :, :], ALU.subtract, "b_dve")

            def v_b_nat():
                v.see("b_nat")
                kp = P[:, 2:4, :].rearrange("p i (h s) -> p (i h) s", s=128)
                vp = P[:, 4:6, :].rearrange("p i (h s) -> p (i h) s", s=128)
                tt(b_kbg[:, :, :], kp, along(small[:, 104:112], 128), ALU.mult)
                tt(b_kd[:, :, :], kp, along(small[:, 80:88], 128), ALU.mult)
                tt(b_vb[:, :, :], vp, along(small[:, 16:24], 128), ALU.mult)
                v.see("b_act")

            def v_b_y(lv):
                tt(b_Nl[:, :, :], b_N[:, :, :], over(masks[:, lv, :], 8), ALU.mult, "b_dve")

            def v_b_xy(lv):
                v.see("b_XY")
                if lv < 5:
                    tt(b_X[:, :, :], b_X[:, :, :], P[:, 4:6, :].rearrange("p i (h s) -> p (i h) s", s=128), ALU.subtract)
                tt(b_XT[:, :, :], b_XT[:, :, :], P[:, 6:8, :].rearrange("p i (h s) -> p (i h) s", s=128), ALU.subtract,
                   "b_dve" if lv == 5 else None)

            def v_b_uw():
                for i in range(2):
                    tt(b_qd[:, 4 * i:4 * i + 4, :], qkv[:, 0:4, i * 128:i * 128 + 128], b_eg[:, 4 * i:4 * i + 4, :], ALU.mult)
                v.see("b_act")
                v.mark("b_dve")

            def v_b_w(c):
                i, b = c // 2, 64 * (c % 2)
                r = slice(b, b + 64)
                if c == 0:
                    copy(b_vn[r, :, :], b_u[r, 0:4, :], "b_dve")
                    return
                v.see("b_wS")
                tt(b_vn[r, :, :], b_u[r, 4 * i:4 * i + 4, :], P[r, 2, :].rearrange("p (h s) -> p h s", s=128), ALU.subtract, "b_dve")

            def v_b_o(c):
                v.see("b_o")
                if c == 3:
                    return
                if c == 0:
                    copy(b_S[:, :, :], P[:, 3, :].rearrange("p (h s) -> p h s", s=128), "b_dve")
                    return
                tt(b_S[:, :, :], b_S[:, :, :], along(small[:, 88 + 4 * c:92 + 4 * c], 128), ALU.mult)
                tt(b_S[:, :, :], b_S[:, :, :], P[:, 3, :].rearrange("p (h s) -> p h s", s=128), ALU.add, "b_dve")

            def v_b_end():
                v.see("b_act")
                branch_end(b_sq[:, :, :].rearrange("p a b -> p (a b)"), 6, V_NB, gate_b, yT[1], "y1")
                v.mark("b_read")

            def v_merge(k):
                d = k % DT
                v.see("sg")
                if d % 4 == 3:
                    v.mark("unit_used", 3)
                p = P[:, k % 2, S:2 * S]
                if k < DT:
                    tt(merged[:, d, :], sg[:, k % 2, :], p, ALU.mult, "merged")
                else:
                    tt(tmpm[:, :], sg[:, k % 2, :], p, ALU.mult)
                    tt(merged[:, d, :], merged[:, d, :], tmpm[:, :], ALU.add, "merged")

            dve_steps = {"a_mult": v_a_mult, "a_scan": v_a_scan, "angles": rope_angles, "cols": v_cols,
                         "small": v_small, "a_conv": v_a_conv, "a_gates": v_a_gates, "b_conv": v_b_conv,
                         "b_norm": v_b_norm, "c_z": v_c_z, "c_cum": v_c_cum, "d_gate": v_d_gate, "d_attn": v_d_attn,
                         "d_chunk": v_d_chunk, "d_end": v_d_end, "b_rows": v_b_rows, "b_decay": v_b_decay,
                         "b_kk": v_b_kk, "b_nat": v_b_nat, "b_y": v_b_y, "b_xy": v_b_xy, "b_uw": v_b_uw,
                         "b_w": v_b_w, "b_o": v_b_o, "b_end": v_b_end, "merge": v_merge}

            def layer_norm(g, b, name):
                for i in range(2):
                    for c in range(2):
                        v.done(dve.bn_stats(st[:, 20 + 6 * c:26 + 6 * c], xs[:, i, c * 512:c * 512 + 512]))
                    v.done(dve.bn_aggr(st[:, 2 * i:2 * i + 2], st[:, 20:32].rearrange("p (c k) -> p c k", k=6)))
                for i in range(2):
                    copy(st[:, 4 + i:5 + i], st[:, 2 * i + 1:2 * i + 2], "var" if i else None)
                v.see("rs")
                recip(st[:, 4:6], st[:, 4:6])
                for i in range(2):
                    ts(xs[:, i, :], xs[:, i, :], st[:, 2 * i:2 * i + 1], st[:, 4 + i:5 + i], ALU.subtract, ALU.mult)
                    tt(xs[:, i, :], xs[:, i, :], rowbc[:, g, :], ALU.mult)
                    tt(xs[:, i, :], xs[:, i, :], rowbc[:, b, :], ALU.add, name)

            def route():
                s = lambda k: rt[:, k, :]
                g4 = lambda ap: ap.rearrange("p (i g e) -> p i g e", i=2, e=4)
                v.see("sc")
                tt(s(0).rearrange("p (i e) -> p i e", i=2), sc[:, :].rearrange("p (i e) -> p i e", i=2), over(rt[:, 15, 0:16], 2), ALU.add)
                b4 = g4(s(0)).rearrange("p i g e -> p (i g) e")
                gs, pair = s(1)[:, 0:8], s(2)[:, 0:8]
                first_pair = True
                for x in range(4):
                    for y in range(x + 1, 4):
                        tt((gs if first_pair else pair).unsqueeze(2), b4[:, :, x:x + 1], b4[:, :, y:y + 1], ALU.add)
                        if not first_pair:
                            tt(gs, gs, pair, ALU.max)
                        first_pair = False

                def first_best(vals, n, dst, cum):
                    v3 = vals.rearrange("p (i n) -> p i n", i=2)
                    d3 = dst.rearrange("p (i n) -> p i n", i=2)
                    v.done(dve.tensor_reduce(s(3)[:, 0:2], v3, AX.X, ALU.max))
                    tt(d3, v3, along(s(3)[:, 0:2], n), ALU.is_equal)
                    for i in range(2):
                        v.done(dve.tensor_tensor_scan(cum[:, i * n:i * n + n], ones[:, 0:n], dst[:, i * n:i * n + n], 0.0,
                                                      ALU.mult, ALU.add))
                    stt(dst, cum, 1.0, dst, ALU.is_equal, ALU.mult)

                yield
                first_best(gs, 4, s(4)[:, 0:8], s(5)[:, 0:8])
                ts(s(6)[:, 0:8], s(4)[:, 0:8], -1.0, BIG, ALU.add, ALU.mult)
                tt(s(7).rearrange("p (g e) -> p g e", e=4), b4, along(s(6)[:, 0:8], 4), ALU.add)
                yield
                first_best(s(7), 16, s(8), s(9))
                stt(s(7), s(8), -BIG, s(7), ALU.mult, ALU.add)
                yield
                first_best(s(7), 16, s(10), s(9))
                tt(s(8), s(8), s(10), ALU.add)
                tt(s(8), s(8), sc[:, :], ALU.mult)
                v.done(dve.tensor_reduce(s(3)[:, 0:2], s(8).rearrange("p (i n) -> p i n", i=2), AX.X, ALU.add))
                recip(s(3)[:, 0:2], s(3)[:, 0:2])
                tt(comb[:, :].rearrange("p (i n) -> p i n", i=2), s(8).rearrange("p (i n) -> p i n", i=2), along(s(3)[:, 0:2], 16), ALU.mult)
                ts(xs[:, :, :], xs[:, :, :], DN_ALPHA)

            def hidden(k, r, h0, done=0):
                n = 2 * (h0 + k)
                for part in (hid_hi, hid_lo) if done else ():
                    ts(part[0:done, k, :], ones256[0:done, :], 0.0)
                x, hi = hid[done:128, k % 2, :], hid_hi[done:128, k, :]
                dve.wait_ge(sem("silu"), r * 4 + (h0 + k + 1))
                dve.tensor_tensor(x, silu[done:128, k % 2, :], P[done:128, k % 2, S:2 * S], ALU.mult).then_inc(sem("hid_part"), 1)
                dve.wait_ge(sem("hid_part"), r * 8 + (n + 1))
                dve.tensor_copy(hi, x).then_inc(sem("hid_part"), 1)
                dve.wait_ge(sem("hid_part"), r * 8 + (n + 2))
                dve.tensor_tensor(hid_lo[done:128, k, :], x, hi.bitcast(F32), ALU.subtract).then_inc(sem("hid"), 1)

            def ada_halves(halves, r, prior=True):
                for i in halves:
                    j = i // 2
                    dve.wait_ge(sem("ada%d" % (i % 3)), r * 32 + 16 * (i // 3 + 1))
                    if i % 2 == 0 and prior:
                        dve.wait_ge(sem("ada_read"), r * 3 + (j - 2))
                    for d in range(4):
                        w, c = ada[:, i % 3, d, :], cols[:, V_C + 4 * (i % 2) + d:V_C + 4 * (i % 2) + d + 1]
                        if i % 2 == 0 and d == 0:
                            x = dve.tensor_scalar(acc[:, j, :], w, c, None, ALU.mult)
                        else:
                            if d == 0:
                                dve.wait_ge(sem("ada_half"), r * 6 + i)
                            else:
                                dve.wait_ge(sem("ada_step"), r * 18 + (3 * i + d))
                            x = dve.scalar_tensor_tensor(out=acc[:, j, :], in0=w, scalar=c, in1=acc[:, j, :],
                                                         op0=ALU.mult, op1=ALU.add)
                        x.then_inc(sem("ada_step" if d < 3 else "ada_half"), 1)

            def add_expert(e, r):
                dve.wait_ge(sem("expert_out"), r)
                dve.sem_inc(sem("unit_used"), 1)
                dve.wait_ge(sem("y_added"), r - 1)
                for b in range(4):
                    i, c = b // 2, b % 2
                    x = dve.scalar_tensor_tensor(out=xs[:, i, c * 512:c * 512 + 512], in0=P[:, 4 + b, :],
                                                 scalar=comb[:, bass.ds(e + 16 * i, 1)], in1=xs[:, i, c * 512:c * 512 + 512],
                                                 op0=ALU.mult, op1=ALU.add)
                x.then_inc(sem("y_added"), 1)

            tiles, unit = [0], [moe]

            def v_experts():
                take_xT()
                low_xT()
                n0 = unit[0]
                low(n0, (0, 1, 2))
                routing = route()
                v.see("cond")
                for k in range(4):
                    hidden(k, 0, 0)
                    low(n0, AFTER[k])
                    next(routing, None)
                    ada_halves(HALVES[k], 0, False)
                with dve.Fori(0, EXPERTS - 1) as r:
                    hidden(0, r, 4)
                    add_expert(r, r + 1)
                    low(n0 + 6, AFTER[0], r)
                    ada_halves(HALVES[0], r + 1)
                    for k in range(1, 4):
                        hidden(k, r, 4)
                        low(n0 + 6, AFTER[k], r)
                        ada_halves(HALVES[k], r + 1)
                unit[0] += 6 * EXPERTS
                add_expert(EXPERTS - 1, EXPERTS)
                dve.wait_ge(sem("y_added"), EXPERTS)
                tiles[0] += 4 * EXPERTS
                dve.wait_ge(sem("ada_read"), 3 * EXPERTS)
                copy(adac[:, :], P[:, 2, 0:2 * N_COLS], "adac")
                v.see("modt")
                for l in range(2):
                    tt(modr[:, l, :], P[0:N_COLS, 3, l * 128:l * 128 + 128], adab[:, l, :], ALU.add, "modr" if l else None)
                v.mark("modr_ready")
                v.see("modt")
                copy(modc[:, :, :, :].rearrange("p n k t -> p (n k t)"), P[:, 3, 0:2 * N_COLS])
                stt(x_scale[:, :, :], modc[:, :, 1, :], 1.0,
                    P[:, 3, 2 * N_COLS:2 * N_COLS + 6 * DT].rearrange("p (n t) -> p n t", t=DT), ALU.add, ALU.mult)
                layer_norm(2, 3, "x_ready2")
                v.mark("post_free")

            def before(n, kind, unsplit):
                for i in range(2):
                    v.see("rs_in")
                    recip(st[:, 8 + i:9 + i], st[:, 8 + i:9 + i])
                    ts(h[:, i, :], xs[:, i, :], st[:, 8 + i:9 + i], name="h_ready")
                low(unit[0], unsplit[:-1])
                take_xT(n)
                low_xT()
                low(unit[0], unsplit[-1:])
                dve.wait_ge(sem("post_here"), 32 * (n + 1))
                stt(rowbc[:, 1, :], rowbc[:, 1, :], 0.5 if kind == "ffn" else 1.0, rowbc[:, 0, :], ALU.mult, ALU.mult)

            def after(n):
                for b in range(4):
                    v.see("y_ss")
                    if b == 3:
                        v.done(dve.tensor_reduce(st[:, 16:18], st[:, 12:16].rearrange("p (i c) -> p i c", c=2), AX.X, ALU.add), "y_sum")
                    i, c = b // 2, slice((b % 2) * 512, (b % 2) * 512 + 512)
                    tt(h[:, i, c], P[:, 4 + b, :], rowbc[:, 1, c], ALU.mult)
                if n < 5:
                    v.mark("post_free")
                v.see("y_rs")
                recip(st[:, 16:18], st[:, 16:18])
                for i in range(2):
                    stt(xs[:, i, :], h[:, i, :], st[:, 16 + i:17 + i], xs[:, i, :], ALU.mult, ALU.add,
                        "x_final" if n == 5 else "x_ready2")

            def v_ffn():
                h0, n0 = tiles[0], unit[0]
                for k in range(4):
                    hidden(k, 0, h0)
                    low(n0, AFTER[k])
                with dve.Fori(0, 4) as r:
                    for k in range(4):
                        hidden(k, r, h0 + 4)
                        low(n0 + 6, AFTER[k], r)
                for k in range(2):
                    hidden(k, 0, h0 + 20, 0 if k else FF_DONE)
                    low(n0 + 30, LAST_AFTER[k])
                tiles[0] += 22
                unit[0] += 3 * FF_GROUPS

            def apply_rope(i, c0, heads):
                x = proj[:, i, c0:c0 + 64 * heads].rearrange("p (h d) -> p h d", d=64)
                x1, x2 = x[:, :, 0:8], x[:, :, 8:16]
                w = [big[:, k, 0:8 * heads].rearrange("p (h d) -> p h d", d=8) for k in range(4)]
                sin, cos = over(rope[:, i, 0, :], heads), over(rope[:, i, 1, :], heads)
                tt(w[0], x1, cos, ALU.mult)
                tt(w[1], x2, sin, ALU.mult)
                tt(w[2], x2, cos, ALU.mult)
                tt(w[3], x1, sin, ALU.mult)
                tt(x1, w[0], w[1], ALU.subtract)
                tt(x2, w[2], w[3], ALU.add)

            def probs_rows(i, mask):
                kw = 128 * (i + 1)
                v.see("s_psum")
                s4 = halves(0)[:, :, 0:kw]
                stt(big[:, :, 0:kw], s4, 64 ** -0.5, over(mask, 4), ALU.mult, ALU.add, "s_read")
                v.done(dve.tensor_reduce(st[:, 24:28], big[:, :, 0:kw], AX.X, ALU.max))
                ts(st[:, 24:28], st[:, 24:28], -1.0, name="nmax")
                v.see("exps")
                recip(st[:, 28:32], st[:, 28:32])

            def v_sparse():
                low(unit[0], range(3, len(SPARSE_WIDTHS)))
                dve.wait_ge(sem("proj_out"), proj_before[0] + 14)
                proj_before[0] += 14
                for i in range(2):
                    apply_rope(i, 0, 17)
                    apply_rope(i, 1152, 9)
                v.mark("roped")
                for i in range(2):
                    for e in range(2):
                        copy(dup[:, i, 64 * e:64 * e + 64], proj[:, i, 1024:1088])
                        copy(big[:, 0, 128 * i + 64 * e:128 * i + 64 * e + 64], proj[:, i, 1664:1728],
                             "dup" if i + e == 2 else None)
                n = 0
                for i in range(2):
                    kw = 128 * (i + 1)
                    w8 = st[:, 40:48]
                    ts(w8, proj[:, i, 1728:1736], float(np.float32(8 ** -0.5 * 64 ** -0.5)))
                    for hh in range(8):
                        v.see("idx_relu")
                        if hh == 0:
                            ts(score[:, 0:kw], wk[:, n % 2, 0:kw], w8[:, 0:1], name="idx_add")
                        else:
                            stt(score[:, 0:kw], wk[:, n % 2, 0:kw], w8[:, hh:hh + 1], score[:, 0:kw], ALU.mult, ALU.add, "idx_add")
                        n += 1
                    d0 = 128 * i
                    tt(score[:, d0:d0 + 128], score[:, d0:d0 + 128], causal_neg[:, :], ALU.add)
                    best = st[:, 48:56]
                    src = score[:, 0:kw]
                    for k in range(TOPK // 8):
                        v.done(dve.max(best, src))
                        if k < TOPK // 8 - 1:
                            v.done(dve.match_replace(rl[:, 0:kw], best, src, -3e38))
                            src = rl[:, 0:kw]
                    thr = best[:, 7:8]
                    m = keep[:, i, 0:kw]
                    more, same, cum = big[:, 1, 0:kw], big[:, 2, 0:kw], big[:, 3, 0:kw]
                    ts(more, score[:, 0:kw], thr, None, ALU.is_gt)
                    ts(same, score[:, 0:kw], thr, None, ALU.is_equal)
                    v.done(dve.tensor_reduce(st[:, 32:33], more, AX.X, ALU.add))
                    ts(st[:, 32:33], st[:, 32:33], -1.0, float(TOPK), ALU.mult, ALU.add)
                    v.done(dve.tensor_tensor_scan(cum, ones256[:, 0:kw], same, 0.0, ALU.mult, ALU.add))
                    stt(m, cum, st[:, 32:33], same, ALU.is_le, ALU.mult)
                    tt(m, m, more, ALU.add)
                    ts(m, m, -1.0, BIG, ALU.add, ALU.mult)
                    tt(keep[:, i, d0:d0 + 128], keep[:, i, d0:d0 + 128], causal_neg[:, :], ALU.add)
                for n in range(8):
                    i, hg = n // 4, n % 4
                    kw = 128 * (i + 1)
                    probs_rows(i, keep[:, i, 0:kw])
                    if n >= 1:
                        dve.wait_ge(sem("pt"), pt_count(n))
                    tt(pr[:, :, 0:kw], big[:, :, 0:kw], along(st[:, 28:32], kw), ALU.mult, "p_ready")

            def pt_count(n):
                return n if n <= 4 else 4 + 2 * (n - 4)

            proj_before = [48]

            def v_differential():
                low(unit[0], range(3, DIFF_IN // 256))
                dve.wait_ge(sem("lam_here"), 16)
                lam = lamb[:, :].rearrange("p (a b c) -> p a b c", a=2, b=2)
                tt(h[:, 0, 0:128].rearrange("p (a c) -> p a c", a=2), lam[:, :, 0, :], lam[:, :, 1, :], ALU.mult)
                v.done(dve.tensor_reduce(st[:, 56:58], h[:, 0, 0:128].rearrange("p (a c) -> p a c", a=2), AX.X, ALU.add), "lam_in")
                v.see("lam_exp")
                tt(st[:, 58:59], st[:, 56:57], st[:, 57:58], ALU.subtract)
                ts(st[:, 58:59], st[:, 58:59], LAM_INIT, None, ALU.add)
                dve.wait_ge(sem("proj_out"), proj_before[0] + 24)
                for i in range(2):
                    apply_rope(i, 0, 32)
                v.mark("roped")
                v.done(dve.memset(keep[:, 1, 0:128], 0.0))
                copy(keep[:, 1, 128:256], causal_neg[:, :])
                for n in range(8):
                    i, hg = n // 4, n % 4
                    kw = 128 * (i + 1)
                    probs_rows(i, keep[:, 1, 128:256] if i == 0 else keep[:, 1, :])
                    ts(st[:, 29:32:2], st[:, 29:32:2], st[:, 58:59])
                    if n >= 1:
                        dve.wait_ge(sem("pt"), pt_count(8) + n)
                    for k in range(2):
                        ts(big[:, 2 * k + 1, 0:kw], big[:, 2 * k + 1, 0:kw], st[:, 29 + 2 * k:30 + 2 * k])
                        stt(pr[:, k, 0:kw], big[:, 2 * k, 0:kw], st[:, 28 + 2 * k:29 + 2 * k], big[:, 2 * k + 1, 0:kw],
                            ALU.mult, ALU.subtract, "p_ready" if k else None)
                ts(st[:, 59:60], cols[:, V_SUB:V_SUB + 1], 1.0 - LAM_INIT)
                v.see("o_rs")
                stt(oT[:, :, :].rearrange("p a b -> p (a b)"), sq_o[:, :], st[:, 59:60], P[:, 4:8, :].rearrange("p a b -> p (a b)"),
                    ALU.mult, ALU.mult, "o_normed")

            v.see("consts")
            take_xT()
            for step, *which in STEPS:
                if step in dve_steps:
                    dve_steps[step](*which)
            v.see("mixer_out")
            v.mark("unit_used")
            for b in range(4):
                i, c = b // 2, slice((b % 2) * 512, (b % 2) * 512 + 512)
                stt(xs[:, i, c], xs[:, i, c], DN_ALPHA, P[:, 4 + b, :], ALU.mult, ALU.add)
            dve.wait_ge(sem("ln_here"), 64)
            layer_norm(0, 1, "x_ready")
            v.mark("mixed")
            v_experts()
            for n, (kind, unsplit) in enumerate(SUBLAYERS):
                before(n, kind, unsplit)
                {"ffn": v_ffn, "sparse": v_sparse, "differential": v_differential}[kind]()
                unit[0] += ATTENTION_UNITS[kind]
                after(n)


def kernel(**inputs):
    import concourse.bacc as bacc
    from concourse.bass_utils import run_bass_kernel_spmd

    nc = bacc.Bacc("TRN2", target_bir_lowering=False, num_devices=1)
    arrays, aps = {}, {}
    for name, a in inputs.items():
        a = np.ascontiguousarray(a)
        arrays["in_" + name] = a
        aps[name] = nc.dram_tensor("in_" + name, a.shape, mybir.dt.from_np(a.dtype), kind="ExternalInput").ap()
    out = nc.dram_tensor("out", (1, S, D), F32, kind="ExternalOutput").ap()
    build(nc, aps, out)
    return run_bass_kernel_spmd(nc, [arrays], core_ids=[0]).results[0]["out"]
```
